# Optimizing a Trainium2 kernel written in Bass

```python
import jax, jax.numpy as jnp
from jax import lax
import numpy as np

D_MODEL = 2048
BATCH = 1
SEQ = 256
DEPTH = 1
DEC_BATCH = 8
DEC_SEQ = 8
PAST_LEN = 2048
PAGE_SIZE = 128

MIX_WIDTH = D_MODEL
POOL_WIDTH = MIX_WIDTH // 2
POOL_WINDOWS = (2, 4, 8, 16)
POOL_GROUP = POOL_WIDTH // len(POOL_WINDOWS)
POOL_BUF = max(POOL_WINDOWS) - 1
RWKV_WIDTH = MIX_WIDTH - POOL_WIDTH
HEAD_DIM = 64
N_HEADS = RWKV_WIDTH // HEAD_DIM
DECAY_LORA = 64
AAA_LORA = 64
GATE_LORA = 160
SHIFT_WIDTH = 3 * RWKV_WIDTH + DECAY_LORA + AAA_LORA + GATE_LORA
PROJ_WIDTH = POOL_WIDTH + SHIFT_WIDTH
LNX_EPS = 64e-5
RMS_EPS = 1e-6
N_EXPERTS = 16
N_EXPERT_GROUPS = 4
EXPERTS_PER_GROUP = N_EXPERTS // N_EXPERT_GROUPS
TOP_K = 2
GROUP_SCORE_K = 2
D_EXPERT = D_MODEL // 2
MOE_BLOCK = 128

kernel_name = "hybrid_pool_rwkv7_moe_adaln_step"

def _rmsnorm(x, g):
    xf = x.astype(jnp.float32)
    return xf * lax.rsqrt(jnp.mean(xf * xf, -1, keepdims=True) + RMS_EPS) * g.astype(jnp.float32)

def _ada_norm(x, g, shift, scale):
    h = _rmsnorm(x, g) * (1.0 + scale[:, None, :].astype(jnp.float32)) + shift[:, None, :].astype(jnp.float32)
    return h.astype(x.dtype)

def _pool_mixer(p, buf, pos0, w_pool, scale):
    B, L, _ = p.shape
    ext = jnp.concatenate([buf.astype(p.dtype), p], 1)
    cs = jnp.concatenate([jnp.zeros((B, 1, POOL_WIDTH), jnp.float32),
                          jnp.cumsum(ext.astype(jnp.float32), 1)], 1)
    end = cs[:, POOL_BUF + 1:]
    pos = pos0 + jnp.arange(L)
    pf = p.astype(jnp.float32)
    outs = []
    for gi, win in enumerate(POOL_WINDOWS):
        sl = slice(gi * POOL_GROUP, (gi + 1) * POOL_GROUP)
        s0 = POOL_BUF + 1 - win
        wsum = end[..., sl] - cs[:, s0:s0 + L, sl]
        cnt = jnp.minimum(pos + 1, win).astype(jnp.float32)[None, :, None]
        pooled = wsum / cnt - pf[..., sl]
        outs.append(jnp.einsum('blc,cd->bld', pooled, w_pool[gi].astype(jnp.float32)))
    y = jnp.concatenate(outs, -1) * scale.astype(jnp.float32)
    return y.astype(p.dtype), ext[:, -POOL_BUF:]

def _rwkv7(z, shift_prev, S0, mu, w0, w2, a0, a2, g2, k_k, k_a, r_k, lnx_w, lnx_b):
    B, L, _ = z.shape
    f32 = jnp.float32
    zf = z.astype(f32)
    zprev = jnp.concatenate([shift_prev.astype(f32)[:, None], zf[:, :-1]], 1)
    zs = zf + (zprev - zf) * mu.astype(f32)
    o = 3 * RWKV_WIDTH
    r = zs[..., :RWKV_WIDTH]
    k = zs[..., RWKV_WIDTH:2 * RWKV_WIDTH]
    v = zs[..., 2 * RWKV_WIDTH:o]
    wd = zs[..., o:o + DECAY_LORA]
    ad = zs[..., o + DECAY_LORA:o + DECAY_LORA + AAA_LORA]
    gd = zs[..., o + DECAY_LORA + AAA_LORA:]
    w = -jax.nn.softplus(-(w0.astype(f32) + jnp.tanh(wd) @ w2.astype(f32))) - 0.5
    a = jax.nn.sigmoid(a0.astype(f32) + ad @ a2.astype(f32))
    g = jax.nn.sigmoid(gd) @ g2.astype(f32)
    heads = lambda t: t.reshape(B, L, N_HEADS, HEAD_DIM)
    kk = heads(k * k_k.astype(f32))
    kk = kk / jnp.maximum(jnp.sqrt(jnp.sum(kk * kk, -1, keepdims=True)), 1e-12)
    k = k * (1.0 + (a - 1.0) * k_a.astype(f32))
    decay = jnp.exp(-jnp.exp(w))
    tm = lambda t: jnp.moveaxis(t, 1, 0)
    seqs = (tm(heads(r)), tm(heads(decay)), tm(heads(k)), tm(heads(v)), tm(-kk), tm(kk * heads(a)))

    def step(S, inp):
        rt, wt, kt, vt, at, bt = inp
        sa = jnp.einsum('bhij,bhj->bhi', S, at)
        S = S * wt[:, :, None, :] + sa[..., None] * bt[:, :, None, :] + vt[..., None] * kt[:, :, None, :]
        return S, jnp.einsum('bhij,bhj->bhi', S, rt)

    S_fin, ys = lax.scan(step, S0.astype(f32), seqs)
    y = jnp.moveaxis(ys, 0, 1)
    mean = jnp.mean(y, -1, keepdims=True)
    var = jnp.mean(jnp.square(y - mean), -1, keepdims=True)
    y = ((y - mean) * lax.rsqrt(var + LNX_EPS)).reshape(B, L, RWKV_WIDTH) * lnx_w.astype(f32) + lnx_b.astype(f32)
    bonus = jnp.sum(heads(r * k * r_k.astype(f32)), -1, keepdims=True) * heads(v)
    y = (y + bonus.reshape(B, L, RWKV_WIDTH)) * g
    return y.astype(z.dtype), S_fin, z[:, -1]

def _moe(h, w_router, b_router, w_gate, w_up, w_down):
    T, D = h.shape
    f32 = jnp.float32
    scores = jax.nn.sigmoid(jnp.einsum('td,de->te', h, w_router).astype(f32))
    sel = scores + b_router.astype(f32)
    gscore = jnp.sum(lax.top_k(sel.reshape(T, N_EXPERT_GROUPS, EXPERTS_PER_GROUP), GROUP_SCORE_K)[0], -1)
    gbest = jnp.argmax(gscore, -1)
    in_group = (jnp.arange(N_EXPERTS) // EXPERTS_PER_GROUP)[None, :] == gbest[:, None]
    _, idx = lax.top_k(jnp.where(in_group, sel, -jnp.inf), TOP_K)
    wts = jnp.take_along_axis(scores, idx, 1)
    wts = wts / jnp.sum(wts, -1, keepdims=True)
    A = T * TOP_K
    e_flat = idx.reshape(A)
    tok_flat = jnp.repeat(jnp.arange(T, dtype=jnp.int32), TOP_K)
    w_flat = wts.reshape(A)
    order = jnp.argsort(e_flat, stable=True)
    e_sorted = e_flat[order]
    counts = jnp.bincount(e_flat, length=N_EXPERTS)
    start = jnp.cumsum(counts) - counts
    padded = (counts + MOE_BLOCK - 1) // MOE_BLOCK * MOE_BLOCK
    pend = jnp.cumsum(padded)
    pstart = pend - padded
    dest = pstart[e_sorted] + (jnp.arange(A) - start[e_sorted])
    n_blocks = -(-(A + N_EXPERTS * (MOE_BLOCK - 1)) // MOE_BLOCK)
    R = n_blocks * MOE_BLOCK
    row_tok = jnp.zeros((R,), jnp.int32).at[dest].set(tok_flat[order])
    row_w = jnp.zeros((R,), f32).at[dest].set(w_flat[order])
    block_e = jnp.searchsorted(pend, jnp.arange(n_blocks) * MOE_BLOCK, side='right')
    block_e = jnp.minimum(block_e, N_EXPERTS - 1)

    def run_block(args):
        toks, e = args
        xb = h[toks]
        act = jax.nn.silu(xb @ w_gate[e]) * (xb @ w_up[e])
        return act @ w_down[e]

    yb = lax.map(run_block, (row_tok.reshape(n_blocks, MOE_BLOCK), block_e))
    y = yb.reshape(R, D) * row_w[:, None].astype(yb.dtype)
    return jnp.zeros_like(h).at[row_tok].add(y.astype(h.dtype))

def _trunk(x, c, st_wkv, st_pool, st_shift, pos0, prm):
    B, L, D = x.shape
    new_wkv, new_pool, new_shift = [], [], []
    for l in range(DEPTH):
        mod = jnp.einsum('bd,dk->bk', jax.nn.silu(c), prm['w_ada'][l]) + prm['b_ada'][l]
        sh_a, sc_a, gt_a, sh_m, sc_m, gt_m = jnp.split(mod, 6, axis=-1)
        h = _ada_norm(x, prm['norm1_g'][l], sh_a, sc_a)
        proj = jnp.einsum('bld,dp->blp', h, prm['w_in'][l])
        y_pool, buf = _pool_mixer(proj[..., :POOL_WIDTH], st_pool[l], pos0, prm['w_pool'][l], prm['pool_scale'][l])
        y_rwkv, S_fin, sh = _rwkv7(proj[..., POOL_WIDTH:], st_shift[l], st_wkv[l], prm['mu_shift'][l],
                                   prm['w0'][l], prm['w2'][l], prm['a0'][l], prm['a2'][l], prm['g2'][l],
                                   prm['k_k'][l], prm['k_a'][l], prm['r_k'][l], prm['lnx_w'][l], prm['lnx_b'][l])
        mix = jnp.einsum('blm,md->bld', jnp.concatenate([y_pool, y_rwkv], -1), prm['w_out'][l])
        x = x + (gt_a[:, None, :] * mix).astype(x.dtype)
        h2 = _ada_norm(x, prm['norm2_g'][l], sh_m, sc_m)
        ff = _moe(h2.reshape(B * L, D), prm['w_router'], prm['b_router'],
                  prm['w_gate'][l], prm['w_up'][l], prm['w_down'][l]).reshape(B, L, D)
        x = x + (gt_m[:, None, :] * ff).astype(x.dtype)
        new_wkv.append(S_fin.astype(x.dtype))
        new_pool.append(buf.astype(x.dtype))
        new_shift.append(sh.astype(x.dtype))
    y = _rmsnorm(x, prm['final_g']).astype(x.dtype)
    return y, jnp.stack(new_wkv), jnp.stack(new_pool), jnp.stack(new_shift)

def setup_inputs(seed: int = 0) -> dict:
    key = jax.random.key(seed)
    k = jax.random.split(key, 32)
    f32 = jnp.float32
    D = D_MODEL
    nrm = lambda kk, shape, s: jax.random.normal(kk, shape, f32) * s
    return {
        'x_prompt': nrm(k[0], (BATCH, SEQ, D), 1.0),
        'x_sample': nrm(k[1], (DEC_BATCH, DEC_SEQ, D), 1.0),
        'state_wkv': nrm(k[2], (DEPTH, DEC_BATCH, N_HEADS, HEAD_DIM, HEAD_DIM), 0.3),
        'state_pool': nrm(k[3], (DEPTH, DEC_BATCH, POOL_BUF, POOL_WIDTH), 1.0),
        'state_shift': nrm(k[4], (DEPTH, DEC_BATCH, SHIFT_WIDTH), 1.0),
        'c_prompt': nrm(k[5], (BATCH, D), 1.0),
        'c_sample': nrm(k[6], (DEC_BATCH, D), 1.0),
        'w_ada': nrm(k[7], (DEPTH, D, 6 * D), 0.5 * D ** -0.5),
        'b_ada': nrm(k[8], (DEPTH, 6 * D), 0.02),
        'norm1_g': 1.0 + nrm(k[9], (DEPTH, D), 0.02),
        'norm2_g': 1.0 + nrm(k[10], (DEPTH, D), 0.02),
        'w_in': nrm(k[11], (DEPTH, D, PROJ_WIDTH), D ** -0.5),
        'w_pool': nrm(k[12], (DEPTH, len(POOL_WINDOWS), POOL_GROUP, POOL_GROUP), POOL_GROUP ** -0.5),
        'pool_scale': 1.0 + nrm(k[13], (DEPTH, POOL_WIDTH), 0.1),
        'mu_shift': jax.random.uniform(k[14], (DEPTH, SHIFT_WIDTH), f32, 0.0, 1.0),
        'w0': jax.random.uniform(k[15], (DEPTH, RWKV_WIDTH), f32, -4.0, 0.0),
        'w2': nrm(k[16], (DEPTH, DECAY_LORA, RWKV_WIDTH), 0.1 * DECAY_LORA ** -0.5),
        'a0': nrm(k[17], (DEPTH, RWKV_WIDTH), 0.1),
        'a2': nrm(k[18], (DEPTH, AAA_LORA, RWKV_WIDTH), 0.1 * AAA_LORA ** -0.5),
        'g2': nrm(k[19], (DEPTH, GATE_LORA, RWKV_WIDTH), GATE_LORA ** -0.5),
        'k_k': 0.85 + nrm(k[20], (DEPTH, RWKV_WIDTH), 0.05),
        'k_a': 1.0 + nrm(k[21], (DEPTH, RWKV_WIDTH), 0.05),
        'r_k': nrm(k[22], (DEPTH, RWKV_WIDTH), 0.1),
        'lnx_w': 1.0 + nrm(k[23], (DEPTH, RWKV_WIDTH), 0.02),
        'lnx_b': nrm(k[24], (DEPTH, RWKV_WIDTH), 0.02),
        'w_out': nrm(k[25], (DEPTH, MIX_WIDTH, D), MIX_WIDTH ** -0.5),
        'w_router': nrm(k[26], (D, N_EXPERTS), D ** -0.5),
        'b_router': nrm(k[27], (N_EXPERTS,), 0.01),
        'w_gate': nrm(k[28], (DEPTH, N_EXPERTS, D, D_EXPERT), D ** -0.5),
        'w_up': nrm(k[29], (DEPTH, N_EXPERTS, D, D_EXPERT), D ** -0.5),
        'w_down': nrm(k[30], (DEPTH, N_EXPERTS, D_EXPERT, D), D_EXPERT ** -0.5),
        'final_g': 1.0 + nrm(k[31], (D,), 0.02),
    }

def reference(x_prompt, x_sample, state_wkv, state_pool, state_shift, c_prompt, c_sample,
              w_ada, b_ada, norm1_g, norm2_g, w_in, w_pool, pool_scale, mu_shift,
              w0, w2, a0, a2, g2, k_k, k_a, r_k, lnx_w, lnx_b, w_out,
              w_router, b_router, w_gate, w_up, w_down, final_g):
    prm = dict(w_ada=w_ada, b_ada=b_ada, norm1_g=norm1_g, norm2_g=norm2_g, w_in=w_in, w_pool=w_pool,
               pool_scale=pool_scale, mu_shift=mu_shift, w0=w0, w2=w2, a0=a0, a2=a2, g2=g2,
               k_k=k_k, k_a=k_a, r_k=r_k, lnx_w=lnx_w, lnx_b=lnx_b, w_out=w_out,
               w_router=w_router, b_router=b_router, w_gate=w_gate, w_up=w_up, w_down=w_down,
               final_g=final_g)
    B = x_prompt.shape[0]
    dt = x_prompt.dtype
    z_wkv = jnp.zeros((DEPTH, B, N_HEADS, HEAD_DIM, HEAD_DIM), dt)
    z_pool = jnp.zeros((DEPTH, B, POOL_BUF, POOL_WIDTH), dt)
    z_shift = jnp.zeros((DEPTH, B, SHIFT_WIDTH), dt)
    y_prompt, wkv_p, pool_p, shift_p = _trunk(x_prompt, c_prompt, z_wkv, z_pool, z_shift, 0, prm)
    y_sample, wkv_s, pool_s, shift_s = _trunk(x_sample, c_sample, state_wkv, state_pool, state_shift, PAST_LEN, prm)
    return (y_prompt, y_sample, wkv_p, pool_p, shift_p, wkv_s, pool_s, shift_s)


_drawn_inputs = setup_inputs


def setup_inputs(seed=0):
    import zlib

    import numpy as np

    out = dict(_drawn_inputs(seed))
    spreads = {}
    factors = {'w2': 3.873, 'lnx_w': 12.434, 'lnx_b': 13.619, 'final_g': 8.276, 'norm2_g': 3.215}
    for name, (base, spread) in spreads.items():
        noise = np.random.default_rng([zlib.crc32(name.encode()), seed]).standard_normal(out[name].shape)
        drawn = base * np.exp(spread * noise) if base else spread * noise
        out[name] = __import__('jax').numpy.asarray(drawn.astype(out[name].dtype))
    for name, factor in factors.items():
        out[name] = (out[name] * factor).astype(out[name].dtype)
    return out
```

```python
from contextlib import ExitStack

import concourse.bass as bass
from concourse import mybir
from concourse.alu_op_type import AluOpType as ALU

ACT = mybir.ActivationFunctionType
AX = mybir.AxisListType
F32 = mybir.dt.float32
I32 = mybir.dt.int32
U32 = mybir.dt.uint32

P = 128
D = 2048
KT = D // P
NP_TOK, NB, NL = 256, 8, 8
T = NP_TOK + NB * NL
TILES = [(0, 128), (128, 128), (256, 64)]
NC9 = 1 + NB
WIN = (2, 4, 8, 16)
BUF = 15
PW = 1024
RW = 1024
HD = 64
PAIRS = RW // P
SH = 3 * RW + 64 + 64 + 160
PROJ = PW + SH
C = 64
NCH = T // C
EXT = BUF + NP_TOK
EXTS = BUF + NL
ZS = 1 + NL
ZW = 1 + NP_TOK + NB * ZS
NE, NG, EPG = 16, 4, 4
FE = 1024
FT = FE // P
SLOT = 64
MAXB = NE + (2 * T - NE) // SLOT
YROWS = 28 * SLOT
RMS_EPS, LNX_EPS = 1e-6, 64e-5
DECAY = 0.6065306597126334
K_MU, K_W0, K_A0, K_KK, K_KA, K_RK, K_LW, K_LB = 0, 3, 4, 5, 6, 7, 8, 9
R_PS, R_G1, R_G2, R_MUT = 80, 88, 104, 120
NROW = 123
NADA = 6 * KT
SH_A, SC_A, GT_A, SH_M, SC_M, GT_M = (k * KT for k in range(6))


class Order:

    def __init__(self, eng, sem, base=0):
        self.eng, self.sem, self.base, self.n = eng, sem, base, 0

    def did(self, ins):
        self.n += 1
        ins.then_inc(self.sem, 1)
        return ins

    def settle(self):
        self.eng.wait_ge(self.sem, self.base + self.n)


def clear(nc, sems):
    nums = sorted(s.num for s in sems)
    runs = []
    for n in nums:
        if runs and n == runs[-1][1]:
            runs[-1][1] = n + 1
        else:
            runs.append([n, n + 1])
    with nc.Block() as block:
        @block.gpsimd
        def _(pool):
            for lo, hi in runs:
                pool.sem_clear(range(lo, hi))


def build(nc, A, O):
    ctx = ExitStack()
    with ctx:
        def sb(name, shape, dt=F32, scope=None):
            return (scope or ctx).enter_context(nc.sbuf_tensor(name, shape, dt))

        ybuf = nc.dram_tensor("ybuf", (YROWS, D), F32, kind="Internal").ap()
        own = {}

        def sem(name, scope=None):
            handle = (scope or ctx).enter_context(nc.semaphore(name))
            own.setdefault(id(scope), []).append(handle)
            return handle

        PS = ctx.enter_context(nc.psum_tensor("PS", [P, 8, 512], F32))
        ident = sb("ident", [P, P])
        eps = sb("eps", [P, 2])
        PT = sb("PT", [P, P])
        bT = sb("bT", [P, NADA])
        adaT = sb("adaT", [P, NADA, NC9])
        silT = sb("silT", [P, KT, 32])
        catT = sb("catT", [P, KT, T])

        early = ExitStack()
        prep = ExitStack()
        ctx.enter_context(early)
        hT = sb("hT", [P, KT, T], scope=early)
        wbuf = sb("wbuf", [P, 3, KT, P], scope=early)
        abuf = sb("abuf", [P, 2, KT // 2, 512], scope=early)
        asum = sb("asum", [P, 512], scope=early)
        sprevT = sb("sprevT", [P, 27, NB], scope=early)
        spT = sb("spT", [P, 8, NB * BUF], scope=early)
        onesb = sb("onesb", [P, P], scope=early)
        onesd = sb("onesd", [P, P], scope=early)
        w_in = A["w_in"][0].rearrange("(k p) n -> p k n", p=P)
        w_ada = A["w_ada"][0].rearrange("(u k p) n -> u p k n", p=P, u=2)
        ld_w = [sem(f"ld_w{j}") for j in range(3)]
        past_pe, past_ve, past_pool = (sem(n) for n in "past_pe past_ve past_pool".split())

        phase_a(nc, A, O, sb, sem, prep, locals())
        clear(nc, own[id(prep)])
        prep.close()
        heads = ExitStack()
        phase_b(nc, A, O, sb, sem, heads, locals())
        clear(nc, own[id(heads)])
        heads.close()
        early.close()
        phase_mix(nc, A, O, sb, sem, locals())


def phase_a(nc, A, O, sb, sem, sc, G):
    PS, ident, eps, PT, bT, adaT, silT = (G[k] for k in "PS ident eps PT bT adaT silT".split())
    hT, wbuf, abuf, sprevT, spT, onesb, onesd, asum = (G[k] for k in "hT wbuf abuf sprevT spT onesb onesd asum".split())
    w_in, w_ada, ld_w = G["w_in"], G["w_ada"], G["ld_w"]
    with ExitStack() as es:
        x = sb("x_a", [P, 3, D], scope=sc)
        junk = sb("junk", [P, D], scope=sc)
        crow = sb("crow", [NC9, D], scope=sc)
        srow = sb("srow", [NB, SH], scope=sc)
        prow = sb("prow", [P, P], scope=sc)
        brow = sb("brow", [NADA, P], scope=sc)
        poolrow = sb("poolrow", [NB * BUF, PW], scope=sc)
        ss = sb("ss", [P, 4], scope=sc)
        ss2 = sb("ss2", [P, 4], scope=sc)
        gs = sb("gs", [P, KT, NC9], scope=sc)
        asum4 = sb("asum4", [P, 4, NC9], scope=sc)
        ld_x = [sem(f"ld_x{i}", sc) for i in range(3)]
        ld_c, ld_s, ld_p, ld_b, ld_pool = (sem(n, sc) for n in "ld_c ld_s ld_p ld_b ld_pool".split())
        ld_a = [sem(f"ld_a{j}", sc) for j in range(2)]
        id_ready, prow_zero, cs_ready = (sem(n, sc) for n in "id_ready prow_zero cs_ready".split())
        t_par, t_c, t_s, t_pool, t_x, x_evac, ada_mm, ada_used, ada_psum_free = (
            sem(n, sc) for n in "t_par t_c t_s t_pool t_x x_evac ada_mm ada_used ada_psum_free".split())
        ada_copied, ada_red, par_ev, c_ev, sq_done, sqrt_done, xs_done, gp_seq, ve_seq, sil_a, pe_own = (
            sem(n, sc) for n in "ada_copied ada_red par_ev c_ev sq_done sqrt_done xs_done gp_seq ve_seq sil_a pe_own".split())
        block = es.enter_context(nc.Block())

        @block.sync
        def _(sp):
            sp.dma_start(crow[0:1, :], A["c_prompt"]).then_inc(ld_c, 16)
            sp.dma_start(crow[1:NC9, :], A["c_sample"]).then_inc(ld_c, 16)
            for u in range(2):
                sp.dma_start(abuf[:, u], w_ada[u, :, :, 0:512]).then_inc(ld_a[u], 16)
            with sp.Fori(1, 8) as i:
                for u in range(2):
                    sp.wait_ge(ada_used, i * 2 - 1 + u)
                    sp.dma_start(abuf[:, u], w_ada[u, :, :, bass.ds(i * 512, 512)]).then_inc(ld_a[u], 16)
            for j in range(3):
                sp.dma_start(wbuf[:, j], w_in[:, :, j * P:(j + 1) * P]).then_inc(ld_w[j], 16)

        @block.scalar
        def _(act):
            for i, (t0, n) in enumerate(TILES):
                src = A["x_prompt"][0, t0:t0 + n] if i < 2 else A["x_sample"].rearrange("b l d -> (b l) d")
                act.dma_start(x[0:n, i, :], src).then_inc(ld_x[i], 16)
            act.dma_start(brow[:, :], A["b_ada"][0].rearrange("(r c) -> r c", c=P)).then_inc(ld_b, 16)
            act.dma_start(srow[:, :], A["state_shift"][0]).then_inc(ld_s, 16)
            act.dma_start(poolrow[:, :], A["state_pool"][0].rearrange("b l d -> (b l) d")).then_inc(ld_pool, 16)
            act.wait_ge(prow_zero, 1)
            rows = [("mu_shift", 0, 0, 24)] + [(n, 24 + 8 * k, 0, 8) for k, n in enumerate(
                ["w0", "a0", "k_k", "k_a", "r_k", "lnx_w", "lnx_b", "pool_scale"])]
            rows += [("norm1_g", R_G1, 0, 16), ("norm2_g", R_G2, 0, 16), ("mu_shift", R_MUT, 24, 2)]
            for name, at, r0, n in rows:
                act.dma_start(prow[at:at + n, :], A[name][0, r0 * P:(r0 + n) * P].rearrange("(r c) -> r c", c=P)
                              ).then_inc(ld_p, 16)
            act.dma_start(prow[R_MUT + 2:R_MUT + 3, 0:32], A["mu_shift"][0:1, 26 * P:SH]).then_inc(ld_p, 16)
            act.wait_ge(ld_c, 32)
            nc.scalar.activation(junk[0:NC9, :], crow[:, :], ACT.Sigmoid).then_inc(sil_a, 1)
            act.wait_ge(cs_ready, 1)
            for i, (t0, n) in enumerate(TILES):
                act.wait_ge(ld_x[i], 16)
                nc.scalar.activation(junk[0:n, :], x[0:n, i, :], ACT.Square,
                                     accum_out=ss[0:n, i:i + 1]).then_inc(sq_done, 1)
                act.wait_ge(sq_done, i + 1)
            act.wait_ge(gp_seq, 1)
            for i, (t0, n) in enumerate(TILES):
                nc.scalar.activation(ss2[0:n, i:i + 1], ss[0:n, i:i + 1], ACT.Sqrt, bias=eps[0:n, 0:1],
                                     scale=1.0 / D).then_inc(sqrt_done, 1)
            for k in range(0, KT, 2):
                act.wait_ge(t_x, k + 1)
                nc.scalar.copy(hT[:, k, :], PS[:, 4 + k % 4, 0:T]).then_inc(x_evac, 1)

        @block.gpsimd
        def _(pool):
            nc.gpsimd.memset(eps[:, 0:1], RMS_EPS)
            nc.gpsimd.memset(eps[:, 1:2], LNX_EPS).then_inc(gp_seq, 1)
            nc.gpsimd.memset(ident[:, :], 0.0).then_inc(gp_seq, 1)
            pool.wait_ge(gp_seq, 2)
            nc.gpsimd.affine_select(out=ident[:, :], in_=ident[:, :], compare_op=ALU.not_equal, fill=1.0, base=0,
                                    pattern=[[-1, P]], channel_multiplier=1).then_inc(id_ready, 1)
            for t, v in ((onesb, 1.0), (onesd, 1.0 / HD)):
                nc.gpsimd.memset(t[:, :], 0.0).then_inc(gp_seq, 1)
            pool.wait_ge(gp_seq, 4)
            for t, v in ((onesb, 1.0), (onesd, 1.0 / HD)):
                nc.gpsimd.memset(t[0:64, 0:64], v)
                nc.gpsimd.memset(t[64:P, 64:P], v)

        @block.tensor
        def _(pe):
            pe.wait_ge(id_ready, 1)
            pe.wait_ge(cs_ready, 1)
            for k in range(KT):
                m = nc.tensor.transpose(PS[:, 0, k * NC9:(k + 1) * NC9], crow[:, k * P:(k + 1) * P],
                                        ident[0:NC9, 0:NC9])
            m.then_inc(t_c, 1)
            pe.wait_ge(ld_p, 16 * 13)
            nc.tensor.transpose(PS[:, 1, 0:NROW], prow[0:NROW, :], ident[0:NROW, 0:NROW])
            pe.wait_ge(ld_b, 16)
            nc.tensor.transpose(PS[:, 1, P:P + NADA], brow[:, :], ident[0:NADA, 0:NADA]).then_inc(t_par, 1)
            pe.wait_ge(ld_s, 16)
            for j in range(27):
                n = min(P, SH - j * P)
                m = nc.tensor.transpose(PS[0:n, 2, j * NB:(j + 1) * NB], srow[:, j * P:j * P + n],
                                        ident[0:NB, 0:NB])
            m.then_inc(t_s, 1)
            pe.wait_ge(ld_pool, 16)
            for j in range(8):
                m = nc.tensor.transpose(PS[:, 4 + j // 4, (j % 4) * 120:(j % 4) * 120 + 120],
                                        poolrow[:, j * P:(j + 1) * P], ident[0:120, 0:120])
            m.then_inc(t_pool, 1)
            pe.wait_ge(par_ev, 1)
            pe.wait_ge(xs_done, 3)
            for k in range(KT):
                if k >= 4:
                    pe.wait_ge(x_evac if k % 2 == 0 else ve_seq, k // 2 - 1 if k % 2 == 0 else 20 + k // 2 - 1)
                for i, (t0, n) in enumerate(TILES):
                    m = nc.tensor.transpose(PS[:, 4 + k % 4, t0:t0 + n], x[0:n, i, k * P:(k + 1) * P],
                                            ident[0:n, 0:n])
                m.then_inc(t_x, 1)
            pe.wait_ge(c_ev, 1)
            with pe.Fori(0, 8) as i:
                for u in range(2):
                    pe.wait_ge(ld_a[u], 16 * i + 16)
                    if u == 0:
                        pe.wait_ge(ada_psum_free, i + 1)
                    ada_half(nc, PS[:, 0, :], silT, abuf, u).then_inc(ada_used, 1)
                pe.wait_ge(ada_copied, i + 1)
                ada_turn(nc, PS[:, 1, :], asum, ident).then_inc(ada_mm, 1)

        @block.vector
        def _(ve):
            o = Order(ve, ve_seq)
            nc.vector.memset(prow[:, :], 0.0).then_inc(prow_zero, 1)
            ve.wait_ge(sil_a, 1)
            nc.vector.tensor_tensor(crow[:, :], crow[:, :], junk[0:NC9, :], ALU.mult).then_inc(cs_ready, 1)
            ve.wait_ge(t_c, 1)
            o.did(nc.vector.memset(silT[:, :, :], 0.0))
            o.settle()
            nc.vector.tensor_copy(silT[:, :, 0:NC9], PS[:, 0, 0:KT * NC9].rearrange("p (k c) -> p k c", c=NC9)
                                  ).then_inc(c_ev, 1)
            ve.wait_ge(t_par, 1)
            o.did(nc.vector.tensor_copy(PT[:, 0:NROW], PS[:, 1, 0:NROW]))
            o.did(nc.vector.tensor_copy(bT[:, :], PS[:, 1, P:P + NADA]))
            ve.wait_ge(t_s, 1)
            o.did(nc.vector.tensor_copy(sprevT[:, 0:26, :], PS[:, 2, 0:26 * NB].rearrange("p (j b) -> p j b", b=NB)))
            o.did(nc.vector.tensor_copy(sprevT[0:32, 26, :], PS[0:32, 2, 26 * NB:27 * NB]))
            ve.wait_ge(t_pool, 1)
            for h in range(2):
                m = o.did(nc.vector.tensor_copy(spT[:, 4 * h:4 * h + 4, :],
                                                PS[:, 4 + h, 0:480].rearrange("p (j b) -> p j b", b=120)))
            o.settle()
            o.did(nc.vector.memset(ss2[:, 3:4], 0.0))
            nc.vector.memset(ss[:, 3:4], 0.0).then_inc(par_ev, 1)
            for i, (t0, n) in enumerate(TILES):
                ve.wait_ge(sqrt_done, i + 1)
                o.did(nc.vector.reciprocal(ss2[0:n, i:i + 1], ss2[0:n, i:i + 1]))
            o.settle()
            for i, (t0, n) in enumerate(TILES):
                nc.vector.tensor_scalar(x[0:n, i, :], x[0:n, i, :], ss2[0:n, i:i + 1], None, ALU.mult
                                        ).then_inc(xs_done, 1)
            while o.n < 20:
                o.did(nc.vector.memset(ss[:, 3:4], 0.0))
                o.settle()
            for k in range(1, KT, 2):
                ve.wait_ge(t_x, k + 1)
                o.did(nc.vector.tensor_copy(hT[:, k, :], PS[:, 4 + k % 4, 0:T]))
            o.settle()
            ve.sem_inc(ada_psum_free, 1)
            with ve.Fori(0, 8) as i:
                ve.wait_ge(ada_used, 2 * i + 2)
                nc.vector.tensor_copy(asum[:, :], PS[:, 0, :]).then_inc(ada_copied, 1)
                ve.wait_ge(ada_mm, i + 1)
                nc.vector.tensor_reduce(asum4[:, :, :], ada_parts(PS[:, 1, :]), AX.X, ALU.add).then_inc(ada_red, 1)
                ve.wait_ge(ada_red, i + 1)
                nc.vector.tensor_tensor(adaT[:, bass.ds(i * 4, 4), :], asum4[:, :, :],
                                        bT[:, bass.ds(i * 4, 4)].unsqueeze(2).broadcast_to([P, 4, NC9]),
                                        ALU.add).then_inc(ada_psum_free, 1)
            ve.wait_ge(ada_psum_free, 9)
            o.did(nc.vector.tensor_scalar(gs[:, :, :], adaT[:, SC_A:SC_A + KT, :], 1.0, None, ALU.add))
            o.settle()
            o.did(nc.vector.tensor_tensor(gs[:, :, :], gs[:, :, :],
                                          PT[:, R_G1:R_G1 + KT].unsqueeze(2).broadcast_to([P, KT, NC9]), ALU.mult))
            o.settle()
            ve.wait_ge(x_evac, KT // 2)
            modulate(nc, ve, o, hT, gs, adaT[:, SH_A:SH_A + KT, :])


def ada_half(nc, psum, silT, abuf, u):
    for k in range(KT // 2):
        kt, g = u * (KT // 2) + k, k % 4
        m = nc.tensor.matmul(psum[32 * g:32 * g + 32, :], silT[:, kt, :], abuf[:, u, k, :],
                             start=(kt < 4), stop=(kt >= KT - 4))
    return m


def ada_turn(nc, psum, asum, ident):
    for m_ in range(4):
        m = nc.tensor.transpose(psum[:, m_ * P:(m_ + 1) * P], asum[:, m_ * P:(m_ + 1) * P], ident[:, :])
    return m


def ada_parts(psum):
    return psum.rearrange("p (m g c) -> p m c g", m=4, g=4)[:, :, 0:NC9, :]


def modulate(nc, ve, o, hT, gs, sh):
    for k in range(KT):
        o.did(nc.vector.tensor_scalar(hT[:, k, 0:NP_TOK], hT[:, k, 0:NP_TOK], gs[:, k, 0:1], sh[:, k, 0:1],
                                      ALU.mult, ALU.add))
    s = hT[:, :, NP_TOK:T].rearrange("p k (b l) -> p k b l", l=NL)
    for op, v in ((ALU.mult, gs), (ALU.add, sh)):
        o.did(nc.vector.tensor_tensor(s, s, v[:, :, 1:NC9].unsqueeze(3).broadcast_to([P, KT, NB, NL]), op))
        o.settle()


def ext_prompt(e, k0=0, n=NP_TOK):
    return e[:, BUF + k0:BUF + k0 + n]


def ext_sample(e, k0=BUF, n=NL):
    return e[:, EXT:EXT + NB * EXTS].rearrange("p (b l) -> p b l", l=EXTS)[:, :, k0:k0 + n]


N_DVE, N_POOL = 59, 6
NPRE = 11
LEVELS = (2, 4, 8, 16)


def phase_b(nc, A, O, sb, sem, sc, G):
    PS, ident, eps, PT, bT, adaT, silT, catT = (G[k] for k in "PS ident eps PT bT adaT silT catT".split())
    hT, wbuf, abuf, sprevT, spT, onesb, onesd, asum = (
        G[k] for k in "hT wbuf abuf sprevT spT onesb onesd asum".split())
    w_in, w_ada, ld_w = G["w_in"], G["w_ada"], G["ld_w"]
    past_pe, past_ve, past_pool = G["past_pe"], G["past_ve"], G["past_pool"]
    W = [PS[:, 4 + b, :] for b in range(4)]
    with ExitStack() as es:
        t = lambda name, shape, dt=F32: sb(name, shape, dt, scope=sc)
        s = lambda names: [sem(n, None if n in ("ld_lora", "ld_sraw", "out_w", "out_p") else sc)
                           for n in names.split()]
        EW = EXT + NB * EXTS
        sraw, s0t, sfin, sout = (t(n, [P, NB, C]) for n in "sraw s0t sfin sout".split())
        ext, sa, sb_ = (x_[:, :, :].rearrange("p b i -> p (b i)")[:, 0:EW] for x_ in (sout, s0t, sfin))
        uvx = t("uvx", [P, 2, NB, C])
        rc = uvx[:, :, :, :].rearrange("p h b i -> p (h b i)").rearrange("p (g n) -> p g n", g=4)
        zd = t("zd", [P, 3, T])
        pooled = zd[:, 0:2, :]
        late = t("late", [P, 2048])
        wp = late[:, :].rearrange("p (g k n) -> p g k n", g=4, k=2)
        kk, rn, ka, k2, rk, bv, tb, yw = (t(n, [P, T]) for n in "kk rn ka k2 rk bv tb yw".split())
        plast = t("plast", [P, P])
        ptok = t("ptok", [P, 512])
        mrow, mcol = t("mrow", [P, P], I32), t("mcol", [P, P], I32)
        mx, mf, mg = t("mx", [P, P], I32), kk[:, 0:P], rn[:, 0:P]
        mask_p, mask_s = t("mask_p", [P, P]), t("mask_s", [P, P])
        lvl_t, lvl_n = t("lvl_t", [C, 6, C], I32), t("lvl_n", [C, 6, C], I32)
        bmask, bmask_i = t("bmask", [P, NB]), t("bmask_i", [P, NB], I32)
        rmask = t("rmask", [P, T])
        lwa, lg1, lg2 = t("lwa", [P, T]), t("lg1", [P, T]), t("lg2", [P, T])
        lz, lzd = t("lz", [P, ZW]), bv
        w2a2, g2a, g2b = t("w2a2", [P, 2, P]), t("g2a", [P, P]), t("g2b", [P, P])
        pc, pomk = t("pc", [P, 10]), t("pomk", [P, 1])
        z3 = t("z3", [P, 3, ZW])
        zr, zk, vp = t("zr", [P, T]), t("zk", [P, T]), t("vp", [P, C + T])
        sg, aa, gg, cs, cse = (t(n, [P, T]) for n in "sg aa gg cs cse".split())
        lam, ilam, lame = (t(n, [P, T]) for n in "lam ilam lame".split())
        ra = t("ra", [P, NCH, 2, 2, C])
        bk = t("bk", [P, NCH, 2, C])
        bkt = late[:, 1280:1920].rearrange("p (c j) -> p c j", c=NCH)
        uv = t("uv", [P, NCH, P])
        mm = late[:, 0:1280].rearrange("p (c h x t) -> p c h x t", c=NCH, h=2, x=2)
        inv, invt, zs = (t(n, [P, 2, NCH, C]) for n in "inv invt zs".split())
        st, stl, pout = late[:, 1920:1984], late[:, 1984:2048], t("pout", [C, P])
        sgy, gs_, ys = t("sgy", [P, 2, C]), t("gs_", [P, P]), t("ys", [C, NCH, P])
        zlast = t("zlast", [P, 27, NC9])
        (k_iota, k_masks, k_zero, pre_mm, pre_ev, w_used, pool_in, pooled_ok, t_pool, t_pt, ptok_ok, ld_wp,
         ld_lora, ld_sraw, ld_a2) = s(
            "k_iota k_masks k_zero pre_mm pre_ev w_used pool_in pooled_ok t_pool2 t_pt ptok_ok ld_wp "
            "ld_lora ld_sraw ld_a2")
        ld_a2 = [ld_a2, sem("ld_a3", sc)]
        wu = s("wu0 wu1 wu2")
        (t_s0, s0_ev, l_q, l_a, l_g, lev, z_ev, z_done, pc_ok, t_ss, sq_ok, ss_ev, t_bs, rk_ok, bs_ev, bk_ok, ra_ok,
         v_ok, t_tok, tok_ev, t_mm, mm_ev, rst, t_z, z_cp, t_e, inv_ok, a_half, a_cp, a_turn, a_red, t_sg, sg_ev,
         t_g, g_ev, t_u, u_ev, t_st, st_ok, t_y, y_ev, uvx_ok, t_sf, sf_ok, t_so, so_ev, t_yt, yt_ev, t_mn, yc_ok,
         t_vr, vr_ev, fin, cs_ok, cse_ok, e_ok, k2_ok, t_proj, out_w, a_own, v_own, p_own, t_sh, sh_ev, out_p, mix_ev, ptok_ev, ext_ok, ext_used, lzs_ok, lora_ok, k_masks2) = s(
            "t_s0 s0_ev l_q l_a l_g lev z_ev z_done pc_ok t_ss sq_ok ss_ev t_bs rk_ok bs_ev bk_ok ra_ok "
            "v_ok t_tok tok_ev t_mm mm_ev rst t_z z_cp t_e inv_ok a_half a_cp a_turn a_red t_sg sg_ev "
            "t_g g_ev t_u u_ev t_st st_ok t_y y_ev uvx_ok t_sf sf_ok t_so so_ev t_yt yt_ev t_mn yc_ok "
            "t_vr vr_ev fin cs_ok cse_ok e_ok k2_ok t_proj out_w a_own v_own p_own t_sh sh_ev out_p mix_ev ptok_ev ext_ok ext_used lzs_ok lora_ok k_masks2")
        a4 = t("a4", [P, 4, NC9])
        zero = t("zero", [P, 512])
        y_zero = sem("y_zero")
        yz = G["ybuf"].rearrange("r d -> (r d)").rearrange("(p q n) -> p q n", p=P, n=512)
        YQ = YROWS * D // P // 512 // PAIRS
        shrow = abuf[0:NC9].rearrange("p u k n -> p (u k n)")
        state_in = A["state_wkv"][0].rearrange("b h i j -> (h i) b j")
        state_out = O["wkv_s"][0].rearrange("(q b) h i j -> b i q h j", b=2)
        prompt_out = O["wkv_p"][0, 0].rearrange("h i j -> i h j")
        RKV = [PW + j * RW for j in range(3)]
        LORA = PW + 3 * RW
        pre_cols = [(k * P, P) for k in range(8)] + [(LORA, P), (LORA + P, P), (LORA + 2 * P, 32)]
        WBASE = [16 * len(range(j, NPRE, 3)) for j in range(3)]
        UBASE = [len(range(j, NPRE, 3)) for j in range(3)]
        lvl_bank = [(0, 3, 1, 2, 0, 3), (1, 2, 0, 3, 1, 2)]
        def mix_out(act, g):
            act.wait_ge(t_pool, g + 1)
            for m_ in range(2):
                m = nc.scalar.activation(catT[:, 2 * g + m_, :], W[m_][:, 0:T], ACT.Copy,
                                         scale=PT[:, R_PS + 2 * g + m_:R_PS + 2 * g + m_ + 1])
            m.then_inc(mix_ev, 1)

        def masks(ve, o):
            ve.wait_ge(k_iota, 6)
            tt, ts = nc.vector.tensor_tensor, nc.vector.tensor_scalar
            o.did(tt(mx[:, :], mrow[:, :], mcol[:, :], ALU.bitwise_xor))
            o.did(tt(mask_p[:, 0:C], mcol[:, 0:C], mrow[:, 0:C], ALU.is_ge))
            o.did(tt(mask_p[:, C:P], mcol[:, C:P], mrow[:, C:P], ALU.is_gt))
            o.settle()
            o.did(ts(mf[:, :], mx[:, :], float(NL), None, ALU.is_lt))
            o.settle()
            o.did(tt(mask_s[:, :], mask_p[:, :], mf[:, :], ALU.mult))
            for n in range(6):
                o.settle()
                o.did(ts(mf[0:C, 0:C], mx[0:C, 0:C], float(2 ** n), None, ALU.is_ge))
                o.did(ts(mg[0:C, 0:C], mx[0:C, 0:C], float(2 ** (n + 1)), None, ALU.is_lt))
                o.settle()
                o.did(tt(mf[0:C, 0:C], mf[0:C, 0:C], mg[0:C, 0:C], ALU.mult))
                o.settle()
                o.did(tt(lvl_t[:, n, :], mf[0:C, 0:C], mask_p[0:C, C:P], ALU.mult))
                o.settle()
                o.did(ts(mg[0:C, 0:C], mask_p[0:C, 0:C], -1.0, 1.0, ALU.mult, ALU.add))
                o.settle()
                o.did(tt(lvl_n[:, n, :], mf[0:C, 0:C], mg[0:C, 0:C], ALU.mult))
                o.settle()
            o.did(ts(bmask[:, :], bmask_i[:, :], 0.0, None, ALU.is_ge))
            o.did(ts(mg[:, 0:NB], bmask_i[:, :], float(NL), None, ALU.is_lt))
            o.settle()
            o.did(tt(bmask[:, :], bmask[:, :], mg[:, 0:NB], ALU.mult))
            o.settle()

        block = es.enter_context(nc.Block())

        @block.sync
        def _(sp):
            sp.dma_start(wp[:, :, :, :], A["w_pool"][0].rearrange("g (k p) n -> p g k n", p=P)).then_inc(ld_wp, 16)
            for u in range(2):
                sp.dma_start(abuf[:, u], w_ada[u, :, :, 8 * 512:9 * 512]).then_inc(ld_a2[u], 16)
            for q in range(3, NPRE):
                c0, n = pre_cols[q]
                sp.wait_ge(wu[q % 3], q // 3)
                sp.dma_start(wbuf[:, q % 3, :, 0:n], w_in[:, :, c0:c0 + n]).then_inc(ld_w[q % 3], 16)
            for j in range(3):
                sp.wait_ge(wu[j], UBASE[j])
                sp.dma_start(wbuf[:, j], w_in[:, :, RKV[j]:RKV[j] + P]).then_inc(ld_w[j], 16)

            def pair(i, last):
                if last is not True:
                    for j in range(3):
                        sp.wait_ge(wu[j], UBASE[j] + 1 + i)
                        sp.dma_start(wbuf[:, j], w_in[:, :, bass.ds(RKV[j] + (i + 1) * P, P)]).then_inc(ld_w[j], 16)

            with sp.Fori(0, PAIRS - 1) as i:
                pair(i, False)
                for ch in range(2):
                    for u in range(2):
                        sp.wait_ge(a_half, 4 * i + 2 * ch + u + 1)
                        sp.dma_start(abuf[:, u], w_ada[u, :, :, bass.ds((2 * i + ch + 9) * 512, 512)]
                                     ).then_inc(ld_a2[u], 16)
            for u in range(2):
                sp.wait_ge(a_half, 4 * (PAIRS - 1) + u + 1)
                sp.dma_start(abuf[:, u], w_ada[u, :, :, 23 * 512:24 * 512]).then_inc(ld_a2[u], 16)

        @block.gpsimd
        def _(pool):
            for t_, n in ((mrow, 0), (mcol, 1)):
                for h in range(2):
                    nc.gpsimd.iota(t_[64 * h:64 * h + 64, :], pattern=[[0, 2], [n, C]], base=0,
                                   channel_multiplier=1 - n).then_inc(k_iota, 1)
            for h in range(2):
                nc.gpsimd.iota(bmask_i[64 * h:64 * h + 64, :], pattern=[[-8, NB]], base=0,
                               channel_multiplier=1).then_inc(k_iota, 1)
            pool.wait_ge(k_iota, 6)
            for x_ in (ext, rmask, ra, inv, invt, zs, gs_, uv, vp, z3, lz, g2b, lg2, w2a2, zlast, zero):
                nc.gpsimd.memset(x_ if x_ is ext else x_[:], 1.0 if x_ is rmask else 0.0).then_inc(p_own, 1)
            pool.wait_ge(p_own, 16)
            nc.gpsimd.memset(rmask[:, 0:NP_TOK:C], 0.0)
            nc.gpsimd.memset(rmask[:, NP_TOK:T:NL], 0.0)
            for g, w in enumerate(WIN):
                nc.gpsimd.memset(rc[:, g, w - 1:], 1.0 / w)
                for n in range(w - 1):
                    nc.gpsimd.memset(rc[:, g, n:n + 1], 1.0 / (n + 1))
            nc.gpsimd.memset(plast[:, :], 0.0).then_inc(k_zero, 1)
            pool.wait_ge(k_zero, 1)
            pool.dma_start(O["pool_s"][0, :, 0:BUF - NL, :], A["state_pool"][0, :, NL:BUF, :]).then_inc(out_p, 16)
            nc.gpsimd.dma_start(g2b[0:32, :], A["g2"][0, P:160, 0:P]).then_inc(ld_lora, 16)
            nc.gpsimd.dma_start(g2a[:, :], A["g2"][0, 0:P, 0:P]).then_inc(ld_lora, 16)
            nc.gpsimd.dma_start(w2a2[0:64, 0, :], A["w2"][0, :, 0:P]).then_inc(ld_lora, 16)
            nc.gpsimd.dma_start(w2a2[64:P, 1, :], A["a2"][0, :, 0:P]).then_inc(ld_lora, 16)
            nc.gpsimd.dma_start(sraw[:, :, :], state_in[0:P]).then_inc(ld_sraw, 16)
            for hf in range(2):
                pool.wait_ge(ptok_ev, hf + 1)
                pool.dma_start(O["pool_p"][0, 0, :, 512 * hf:512 * hf + 512], ptok[C - BUF:C, :]).then_inc(out_p, 16)
                pool.dma_start(O["pool_s"][0, :, BUF - NL:BUF, 512 * hf:512 * hf + 512], ptok[C:P, :]).then_inc(out_p, 16)
                pool.wait_ge(out_p, 16 * (3 + 2 * hf))
                pool.sem_inc(ptok_ok, 1)

            def pair(i, last):
                o = Order(pool, p_own, 16 + i * N_POOL)
                q_ = slice(YQ * i, YQ * i + YQ) if last is True else bass.ds(i * YQ, YQ)
                pool.dma_start(yz[:, q_, :], zero[:, :].unsqueeze(1).broadcast_to([P, YQ, 512])).then_inc(y_zero, 16)
                pool.wait_ge(t_y, NCH * i)
                pool.sem_inc(past_pool, 1)
                irep = ident[0:C, 0:C].unsqueeze(1).broadcast_to([C, 2 * NCH, C])
                for x_ in (inv, invt):
                    o.did(nc.gpsimd.tensor_copy(x_[0:C].rearrange("p h c t -> p (h c) t"), irep))
                o.did(nc.gpsimd.memset(uv[0:C, :, :], 0.0))
                o.settle()
                pool.sem_inc(rst, 1)
                pool.wait_ge(cs_ok, i + 1)
                pool.wait_ge(t_vr, i)
                nc.gpsimd.tensor_tensor(cse[:, :], cs[:, :], sg[:, :], ALU.subtract).then_inc(cse_ok, 1)
                pool.wait_ge(lev, 3 * i + 3)
                pool.sem_inc(past_pool, 1)
                o.did(nc.gpsimd.tensor_scalar(ka[:, :], aa[:, :], pc[:, K_KA:K_KA + 1], pomk[:, 0:1], ALU.mult, ALU.add))
                o.settle()
                pool.wait_ge(z_done, i + 1)
                nc.gpsimd.tensor_tensor(k2[:, :], zk[:, :], ka[:, :], ALU.mult).then_inc(k2_ok, 1)
                if last is not True:
                    n = i + 1
                    pool.wait_ge(l_g, i + 1)
                    nc.gpsimd.dma_start(g2b[0:32, :], A["g2"][0, P:160, bass.ds(n * P, P)]).then_inc(ld_lora, 16)
                    nc.gpsimd.dma_start(g2a[:, :], A["g2"][0, 0:P, bass.ds(n * P, P)]).then_inc(ld_lora, 16)
                    nc.gpsimd.dma_start(w2a2[0:64, 0, :], A["w2"][0, :, bass.ds(n * P, P)]).then_inc(ld_lora, 16)
                    nc.gpsimd.dma_start(w2a2[64:P, 1, :], A["a2"][0, :, bass.ds(n * P, P)]).then_inc(ld_lora, 16)
                    pool.wait_ge(t_s0, i + 1)
                    nc.gpsimd.dma_start(sraw[:, :, :], state_in[bass.ds(n * P, P)]).then_inc(ld_sraw, 16)
                pool.wait_ge(u_ev, NCH * i + NCH)
                for h in range(2):
                    o.did(nc.gpsimd.tensor_tensor(
                        uvx[:, h], uv[:, 4, C * h:C * h + C].unsqueeze(1).broadcast_to([P, NB, C]),
                        bmask[:, :].unsqueeze(2).broadcast_to([P, NB, C]), ALU.mult))
                o.settle()
                pool.sem_inc(uvx_ok, 1)
                pool.wait_ge(so_ev, 2 * i + 2)
                so = sout[:, :, :].rearrange("p (q h) j -> p q h j", h=2)
                for b in range(2):
                    for h in range(2):
                        head = slice(2 * i + h, 2 * i + h + 1) if last is True else bass.ds(2 * i + h, 1)
                        pool.dma_start(state_out[b, :, :, head, :], so[C * b:C * b + C, :, h:h + 1, :]
                                       ).then_inc(out_w, 16)
                pool.dma_start(prompt_out[:, bass.ds(2 * i, 2), :] if last is not True else
                               prompt_out[:, 2 * i:2 * i + 2, :],
                               pout[:, :].rearrange("p (h j) -> p h j", h=2)).then_inc(out_w, 16)
                assert o.n == N_POOL, o.n

            with pool.Fori(0, PAIRS - 1) as i:
                pair(i, False)
            pair(PAIRS - 1, True)
            pool.wait_ge(out_w, 16 * 5 * PAIRS)
            pool.wait_ge(y_zero, 16 * PAIRS)
            pool.wait_ge(sh_ev, 1)
            for dst, r0, nr in (("shift_p", 0, 1), ("shift_s", 1, NB)):
                pool.dma_start(O[dst][0], shrow[r0:r0 + nr, 0:SH]).then_inc(out_p, 16)
            pool.wait_ge(out_p, 16 * 7)

        @block.tensor
        def _(pe):
            def project(j, k0, k1, i):
                if k0 == 0:
                    pe.wait_ge(ld_w[j], WBASE[j] + 16 * (i + 2))
                    pe.wait_ge(z_done, i + 1)
                for k in range(k0, k1):
                    m = nc.tensor.matmul(PS[:, j, 0:T], wbuf[:, j, k, :], hT[:, k, :], start=(k == 0), stop=(k == KT - 1))
                if k1 == KT:
                    m.then_inc(wu[j], 1)

            def pool_mix(g):
                pe.wait_ge(pooled_ok, g + 1)
                pe.wait_ge(ld_wp, 16)
                for m_ in range(2):
                    for k in range(2):
                        m = nc.tensor.matmul(W[m_][:, 0:T], wp[:, g, k, m_ * P:(m_ + 1) * P], pooled[:, k, :],
                                             start=(k == 0), stop=(k == 1))
                m.then_inc(t_pool, 1)

            pe.wait_ge(k_zero, 1)
            for q in range(NPRE):
                c0, n = pre_cols[q]
                pe.wait_ge(ld_w[q % 3], 16 * (q // 3 + 1))
                if q >= 4:
                    pe.wait_ge(pre_ev, q - 3)
                for k in range(KT):
                    m = nc.tensor.matmul(PS[0:n, q % 4, 0:T], wbuf[:, q % 3, k, 0:n], hT[:, k, :],
                                         start=(k == 0), stop=(k == KT - 1))
                m.then_inc(wu[q % 3], 1)
                if 1 <= q <= 8:
                    pe.wait_ge(pool_in, q)
                    if q == 5:
                        pe.wait_ge(ptok_ok, 1)
                    nc.tensor.transpose(W[2][:, ((q - 1) % 4) * P:((q - 1) % 4 + 1) * P], plast[:, :], ident[:, :]
                                        ).then_inc(t_pt, 1)
                if q in (2, 4, 6, 8):
                    if q > 2:
                        pe.wait_ge(mix_ev, q // 2 - 1)
                    pool_mix(q // 2 - 1)
            pe.wait_ge(ptok_ok, 2)
            pe.wait_ge(mix_ev, 4)
            pe.wait_ge(lora_ok, 1)
            for j in range(3):
                pe.wait_ge(ld_w[j], WBASE[j] + 16)
                pe.wait_ge(pre_ev, NPRE)
                for k in range(KT):
                    m = nc.tensor.matmul(PS[:, j, 0:T], wbuf[:, j, k, :], hT[:, k, :], start=(k == 0), stop=(k == KT - 1))
                m.then_inc(wu[j], 1)

            def ada(i, ch, u):
                pe.wait_ge(ld_a2[u], 16 * (2 * i + ch + 1))
                if u == 0:
                    pe.wait_ge(a_red, 2 * i + ch)
                ada_half(nc, PS[:, 3, :], silT, abuf, u).then_inc(a_half, 1)

            def turn(i, ch):
                pe.wait_ge(a_cp, 2 * i + ch + 1)
                ada_turn(nc, PS[:, 3, :], asum, ident).then_inc(a_turn, 1)

            def pair(i, last):
                fill = (lambda j, k0, k1: None) if last is True else (lambda j, k0, k1: project(j, k0, k1, i))
                pe.wait_ge(fin, i)
                pe.wait_ge(so_ev, 2 * i)
                pe.wait_ge(ld_sraw, 16 * i + 16)
                for q in range(4):
                    m = nc.tensor.transpose(W[0][:, q * P:(q + 1) * P], sraw[:, 2 * q:2 * q + 2, :], ident[:, :])
                m.then_inc(t_s0, 1)
                pe.wait_ge(ld_lora, 64 * i + 64)
                nc.tensor.matmul(W[1][:, 0:T], w2a2[:, 0, :], lwa[:, :], start=True, stop=True).then_inc(l_q, 1)
                nc.tensor.matmul(W[2][:, 0:T], w2a2[:, 1, :], lwa[:, :], start=True, stop=True).then_inc(l_a, 1)
                nc.tensor.matmul(W[3][:, 0:T], g2a[:, :], lg1[:, :], start=True, stop=False)
                nc.tensor.matmul(W[3][:, 0:T], g2b[:, :], lg2[:, :], start=False, stop=True).then_inc(l_g, 1)
                fill(0, 0, KT)
                pe.wait_ge(sq_ok, i + 1)
                pe.wait_ge(s0_ev, i + 1)
                nc.tensor.matmul(W[0][:, 0:T], onesb[:, :], tb[:, :], start=True, stop=True).then_inc(t_ss, 1)
                fill(1, 0, 8)
                pe.wait_ge(rk_ok, i + 1)
                pe.wait_ge(lev, 3 * i + 3)
                nc.tensor.matmul(W[1][:, 0:T], onesb[:, :], rk[:, :], start=True, stop=True).then_inc(t_bs, 1)
                ada(i, 0, 0)
                pe.wait_ge(bk_ok, i + 1)
                pe.wait_ge(ss_ev, i + 1)
                for c in range(NCH):
                    dst = W[2][:, c * P:(c + 1) * P] if c < 4 else W[3][:, 0:P]
                    nc.tensor.transpose(dst, bk[:, c].rearrange("p x t -> p (x t)"), ident[:, :])
                for c in range(NCH):
                    dst = W[0][:, c * P:(c + 1) * P] if c < 4 else W[3][:, P:2 * P]
                    m = nc.tensor.transpose(dst, vp[:, c * C:c * C + P], ident[:, :])
                m.then_inc(t_tok, 1)
                ada(i, 0, 1)
                pe.wait_ge(tok_ev, i + 1)
                pe.wait_ge(ra_ok, i + 1)
                pe.wait_ge(bs_ev, i + 1)
                for c in range(NCH):
                    m = nc.tensor.matmul(W[c // 2][:, (c % 2) * 256:(c % 2) * 256 + 256],
                                         bk[:, c].rearrange("p x t -> p (x t)"),
                                         ra[:, c].rearrange("p h x t -> p (h x t)"), start=True, stop=True)
                m.then_inc(t_mm, 1)
                fill(1, 8, 12)
                turn(i, 0)
                pe.wait_ge(mm_ev, i + 1)
                pe.wait_ge(rst, i + 1)
                for h in range(2):
                    for c in range(NCH):
                        m = nc.tensor.matmul(W[3 * h][0:C, c * C:(c + 1) * C], mm[:, c, h, 1, :], inv[:, h, c, :],
                                             start=(c == 0), stop=(c == NCH - 1), skip_group_check=True)
                    m.then_inc(t_z, 1)
                nlev = 1
                for n, size in enumerate(LEVELS):
                    zb = lvl_bank[(n + 1) % 2]
                    for h in range(2):
                        pe.wait_ge(inv_ok, 12 * i + 2 * n + h + 1)
                        for c in range(NCH):
                            m = nc.tensor.matmul(W[zb[h]][0:C, c * C:(c + 1) * C], mm[:, c, h, 1, :], inv[:, h, c, :],
                                                 start=(c == 0), stop=(c == NCH - 1), skip_group_check=True)
                        m.then_inc(t_z, 1)
                    if n in (0, 2):
                        ada(i, 1, n // 2)
                    else:
                        fill(1, 12, 14) if n == 1 else fill(1, 14, 16)
                    for h in range(2):
                        pe.wait_ge(z_cp, 10 * i + 2 * n + h + 1)
                        if h == 0 and n == 0:
                            pe.wait_ge(inv_ok, 12 * i + 2)
                        for a_, b_, bank in ((invt, zs, zb[2 + 2 * h]), (zs, invt, zb[3 + 2 * h])):
                            for c in range(NCH):
                                m = nc.tensor.matmul(W[bank][0:C, c * C:(c + 1) * C], a_[:, h, c, :], b_[:, h, c, :],
                                                     start=(c == 0), stop=(c == NCH - 1), skip_group_check=True)
                        m.then_inc(t_e, 1)
                zb = lvl_bank[1]
                for h in range(2):
                    pe.wait_ge(inv_ok, 12 * i + 8 + h + 1)
                    for c in range(NCH):
                        m = nc.tensor.matmul(W[zb[h]][0:C, c * C:(c + 1) * C], mm[:, c, h, 1, :], inv[:, h, c, :],
                                             start=(c == 0), stop=(c == NCH - 1), skip_group_check=True)
                    m.then_inc(t_z, 1)
                turn(i, 1)
                for h in range(2):
                    pe.wait_ge(z_cp, 10 * i + 8 + h + 1)
                    for c in range(NCH):
                        m = nc.tensor.matmul(W[zb[2 + h]][0:C, c * C:(c + 1) * C], zs[:, h, c, :], invt[:, h, c, :],
                                             start=(c == 0), stop=(c == NCH - 1), skip_group_check=True)
                    m.then_inc(t_e, 1)
                pe.wait_ge(inv_ok, 12 * i + 12)
                for b in range(NB):
                    for h in range(2):
                        m = nc.tensor.matmul(
                            W[0][C * h:C * h + C, 0:P].rearrange("p (x t) -> p x t", x=2)[:, :, 8 * b:8 * b + 8],
                            s0t[:, b, :], ra[:, 4, h, :, 8 * b:8 * b + 8],
                            start=(b == 0), stop=(b == NB - 1), skip_group_check=True)
                m.then_inc(t_sg, 1)
                for c in range(NCH):
                    if c >= 1:
                        pe.wait_ge(g_ev, NCH * i + c)
                    if 1 <= c <= 3:
                        pe.wait_ge(st_ok, 4 * i + c)
                    if c == 0:
                        pe.wait_ge(sg_ev, i + 1)
                    if c >= 1:
                        pe.wait_ge(y_ev, NCH * i + c)

                    def state_part(x_, bank, stop):
                        if c == 4:
                            nc.tensor.matmul(W[bank][0:C, 0:P], sgy[:, x_, :], ident[:, :], start=True, stop=False,
                                             skip_group_check=True)
                        elif c >= 1:
                            for h in range(2):
                                nc.tensor.matmul(W[bank][0:C, C * h:C * h + C], ra[:, c, h, x_, :], st[:, :],
                                                 start=(h == 0), stop=False, skip_group_check=True)

                    state_part(1, 0, False)
                    for h in range(2):
                        m = nc.tensor.matmul(W[0][0:C, C * h:C * h + C], mm[:, c, h, 1, :], uv[:, c, C * h:C * h + C],
                                             start=(c == 0 and h == 0), stop=(h == 1), skip_group_check=True)
                    m.then_inc(t_g, 1)
                    state_part(0, 3, False)
                    fill(2, 3 * c, 3 * c + 2)
                    pe.wait_ge(g_ev, NCH * i + c + 1)
                    if c >= 1:
                        pe.wait_ge(u_ev, NCH * i + c)
                    for h in range(2):
                        m = nc.tensor.matmul(W[1][0:C, C * h:C * h + C], invt[:, h, c, :], gs_[:, C * h:C * h + C],
                                             start=(h == 0), stop=(h == 1), skip_group_check=True)
                    m.then_inc(t_u, 1)
                    fill(2, 3 * c + 2, 3 * c + 3)
                    pe.wait_ge(u_ev, NCH * i + c + 1)
                    if c < 4:
                        for h in range(2):
                            m = nc.tensor.matmul(W[2][C * h:C * h + C, 0:C], bkt[:, c, C * h:C * h + C],
                                                 uv[:, c, C * h:C * h + C], start=True, stop=True,
                                                 skip_group_check=True)
                        m.then_inc(t_st, 1)
                    for h in range(2):
                        m = nc.tensor.matmul(W[3][0:C, C * h:C * h + C], mm[:, c, h, 0, :], uv[:, c, C * h:C * h + C],
                                             start=(c == 0 and h == 0), stop=(h == 1), skip_group_check=True)
                    m.then_inc(t_y, 1)
                fill(2, 15, 16)
                pe.wait_ge(uvx_ok, i + 1)
                for h in range(2):
                    m = nc.tensor.matmul(W[0][C * h:C * h + C, :], bkt[:, 4, C * h:C * h + C],
                                         uvx[:, h].rearrange("p b i -> p (b i)"), start=True, stop=True,
                                         skip_group_check=True)
                m.then_inc(t_sf, 1)
                pe.wait_ge(y_ev, NCH * i + NCH)
                pe.sem_inc(past_pe, 1)
                for c in range(NCH):
                    m = nc.tensor.transpose(W[3][:, c * C:(c + 1) * C], ys[:, c, :], ident[0:C, 0:C])
                m.then_inc(t_yt, 1)
                pe.wait_ge(st_ok, 4 * i + 4)
                pe.wait_ge(sf_ok, i + 1)
                pe.sem_inc(past_pe, 1)
                nc.tensor.transpose(W[2][0:C, 0:P], st[:, :], ident[:, :])
                for q in range(4):
                    m = nc.tensor.transpose(W[1][:, q * P:(q + 1) * P], sfin[:, 2 * q:2 * q + 2, :], ident[:, :])
                m.then_inc(t_so, 1)
                pe.wait_ge(yt_ev, i + 1)
                nc.tensor.matmul(W[0][:, 0:T], onesd[:, :], yw[:, :], start=True, stop=True).then_inc(t_mn, 1)
                pe.wait_ge(yc_ok, i + 1)
                nc.tensor.matmul(W[3][:, 0:T], onesd[:, :], tb[:, :], start=True, stop=True).then_inc(t_vr, 1)

            with pe.Fori(0, PAIRS - 1) as i:
                pair(i, False)
            pair(PAIRS - 1, True)
            pe.wait_ge(fin, PAIRS)
            for j in range(27):
                n = min(P, SH - j * P)
                m = nc.tensor.transpose(PS[0:NC9, j // 4, (j % 4) * P:(j % 4) * P + n], zlast[0:n, j, :],
                                        ident[0:n, 0:n])
            m.then_inc(t_sh, 1)

        @block.scalar
        def _(act):
            act.wait_ge(k_zero, 1)
            for q in range(8):
                act.wait_ge(wu[q % 3], q // 3 + 1)
                act.wait_ge(ext_used, q)
                nc.scalar.copy(ext_prompt(ext), PS[:, q % 4, 0:NP_TOK])
                nc.scalar.copy(ext_sample(ext, 0, BUF), spT[:, q, :].rearrange("p (b l) -> p b l", l=BUF))
                nc.scalar.copy(ext_sample(ext), PS[:, q % 4, NP_TOK:T].rearrange("p (b l) -> p b l", l=NL)
                               ).then_inc(ext_ok, 1)
                act.wait_ge(t_pt, q)
                nc.scalar.copy(plast[:, :], PS[:, q % 4, T - P:T]).then_inc(pool_in, 1)
                act.wait_ge(pool_in, q + 1)
                act.sem_inc(pre_ev, 1)
                if q == 4:
                    nc.scalar.copy(ptok[:, :], W[2]).then_inc(ptok_ev, 1)
                if q in (3, 5, 7):
                    mix_out(act, q // 2 - 1)
            act.wait_ge(t_pt, 8)
            act.wait_ge(ptok_ok, 1)
            nc.scalar.copy(ptok[:, :], W[2]).then_inc(ptok_ev, 1)
            mix_out(act, 3)
            act.wait_ge(lzs_ok, 1)
            nc.scalar.activation(lwa[0:64, :], lwa[0:64, :], ACT.Tanh)
            act.wait_ge(lzs_ok, 3)
            nc.scalar.activation(lg1[:, :], lg1[:, :], ACT.Sigmoid)
            nc.scalar.activation(lg2[0:32, :], lg2[0:32, :], ACT.Sigmoid).then_inc(lora_ok, 1)

            def pair(i, last):
                for j in range(3):
                    act.wait_ge(wu[j], UBASE[j] + 1 + i)
                nc.scalar.copy(z3[:, :, 1:1 + NP_TOK], PS[:, 0:3, 0:NP_TOK])
                for j in range(3):
                    m = nc.scalar.copy(z3[:, j, 1 + NP_TOK:ZW].rearrange("p (b l) -> p b l", l=ZS)[:, :, 1:ZS],
                                       PS[:, j, NP_TOK:T].rearrange("p (b l) -> p b l", l=NL))
                m.then_inc(z_ev, 1)
                act.wait_ge(pc_ok, i + 1)
                act.wait_ge(l_q, i + 1)
                nc.scalar.activation(sg[:, :], W[1][:, 0:T], ACT.Sigmoid, bias=pc[:, K_W0:K_W0 + 1]).then_inc(lev, 1)
                act.wait_ge(l_a, i + 1)
                nc.scalar.activation(aa[:, :], W[2][:, 0:T], ACT.Sigmoid, bias=pc[:, K_A0:K_A0 + 1]).then_inc(lev, 1)
                act.wait_ge(l_g, i + 1)
                nc.scalar.copy(gg[:, :], W[3][:, 0:T]).then_inc(lev, 1)
                act.wait_ge(t_s0, i + 1)
                w0 = W[0].rearrange("p (q h i) -> p q h i", q=4, h=2)
                s0 = s0t[:, :, :].rearrange("p (q b) i -> p q b i", b=2)
                for b in range(2):
                    for h in range(2):
                        m = nc.scalar.copy(s0[C * h:C * h + C, :, b, :], w0[C * b:C * b + C, :, h, :])
                m.then_inc(s0_ev, 1)
                act.wait_ge(cs_ok, i + 1)
                nc.scalar.activation(ilam[:, :], cs[:, :], ACT.Exp, scale=DECAY).then_inc(e_ok, 1)
                nc.scalar.activation(lam[:, :], cs[:, :], ACT.Exp, scale=-DECAY).then_inc(e_ok, 1)
                act.wait_ge(cse_ok, i + 1)
                nc.scalar.activation(lame[:, :], cse[:, :], ACT.Exp, scale=-DECAY).then_inc(e_ok, 1)
                act.wait_ge(t_ss, i + 1)
                nc.scalar.activation(rn[:, :], W[0][:, 0:T], ACT.Sqrt).then_inc(ss_ev, 1)
                act.wait_ge(t_tok, i + 1)
                nc.scalar.copy(bkt[:, 0:4, :].rearrange("p c j -> p (c j)"), W[2])
                nc.scalar.copy(bkt[:, 4, :], W[3][:, 0:P])
                nc.scalar.copy(uv[C:P, 0:4, :].rearrange("p c j -> p (c j)"), W[0][C:P, :])
                nc.scalar.copy(uv[C:P, 4, :], W[3][C:P, P:2 * P]).then_inc(tok_ev, 1)

                def z_copy(n, h, bank):
                    act.wait_ge(t_z, 12 * i + 2 + 2 * n + h + 1)
                    nc.scalar.copy(zs[0:C, h].rearrange("p c t -> p (c t)"), W[bank][0:C, 0:T]).then_inc(z_cp, 1)

                def a_copy(ch):
                    act.wait_ge(a_half, 4 * i + 2 * ch + 2)
                    if ch == 0:
                        act.wait_ge(a_turn, 2 * i)
                    else:
                        act.wait_ge(a_turn, 2 * i + 1)
                    nc.scalar.copy(asum[:, :], PS[:, 3, :]).then_inc(a_cp, 1)

                a_copy(0)
                for n in range(5):
                    if n >= 1:
                        act.wait_ge(t_e, 10 * i + 2 * n)
                    for h in range(2):
                        z_copy(n, h, lvl_bank[(n + 1) % 2][h])
                    if n == 3:
                        a_copy(1)
                act.wait_ge(t_sg, i + 1)
                nc.scalar.copy(sgy[:, :, :].rearrange("p x t -> p (x t)"), W[0][:, 0:P]).then_inc(sg_ev, 1)
                for c in range(NCH):
                    act.wait_ge(t_g, NCH * i + c + 1)
                    nc.scalar.copy(gs_[0:C, :], W[0][0:C, 0:P]).then_inc(g_ev, 1)
                    act.wait_ge(t_y, NCH * i + c + 1)
                    if c == 0:
                        act.wait_ge(t_yt, i)
                    nc.scalar.copy(ys[:, c, :], W[3][0:C, 0:P]).then_inc(y_ev, 1)
                act.wait_ge(t_yt, i + 1)
                nc.scalar.copy(yw[:, :], W[3][:, 0:T]).then_inc(yt_ev, 1)
                act.wait_ge(t_so, i + 1)
                act.wait_ge(out_w, 80 * i)
                nc.scalar.copy(pout[:, :], W[2][0:C, 0:P]).then_inc(so_ev, 1)
                nc.scalar.copy(sout[:, :, :].rearrange("p b j -> p (b j)"), W[1]).then_inc(so_ev, 1)
                act.wait_ge(t_vr, i + 1)
                nc.scalar.activation(rn[:, :], W[3][:, 0:T], ACT.Sqrt, bias=eps[:, 1:2]).then_inc(vr_ev, 1)

            with act.Fori(0, PAIRS - 1) as i:
                pair(i, False)
            pair(PAIRS - 1, True)
            act.wait_ge(t_sh, 1)
            nc.scalar.copy(shrow[:, 0:27 * P], PS[0:NC9, 0:7, :].rearrange("p b n -> p (b n)")[:, 0:27 * P]
                           ).then_inc(sh_ev, 1)

        @block.vector
        def _(ve):
            o = Order(ve, v_own)
            masks(ve, o)
            for q in range(8):
                g, w = q // 2, WIN[q // 2]
                ve.wait_ge(ext_ok, q + 1)
                src = ext
                for n in range(g + 1):
                    dst, lo, d = (sa, sb_)[n % 2], 2 ** (n + 1) - 1, 2 ** n
                    o.did(nc.vector.tensor_tensor(dst[:, lo:EW], src[:, lo:EW], src[:, lo - d:EW - d], ALU.add))
                    o.settle()
                    src = dst
                if g >= 1:
                    ve.wait_ge(t_pool, g)
                o.did(nc.vector.tensor_tensor(pooled[:, q % 2, 0:NP_TOK], ext_prompt(src), rc[:, g, :], ALU.mult))
                o.settle()
                o.did(nc.vector.tensor_tensor(pooled[:, q % 2, 0:NP_TOK], pooled[:, q % 2, 0:NP_TOK], ext_prompt(ext),
                                              ALU.subtract))
                o.did(nc.vector.scalar_tensor_tensor(
                    out=pooled[:, q % 2, NP_TOK:T].rearrange("p (b l) -> p b l", l=NL), in0=ext_sample(src),
                    scalar=1.0 / w, in1=ext_sample(ext), op0=ALU.mult, op1=ALU.subtract))
                o.settle()
                ve.sem_inc(ext_used, 1)
                if q % 2:
                    ve.sem_inc(pooled_ok, 1)
            for r, (q, n, dst) in enumerate(((8, P, lwa), (9, P, lg1), (10, 32, lg2))):
                ve.wait_ge(wu[q % 3], q // 3 + 1)
                bank = PS[0:n, q % 4, :]
                cur = lz[0:n, 1 + NP_TOK:ZW].rearrange("p (b l) -> p b l", l=ZS)
                o.did(nc.vector.tensor_copy(lz[0:n, 1:1 + NP_TOK], bank[:, 0:NP_TOK]))
                o.did(nc.vector.tensor_copy(cur[:, :, 1:ZS], bank[:, NP_TOK:T].rearrange("p (b l) -> p b l", l=NL)))
                o.did(nc.vector.tensor_copy(cur[:, :, 0], sprevT[0:n, 24 + r, :]))
                o.did(nc.vector.tensor_copy(zlast[0:n, 24 + r, :], bank[:, NP_TOK - 1:T:NL]))
                o.settle()
                o.did(nc.vector.tensor_tensor(lzd[0:n, 0:NP_TOK], lz[0:n, 0:NP_TOK], lz[0:n, 1:1 + NP_TOK], ALU.subtract))
                o.did(nc.vector.tensor_tensor(lzd[0:n, NP_TOK:T].rearrange("p (b l) -> p b l", l=NL),
                                              cur[:, :, 0:NL], cur[:, :, 1:ZS], ALU.subtract))
                o.settle()
                o.did(nc.vector.scalar_tensor_tensor(out=dst[0:n, :], in0=lzd[0:n, :],
                                                     scalar=PT[0:n, R_MUT + r:R_MUT + r + 1], in1=bank[:, 0:T],
                                                     op0=ALU.mult, op1=ALU.add))
                o.settle()
                ve.sem_inc(pre_ev, 1)
                ve.sem_inc(lzs_ok, 1)
            base = o.n

            def pair(i, last):
                o = Order(ve, v_own, base + i * N_DVE)
                col = (lambda x_: x_[:, :, PAIRS - 1:PAIRS]) if last is True else (lambda x_: x_[:, :, bass.ds(i, 1)])
                o.did(nc.vector.tensor_copy(pc[:, :].unsqueeze(2), col(PT[:, 0:80].rearrange("p (k q) -> p k q", q=8))))
                for j in range(3):
                    ve.wait_ge(wu[j], UBASE[j] + 1 + i)
                    zc = z3[:, j, 1 + NP_TOK:ZW].rearrange("p (b l) -> p b l", l=ZS)
                    n_ = slice(8 * j + PAIRS - 1, 8 * j + PAIRS) if last is True else bass.ds(i + 8 * j, 1)
                    o.did(nc.vector.tensor_copy(zc[:, :, 0].unsqueeze(1), sprevT[:, n_, :]))
                o.settle()
                nc.vector.tensor_scalar(pomk[:, :], pc[:, K_KA:K_KA + 1], -1.0, 1.0, ALU.mult, ALU.add).then_inc(pc_ok, 1)
                ve.wait_ge(z_ev, i + 1)
                for j in range(3):
                    n_ = slice(8 * j + PAIRS - 1, 8 * j + PAIRS) if last is True else bass.ds(i + 8 * j, 1)
                    o.did(nc.vector.tensor_copy(zlast[:, n_, :], z3[:, j, NP_TOK:ZW:ZS].unsqueeze(1)))
                o.did(nc.vector.tensor_tensor(zd[:, :, 0:NP_TOK], z3[:, :, 0:NP_TOK], z3[:, :, 1:1 + NP_TOK], ALU.subtract))
                zc = z3[:, :, 1 + NP_TOK:ZW].rearrange("p j (b l) -> p j b l", l=ZS)
                o.did(nc.vector.tensor_tensor(zd[:, :, NP_TOK:T].rearrange("p j (b l) -> p j b l", l=NL),
                                              zc[:, :, :, 0:NL], zc[:, :, :, 1:ZS], ALU.subtract))
                o.settle()
                for j, dst in enumerate((zr[:, :], zk[:, :], vp[:, C:C + T])):
                    o.did(nc.vector.scalar_tensor_tensor(out=dst, in0=zd[:, j, :], scalar=pc[:, K_MU + j:K_MU + j + 1],
                                                         in1=PS[:, j, 0:T], op0=ALU.mult, op1=ALU.add))
                o.settle()
                ve.sem_inc(z_done, 1)
                o.did(nc.vector.tensor_scalar(kk[:, :], zk[:, :], pc[:, K_KK:K_KK + 1], None, ALU.mult))
                o.settle()
                nc.vector.tensor_tensor(tb[:, :], kk[:, :], kk[:, :], ALU.mult).then_inc(sq_ok, 1)
                ve.wait_ge(lev, 3 * i + 1)
                nc.vector.tensor_tensor_scan(cs[:, :], rmask[:, :], sg[:, :], 0.0, ALU.mult, ALU.add).then_inc(cs_ok, 1)
                ve.wait_ge(k2_ok, i + 1)
                nc.vector.scalar_tensor_tensor(out=rk[:, :], in0=zr[:, :], scalar=pc[:, K_RK:K_RK + 1], in1=k2[:, :],
                                               op0=ALU.mult, op1=ALU.mult).then_inc(rk_ok, 1)
                ve.wait_ge(ss_ev, i + 1)
                o.did(nc.vector.tensor_scalar(rn[:, :], rn[:, :], 1e-12, None, ALU.max))
                o.settle()
                o.did(nc.vector.reciprocal(rn[:, :], rn[:, :]))
                o.settle()
                o.did(nc.vector.tensor_tensor(kk[:, :], kk[:, :], rn[:, :], ALU.mult))
                o.settle()
                o.did(nc.vector.tensor_tensor(tb[:, :], kk[:, :], aa[:, :], ALU.mult))
                o.settle()
                ve.wait_ge(e_ok, 3 * i + 3)
                cut = lambda x_: x_.rearrange("p (c t) -> p c t", t=C)
                o.did(nc.vector.tensor_tensor(bk[:, :, 0, :], cut(tb[:, :]), cut(ilam[:, :]), ALU.mult))
                nc.vector.tensor_tensor(bk[:, :, 1, :], cut(k2[:, :]), cut(ilam[:, :]), ALU.mult).then_inc(bk_ok, 1)
                for h in range(2):
                    r_ = slice(C * h, C * h + C)
                    o.did(nc.vector.tensor_tensor(ra[r_, :, h, 0, :], cut(zr[r_, :]), cut(lam[r_, :]), ALU.mult))
                    m = nc.vector.scalar_tensor_tensor(out=ra[r_, :, h, 1, :], in0=cut(kk[r_, :]), scalar=-1.0,
                                                       in1=cut(lame[r_, :]), op0=ALU.mult, op1=ALU.mult)
                    if h == 0:
                        o.did(m)
                m.then_inc(ra_ok, 1)
                ve.wait_ge(t_bs, i + 1)
                nc.vector.tensor_tensor(bv[:, :], W[1][:, 0:T], vp[:, C:C + T], ALU.mult).then_inc(bs_ev, 1)
                ve.wait_ge(t_mm, i + 1)
                for b, mask, n in ((0, mask_p, 2), (1, mask_p, 2), (2, mask_s, 1)):
                    o.did(nc.vector.tensor_tensor(
                        mm[:, 2 * b:2 * b + n].rearrange("p c h x t -> p (c h) (x t)"),
                        W[b][:, 0:256 * n].rearrange("p (g n) -> p g n", n=P),
                        mask[:, :].unsqueeze(1).broadcast_to([P, 2 * n, P]), ALU.mult))
                o.settle()
                ve.sem_inc(mm_ev, 1)
                ve.wait_ge(rst, i + 1)

                def put(dst, mask, src):
                    nc_ = mask.unsqueeze(1).broadcast_to([C, NCH, C])
                    return o.did(nc.vector.copy_predicated(dst, nc_, src))

                for h in range(2):
                    ve.wait_ge(t_z, 12 * i + h + 1)
                    ve.sem_inc(past_ve, 1)
                    put(inv[0:C, h], lvl_n[:, 0, :], cut(W[3 * h][0:C, 0:T]))
                    put(invt[0:C, h], lvl_t[:, 0, :], mm[0:C, :, h, 1, :])
                    o.settle()
                    ve.sem_inc(inv_ok, 1)
                ada_store(i, 0, o, last)
                for n in range(4):
                    zb = lvl_bank[(n + 1) % 2]
                    for h in range(2):
                        ve.wait_ge(t_e, 10 * i + 2 * n + h + 1)
                        ve.sem_inc(past_ve, 1)
                        put(inv[0:C, h], lvl_n[:, n + 1, :], cut(W[zb[2 + 2 * h]][0:C, 0:T]))
                        put(invt[0:C, h], lvl_t[:, n + 1, :], cut(W[zb[3 + 2 * h]][0:C, 0:T]))
                        o.settle()
                        ve.sem_inc(inv_ok, 1)
                for h in range(2):
                    ve.wait_ge(t_e, 10 * i + 8 + h + 1)
                    ve.sem_inc(past_ve, 1)
                    put(invt[0:C, h], lvl_t[:, 5, :], cut(W[lvl_bank[1][2 + h]][0:C, 0:T]))
                    o.settle()
                    ve.sem_inc(inv_ok, 1)
                ada_store(i, 1, o, last)
                for c in range(NCH):
                    ve.wait_ge(t_u, NCH * i + c + 1)
                    nc.vector.tensor_copy(uv[0:C, c, :], W[1][0:C, 0:P]).then_inc(u_ev, 1)
                    if c < 4:
                        ve.wait_ge(t_st, 4 * i + c + 1)
                        end = lam[:, C * c + C - 1:C * c + C]
                        if c == 0:
                            nc.vector.tensor_scalar(st[:, :], W[2][:, 0:C], end, None, ALU.mult).then_inc(st_ok, 1)
                        else:
                            nc.vector.scalar_tensor_tensor(out=st[:, :], in0=W[2][:, 0:C], scalar=end, in1=stl[:, :],
                                                           op0=ALU.mult, op1=ALU.add).then_inc(st_ok, 1)
                        if c < 3:
                            ve.wait_ge(st_ok, 4 * i + c + 1)
                            o.did(nc.vector.tensor_scalar(stl[:, :], st[:, :], lam[:, C * c + 2 * C - 1:C * c + 2 * C],
                                                          None, ALU.mult))
                            o.settle()
                ve.wait_ge(t_sf, i + 1)
                ve.wait_ge(so_ev, 2 * i)
                o.did(nc.vector.tensor_tensor(sfin[:, :, :], W[0].rearrange("p (b j) -> p b j", j=C), s0t[:, :, :], ALU.add))
                o.settle()
                nc.vector.tensor_tensor(sfin[:, :, :], sfin[:, :, :],
                                        lam[:, NP_TOK + NL - 1:T:NL].unsqueeze(2).broadcast_to([P, NB, C]), ALU.mult
                                        ).then_inc(sf_ok, 1)
                ve.wait_ge(t_mn, i + 1)
                o.did(nc.vector.tensor_tensor(yw[:, :], yw[:, :], W[0][:, 0:T], ALU.subtract))
                o.settle()
                nc.vector.tensor_tensor(tb[:, :], yw[:, :], yw[:, :], ALU.mult).then_inc(yc_ok, 1)
                ve.wait_ge(vr_ev, i + 1)
                o.did(nc.vector.reciprocal(rn[:, :], rn[:, :]))
                o.settle()
                o.did(nc.vector.tensor_tensor(yw[:, :], yw[:, :], rn[:, :], ALU.mult))
                o.settle()
                o.did(nc.vector.tensor_scalar(yw[:, :], yw[:, :], pc[:, K_LW:K_LW + 1], pc[:, K_LB:K_LB + 1],
                                              ALU.mult, ALU.add))
                o.settle()
                o.did(nc.vector.tensor_tensor(yw[:, :], yw[:, :], bv[:, :], ALU.add))
                o.settle()
                dst = catT[:, 8 + PAIRS - 1:8 + PAIRS, :] if last is True else catT[:, bass.ds(i + 8, 1), :]
                nc.vector.tensor_tensor(dst, yw[:, :].unsqueeze(1), gg[:, :].unsqueeze(1), ALU.mult).then_inc(fin, 1)
                assert o.n == N_DVE, o.n

            def ada_store(i, ch, o, last):
                ve.wait_ge(a_turn, 2 * i + ch + 1)
                o.did(nc.vector.tensor_reduce(a4[:, :, :], ada_parts(PS[:, 3, :]), AX.X, ALU.add))
                o.settle()
                ve.sem_inc(a_red, 1)
                at0 = 32 + 4 * (2 * i + ch)
                rows = slice(at0, at0 + 4) if last is True else bass.ds(at0, 4)
                o.did(nc.vector.tensor_tensor(adaT[:, rows, :], a4[:, :, :],
                                              bT[:, rows].unsqueeze(2).broadcast_to([P, 4, NC9]), ALU.add))

            with ve.Fori(0, PAIRS - 1) as i:
                pair(i, False)
            pair(PAIRS - 1, True)



def phase_mix(nc, A, O, sb, sem, G):
    PS, ident, eps, PT, adaT, catT = (G[k] for k in "PS ident eps PT adaT catT".split())
    ybuf, past_pe = G["ybuf"], G["past_pe"]
    x2 = sb("x2", [P, 3, D])
    h2 = sb("h2", [P, 3, D])
    chosen, scores, sel, wts, dest = (sb(n, [P, 3, NE]) for n in "chosen scores sel wts dest".split())
    r4 = sb("r4", [P, 8, 12])
    rank = sb("rank", [P, 12, EPG])
    cmp_ = sb("cmp", [P, 12, EPG])
    small = sb("small", [P, 16, 3])
    nb = sb("nb", [P, 4, NE])
    d01 = sb("d01", [P, 2, 3])
    w01 = sb("w01", [P, 2, 3])
    d01i = sb("d01i", [P, 6], U32)
    browt = sb("browt", [P, NE])
    be = sb("be", [1, 32, NE])
    bef = sb("bef", [1, 32])
    bei = sb("bei", [1, 64], I32)
    bnum = sb("bnum", [1, 32])
    bnum_i = sb("bnum_i", [1, 32], I32)
    slotf = sb("slotf", [P, SLOT])
    slot_i = sb("slot_i", [P, SLOT], I32)
    tri = sb("tri", [P, P])
    ones = sb("ones", [P, P])
    pick = sb("pick", [P, 3, SLOT])
    pick2 = sb("pick2", [P, 3, SLOT])
    ssq = sb("ssq", [P, 8])
    (s_x, s_br, s_rt, o_own, p_own, t_mix, gated, t_back, x2_ok, ss_ok, sd_ok, xn_ok, t_h, h_ev, hm_ok, t_lg, sc_ok,
     t_hb, hb_ev, ch_ok, t_pos, be_ok, k_own, a_own, s_fg, s_fin, y_out, y_in) = (
        sem("m_" + n) for n in ("s_x s_br s_rt o_own p_own t_mix gated t_back x2_ok ss_ok sd_ok xn_ok t_h h_ev hm_ok "
                                "t_lg sc_ok t_hb hb_ev ch_ok t_pos be_ok k_own a_own s_fg s_fin y_out y_in").split())
    (pick_ok, t_pk, xs_ev, t_xt, xt_ev, t_gu, act_ev, up_ev, gu_ok, t_at, at_ev, t_dn, dn_ev, y_st, t_gt, gt_ev, t_gm,
     gm_ev) = (
        sem("e_" + n) for n in ("pick_ok t_pk xs_ev t_xt xt_ev t_gu act_ev up_ev gu_ok t_at at_ev t_dn dn_ev y_st "
                                "t_gt gt_ev t_gm gm_ev").split())
    s_wo = [sem(f"s_wo{j}") for j in range(4)]
    u_wo = sem("u_wo")
    ld_e = [sem(f"ld_e{j}") for j in range(6)]
    used = [sem(f"used{j}") for j in range(6)]
    w_out = A["w_out"][0].rearrange("(k p) n -> p k n", p=P)
    w_gate = A["w_gate"][0].rearrange("e (q k p) n -> e q p k n", q=4, p=P)
    w_up = A["w_up"][0].rearrange("e (q k p) n -> e q p k n", q=4, p=P)
    w_down = A["w_down"][0].rearrange("e (q k p) n -> e q p k n", q=4, p=P)

    mixing = ExitStack()
    G["ctx"].enter_context(mixing)
    mg = sb("mg", [P, KT, T], scope=mixing)
    wo = sb("wo", [P, 4, KT, P], scope=mixing)
    gs2 = sb("gs2", [P, KT, NC9], scope=mixing)
    wrt = sb("wrt", [P, KT, NE], scope=mixing)
    junk2 = sb("junk2", [P, D], scope=mixing)
    with nc.Block() as block:
        gated_tile = junk2[:, 0:4 * T].rearrange("p (j t) -> p j t", j=4)

        @block.sync
        def _(sp):
            for j in range(4):
                sp.dma_start(wo[:, j], w_out[:, :, j * P:(j + 1) * P]).then_inc(s_wo[j], 16)
            for i, (t0, n) in enumerate(TILES):
                src = A["x_prompt"][0, t0:t0 + n] if i < 2 else A["x_sample"].rearrange("b l d -> (b l) d")
                sp.dma_start(x2[0:n, i, :], src).then_inc(s_x, 16)
            sp.dma_start(wrt[:, :, :], A["w_router"].rearrange("(k p) e -> p k e", p=P)).then_inc(s_rt, 16)
            sp.dma_start(browt[:, :], A["b_router"].partition_broadcast(P)).then_inc(s_br, 16)
            with sp.Fori(1, 4) as g:
                for j in range(4):
                    sp.wait_ge(u_wo, 4 * g - 3 + j)
                    sp.dma_start(wo[:, j], w_out[:, :, bass.ds(g * 512 + j * P, P)]).then_inc(s_wo[j], 16)

        @block.gpsimd
        def _(pool):
            n_ = [0]

            def own(ins):
                n_[0] += 1
                ins.then_inc(k_own, 1)
                pool.wait_ge(k_own, n_[0])

            own(nc.gpsimd.memset(ones[:, :], 1.0))
            own(nc.gpsimd.affine_select(out=tri[:, :], in_=ones[:, :], compare_op=ALU.is_gt, fill=0.0, base=0,
                                        pattern=[[1, P]], channel_multiplier=-1))
            own(nc.gpsimd.iota(slot_i[:, :], pattern=[[1, SLOT]], base=0, channel_multiplier=0))
            own(nc.gpsimd.iota(bnum_i[:, :], pattern=[[1, 32]], base=0, channel_multiplier=0))
            own(nc.gpsimd.tensor_copy(slotf[:, :], slot_i[:, :]))
            own(nc.gpsimd.tensor_copy(bnum[:, :], bnum_i[:, :]))
            own(nc.gpsimd.memset(scores[:, :, :], 0.0))
            own(nc.gpsimd.memset(h2[:, 2, :], 0.0))
            pool.sem_inc(p_own, 1)

        @block.tensor
        def _(pe):
            with pe.Fori(0, 4) as g:
                for j in range(4):
                    pe.wait_ge(s_wo[j], 16 * g + 16)
                    for k in range(KT):
                        m = nc.tensor.matmul(PS[:, j, 0:T], wo[:, j, k, :], catT[:, k, :], start=(k == 0),
                                             stop=(k == KT - 1))
                    m.then_inc(u_wo, 1)
                pe.wait_ge(gated, g + 1)
                pe.wait_ge(x2_ok, g)
                for j in range(4):
                    for i, (t0, n) in enumerate(TILES):
                        m = nc.tensor.transpose(PS[0:n, 4 + i, j * P:(j + 1) * P], gated_tile[:, j, t0:t0 + n],
                                                ident[:, :])
                m.then_inc(t_back, 1)
            pe.wait_ge(xn_ok, 3)
            for k in range(KT):
                if k >= 8:
                    pe.wait_ge(h_ev, k - 7)
                for i, (t0, n) in enumerate(TILES):
                    m = nc.tensor.transpose(PS[:, k % 8, t0:t0 + n], h2[0:n, i, k * P:(k + 1) * P], ident[0:n, 0:n])
                m.then_inc(t_h, 1)
            pe.wait_ge(hm_ok, 1)
            pe.wait_ge(s_rt, 16)
            for i, (t0, n) in enumerate(TILES):
                for k in range(KT):
                    m = nc.tensor.matmul(PS[0:n, 0, i * NE:(i + 1) * NE], mg[:, k, t0:t0 + n], wrt[:, k, :],
                                         start=(k == 0), stop=(k == KT - 1))
            m.then_inc(t_lg, 1)
            for q in range(12):
                i, (t0, n), c = q % 3, TILES[q % 3], q // 3
                if q >= 6:
                    pe.wait_ge(hb_ev, q - 5)
                for j in range(4):
                    m = nc.tensor.transpose(PS[0:n, 1 + q % 6, j * P:(j + 1) * P], mg[:, 4 * c + j, t0:t0 + n],
                                            ident[:, :])
                m.then_inc(t_hb, 1)
            pe.wait_ge(ch_ok, 1)
            for i in range(3):
                for i2 in range(i + 1):
                    nc.tensor.matmul(PS[:, 7, i * NE:(i + 1) * NE], tri[:, :] if i2 == i else ones[:, :],
                                     chosen[:, i2, :], start=(i2 == 0), stop=(i2 == i))
            for i in range(3):
                m = nc.tensor.matmul(PS[:, 7, 48:64], ones[:, :], chosen[:, i, :], start=(i == 0), stop=(i == 2))
            m.then_inc(t_pos, 1)

        @block.scalar
        def _(act):
            act.wait_ge(x2_ok, 4)
            for i, (t0, n) in enumerate(TILES):
                nc.scalar.activation(junk2[0:n, :], x2[0:n, i, :], ACT.Square, accum_out=ssq[0:n, i:i + 1]
                                     ).then_inc(ss_ok, 1)
                act.wait_ge(ss_ok, i + 1)
            for i, (t0, n) in enumerate(TILES):
                nc.scalar.activation(ssq[0:n, 4 + i:5 + i], ssq[0:n, i:i + 1], ACT.Sqrt, bias=eps[0:n, 0:1],
                                     scale=1.0 / D).then_inc(sd_ok, 1)
            for k in range(KT):
                act.wait_ge(t_h, k + 1)
                nc.scalar.copy(mg[:, k, :], PS[:, k % 8, 0:T]).then_inc(h_ev, 1)
            act.wait_ge(t_lg, 1)
            act.wait_ge(p_own, 1)
            for i, (t0, n) in enumerate(TILES):
                m = nc.scalar.activation(scores[0:n, i, :], PS[0:n, 0, i * NE:(i + 1) * NE], ACT.Sigmoid)
            m.then_inc(sc_ok, 1)
            for q in range(12):
                i, (t0, n), c = q % 3, TILES[q % 3], q // 3
                act.wait_ge(t_hb, q + 1)
                nc.scalar.copy(h2[0:n, i, 512 * c:512 * c + 512], PS[0:n, 1 + q % 6, :]).then_inc(hb_ev, 1)

        @block.vector
        def _(ve):
            o = Order(ve, o_own)
            tt, ts = nc.vector.tensor_tensor, nc.vector.tensor_scalar

            def step(ins):
                o.did(ins)
                o.settle()

            ve.wait_ge(s_x, 48)
            with ve.Fori(0, 4) as g:
                for j in range(4):
                    ve.wait_ge(u_wo, 4 * g + j + 1)
                    if j == 0:
                        ve.wait_ge(t_back, g)
                    nc.vector.tensor_scalar(gated_tile[:, j, 0:NP_TOK], PS[:, j, 0:NP_TOK],
                                            adaT[:, bass.ds(GT_A + 4 * g + j, 1), 0:1].rearrange("p a b -> p (a b)"),
                                            None, ALU.mult)
                    m = nc.vector.tensor_tensor(
                        gated_tile[:, j, NP_TOK:T].rearrange("p (b l) -> p b l", l=NL),
                        PS[:, j, NP_TOK:T].rearrange("p (b l) -> p b l", l=NL),
                        adaT[:, bass.ds(GT_A + 4 * g + j, 1), 1:NC9].rearrange("p a b -> p (a b)").unsqueeze(2)
                        .broadcast_to([P, NB, NL]), ALU.mult)
                m.then_inc(gated, 1)
                ve.wait_ge(t_back, g + 1)
                for i, (t0, n) in enumerate(TILES):
                    xs = x2[0:n, i, bass.ds(g * 512, 512)]
                    m = nc.vector.tensor_tensor(xs, xs, PS[0:n, 4 + i, :], ALU.add)
                m.then_inc(x2_ok, 1)
            ve.wait_ge(p_own, 1)
            for i, (t0, n) in enumerate(TILES):
                ve.wait_ge(sd_ok, i + 1)
                step(nc.vector.reciprocal(ssq[0:n, 4 + i:5 + i], ssq[0:n, 4 + i:5 + i]))
                ts(h2[0:n, i, :], x2[0:n, i, :], ssq[0:n, 4 + i:5 + i], None, ALU.mult).then_inc(xn_ok, 1)
            step(ts(gs2[:, :, :], adaT[:, SC_M:SC_M + KT, :], 1.0, None, ALU.add))
            step(tt(gs2[:, :, :], gs2[:, :, :], PT[:, R_G2:R_G2 + KT].unsqueeze(2).broadcast_to([P, KT, NC9]), ALU.mult))
            ve.wait_ge(h_ev, KT)
            modulate(nc, ve, o, mg, gs2, adaT[:, SH_M:SH_M + KT, :])
            ve.sem_inc(hm_ok, 1)
            ve.wait_ge(sc_ok, 1)
            ve.wait_ge(s_br, 16)
            step(tt(sel[:, :, :], scores[:, :, :], browt[:, :].unsqueeze(1).broadcast_to([P, 3, NE]), ALU.add))
            s4 = sel[:, :, :].rearrange("p i (g e) -> p (i g) e", e=EPG)
            for n, (a, b, op) in enumerate(((0, 1, ALU.max), (0, 1, ALU.min), (2, 3, ALU.max), (2, 3, ALU.min))):
                step(tt(r4[:, n, :], s4[:, :, a], s4[:, :, b], op))
            step(tt(r4[:, 4, :], r4[:, 0, :], r4[:, 2, :], ALU.max))
            step(tt(r4[:, 5, :], r4[:, 0, :], r4[:, 2, :], ALU.min))
            step(tt(r4[:, 6, :], r4[:, 1, :], r4[:, 3, :], ALU.max))
            step(tt(r4[:, 5, :], r4[:, 5, :], r4[:, 6, :], ALU.max))
            step(tt(r4[:, 4, :], r4[:, 4, :], r4[:, 5, :], ALU.add))
            gsc = r4[:, 4, :].rearrange("p (i g) -> p i g", g=NG)
            step(nc.vector.tensor_reduce(small[:, 0, :], gsc, AX.X, ALU.max))
            eq = r4[:, 5, :].rearrange("p (i g) -> p i g", g=NG)
            step(tt(eq, gsc, small[:, 0, :].unsqueeze(2).broadcast_to([P, 3, NG]), ALU.is_equal))
            step(nc.vector.memset(small[:, 1, :], 1.0))
            for g in range(NG):
                step(tt(eq[:, :, g], eq[:, :, g], small[:, 1, :], ALU.mult))
                step(tt(small[:, 1, :], small[:, 1, :], eq[:, :, g], ALU.subtract))
            step(nc.vector.memset(rank[:, :, :], 0.0))
            for j in range(EPG):
                for lo, hi, op in ((0, j, ALU.is_gt), (j + 1, EPG, ALU.is_ge)):
                    if lo < hi:
                        step(tt(cmp_[:, :, lo:hi], s4[:, :, j:j + 1].broadcast_to([P, 12, hi - lo]), s4[:, :, lo:hi], op))
                        step(tt(rank[:, :, lo:hi], rank[:, :, lo:hi], cmp_[:, :, lo:hi], ALU.add))
            step(ts(rank[:, :, :], rank[:, :, :], 2.0, None, ALU.is_lt))
            c4 = chosen[:, :, :].rearrange("p i (g e) -> p (i g) e", e=EPG)
            step(tt(c4, rank[:, :, :], r4[:, 5, :].unsqueeze(2).broadcast_to([P, 12, EPG]), ALU.mult))
            step(nc.vector.memset(chosen[C:P, 2, :], 0.0))
            ve.sem_inc(ch_ok, 1)
            step(tt(wts[:, :, :], scores[:, :, :], chosen[:, :, :], ALU.mult))
            step(nc.vector.tensor_reduce(small[:, 2, :], wts[:, :, :], AX.X, ALU.add))
            step(ts(small[:, 2, :], small[:, 2, :], 1e-37, None, ALU.max))
            step(nc.vector.reciprocal(small[:, 2, :], small[:, 2, :]))
            step(tt(wts[:, :, :], wts[:, :, :], small[:, 2, :].unsqueeze(2).broadcast_to([P, 3, NE]), ALU.mult))
            ve.wait_ge(t_pos, 1)
            step(nc.vector.memset(nb[:, 0, :], 0.0))
            step(nc.vector.memset(nb[:, 3, :], 1.0))
            for k in range(T // SLOT):
                step(nc.vector.scalar_tensor_tensor(out=nb[:, 0, :], in0=PS[:, 7, 48:64], scalar=float(k * SLOT),
                                                    in1=nb[:, 0, :], op0=ALU.is_gt, op1=ALU.add))
            step(nc.vector.tensor_tensor_scan(nb[:, 1, :], nb[:, 3, :], nb[:, 0, :], 0.0, ALU.mult, ALU.add))
            step(tt(nb[:, 2, :], nb[:, 1, :], nb[:, 0, :], ALU.subtract))
            step(ts(nb[:, 2, :], nb[:, 2, :], float(SLOT), None, ALU.mult))
            step(tt(be[:, :, :], nb[0:1, 1, :].unsqueeze(1).broadcast_to([1, 32, NE]),
                    bnum[:, :].unsqueeze(2).broadcast_to([1, 32, NE]), ALU.is_le))
            step(nc.vector.tensor_reduce(bef[:, :], be[:, :, :], AX.X, ALU.add))
            step(ts(bef[:, :], bef[:, :], float(NE - 1), None, ALU.min))
            step(nc.vector.tensor_copy(bei[:, 0:32], bef[:, :]))
            step(nc.vector.tensor_copy(bei[:, 32:33], nb[0:1, 1, NE - 1:NE]))
            step(tt(dest[:, :, :], PS[:, 7, 0:48].rearrange("p (i e) -> p i e", e=NE),
                    nb[:, 2, :].unsqueeze(1).broadcast_to([P, 3, NE]), ALU.add))
            big = 8192.0
            step(ts(sel[:, :, :], dest[:, :, :], -1.0, big, ALU.mult, ALU.add))
            step(tt(sel[:, :, :], sel[:, :, :], chosen[:, :, :], ALU.mult))
            step(nc.vector.tensor_reduce(d01[:, 0, :], sel[:, :, :], AX.X, ALU.max))
            step(ts(d01[:, 0, :], d01[:, 0, :], -1.0, big, ALU.mult, ALU.add))
            step(ts(sel[:, :, :], dest[:, :, :], 1.0, None, ALU.add))
            step(tt(sel[:, :, :], sel[:, :, :], chosen[:, :, :], ALU.mult))
            step(nc.vector.tensor_reduce(d01[:, 1, :], sel[:, :, :], AX.X, ALU.max))
            step(ts(d01[:, 1, :], d01[:, 1, :], -1.0, None, ALU.add))
            for k in range(2):
                step(tt(sel[:, :, :], dest[:, :, :], d01[:, k, :].unsqueeze(2).broadcast_to([P, 3, NE]), ALU.is_equal))
                step(tt(sel[:, :, :], sel[:, :, :], wts[:, :, :], ALU.mult))
                step(nc.vector.tensor_reduce(w01[:, k, :], sel[:, :, :], AX.X, ALU.add))
            step(ts(d01i[:, :], d01[:, :, :].rearrange("p k i -> p (k i)"), 0.0, None, ALU.max))
    mixing.close()

    with ExitStack() as es:
        sc = es
        ring = sb("ring", [P, 6, 4096], scope=sc)
        xs = sb("xs", [P, 2, 512], scope=sc)
        xt = sb("xt", [P, KT, SLOT], scope=sc)
        sgt = sb("sgt", [SLOT, FE], scope=sc)
        ups = sb("ups", [SLOT, FE], scope=sc)
        att = sb("att", [P, FT, SLOT], scope=sc)
        ysb = sb("ysb", [P, 2, 512], scope=sc)
        p2 = sem("e_p2")
        block = es.enter_context(nc.Block())
        blocks = lambda eng: eng.value_load(bei[0:1, 32:33], min_val=1, max_val=MAXB)

        @block.sync
        def _(sp):
            n = blocks(sp)
            with sp.Fori(0, n) as b:
                e = sp.value_load(bei[0:1, bass.ds(b, 1)], min_val=0, max_val=NE - 1)
                for u in range(12):
                    src = (w_gate, w_up)[u % 2][bass.ds(e, 1), u // 2] if u < 8 else w_down[bass.ds(e, 1), u - 8]
                    src = src.rearrange("e p k n -> p (e k) n")
                    sp.wait_ge(used[u % 6], 2 * b + u // 6)
                    sp.dma_start(ring[:, u % 6, :].rearrange("p (k n) -> p k n", n=src.shape[2]), src
                                 ).then_inc(ld_e[u % 6], 16)

        def unit(u, n):
            return ring[:, u % 6, :].rearrange("p (k n) -> p k n", n=n)

        @block.tensor
        def _(pe):
            n = blocks(pe)

            def gather(b):
                pe.wait_ge(pick_ok, b + 1)
                for c in range(4):
                    for i in range(3):
                        m = nc.tensor.matmul(PS[C * (c % 2):C * (c % 2) + C, 4 + c // 2, :], pick[:, i, :],
                                             h2[:, i, 512 * c:512 * c + 512], start=(i == 0), stop=(i == 2),
                                             skip_group_check=True)
                m.then_inc(t_pk, 1)

            def gather_turn(b):
                pe.wait_ge(xs_ev, b + 1)
                for q in range(2):
                    for m_ in range(4):
                        m = nc.tensor.transpose(PS[:, 6 + q, m_ * P:(m_ + 1) * P], xs[:, q, m_ * P:(m_ + 1) * P],
                                                ident[:, :])
                m.then_inc(t_xt, 1)

            gather(0)
            gather_turn(0)
            with pe.Fori(0, n) as b:
                pe.wait_ge(xt_ev, b + 1)
                pe.wait_ge(gu_ok, b)
                for q in range(4):
                    for u in (2 * q, 2 * q + 1):
                        pe.wait_ge(ld_e[u % 6], 32 * b + 16 * (u // 6) + 16)
                    for k in range(4):
                        for c in range(2):
                            for g in range(2):
                                m = nc.tensor.matmul(PS[C * g:C * g + C, c, :], xt[:, 4 * q + k, :],
                                                     unit(2 * q + g, FE)[:, k, 512 * c:512 * c + 512],
                                                     start=(q == 0 and k == 0), stop=(q == 3 and k == 3),
                                                     skip_group_check=True)
                                if k == 3 and c == 1:
                                    m.then_inc(used[(2 * q + g) % 6], 1)
                pe.wait_ge(dn_ev, b)
                gather(b + 1)
                pe.wait_ge(act_ev, 2 * b + 2)
                pe.sem_inc(past_pe, 1)
                for f in range(FT):
                    m = nc.tensor.transpose(PS[:, 3, f * SLOT:(f + 1) * SLOT], sgt[:, f * P:(f + 1) * P],
                                            ident[0:SLOT, 0:SLOT])
                m.then_inc(t_at, 1)
                gather_turn(b + 1)
                pe.wait_ge(at_ev, b + 1)
                pe.wait_ge(xs_ev, b + 2)
                for q in range(4):
                    u = 8 + q
                    pe.wait_ge(ld_e[u % 6], 32 * b + 32)
                    for k in range(2):
                        for c in range(4):
                            m = nc.tensor.matmul(PS[C * (c % 2):C * (c % 2) + C, 4 + c // 2, :], att[:, 2 * q + k, :],
                                                 unit(u, D)[:, k, 512 * c:512 * c + 512],
                                                 start=(q == 0 and k == 0), stop=(q == 3 and k == 1),
                                                 skip_group_check=True)
                    m.then_inc(used[u % 6], 1)

        @block.scalar
        def _(act):
            n = blocks(act)

            def gather_out(b):
                act.wait_ge(t_pk, b + 1)
                nc.scalar.copy(xs[:, 0, :], PS[:, 4, :])
                nc.scalar.copy(xs[:, 1, :], PS[:, 5, :]).then_inc(xs_ev, 1)

            gather_out(0)
            with act.Fori(0, n) as b:
                act.wait_ge(used[7 % 6], 2 * b + 2)
                act.wait_ge(t_at, b)
                nc.scalar.activation(sgt[:, :], PS[0:C, 0:2, :].rearrange("p c n -> p (c n)"), ACT.Sigmoid
                                     ).then_inc(up_ev, 1)
                nc.scalar.copy(ups[:, :], PS[C:P, 0:2, :].rearrange("p c n -> p (c n)")).then_inc(up_ev, 1)
                gather_out(b + 1)
                act.wait_ge(t_at, b + 1)
                nc.scalar.copy(att[:, :, :].rearrange("p f s -> p (f s)"), PS[:, 3, :]).then_inc(at_ev, 1)
                act.wait_ge(used[11 % 6], 2 * b + 2)
                act.wait_ge(y_st, 32 * b)
                for c in range(2):
                    m = nc.scalar.copy(ysb[:, c, :], PS[:, 4 + c, :])
                m.then_inc(dn_ev, 1)

        @block.vector
        def _(ve):
            n = blocks(ve)
            o = [0]

            def picks(b):
                ve.wait_ge(t_pk, b)
                for i in range(3):
                    ts_ = nc.vector.tensor_scalar(pick2[:, i, :], slotf[:, :], d01[:, 0, i:i + 1], None, ALU.is_equal)
                ts_.then_inc(p2, 1)
                ve.wait_ge(p2, 2 * b + 1)
                for i in range(3):
                    m = nc.vector.scalar_tensor_tensor(out=pick[:, i, :], in0=slotf[:, :], scalar=d01[:, 1, i:i + 1],
                                                       in1=pick2[:, i, :], op0=ALU.is_equal, op1=ALU.add)
                m.then_inc(pick_ok, 1)
                ve.wait_ge(pick_ok, b + 1)
                nc.vector.tensor_scalar(slotf[:, :], slotf[:, :], float(SLOT), None, ALU.add).then_inc(p2, 1)
                ve.wait_ge(p2, 2 * b + 2)

            def turned(b):
                ve.wait_ge(t_xt, b + 1)
                for q in range(2):
                    m = nc.vector.tensor_copy(xt[:, 8 * q:8 * q + 8, :].rearrange("p (h m) s -> p m h s", h=2),
                                              PS[:, 6 + q, :].rearrange("p (m h s) -> p m h s", m=4, h=2))
                m.then_inc(xt_ev, 1)

            picks(0)
            turned(0)
            with ve.Fori(0, n) as b:
                picks(b + 1)
                ve.wait_ge(up_ev, 2 * b + 1)
                nc.vector.tensor_tensor(sgt[:, :], sgt[:, :], PS[0:C, 0:2, :].rearrange("p c n -> p (c n)"), ALU.mult
                                        ).then_inc(act_ev, 1)
                ve.wait_ge(up_ev, 2 * b + 2)
                ve.wait_ge(act_ev, 2 * b + 1)
                ve.sem_inc(gu_ok, 1)
                nc.vector.tensor_tensor(sgt[:, :], sgt[:, :], ups[:, :], ALU.mult).then_inc(act_ev, 1)
                turned(b + 1)

        @block.gpsimd
        def _(pool):
            n = blocks(pool)
            yv = ybuf.rearrange("(b s) (q h n) -> b h s q n", s=SLOT, q=2, h=2)
            with pool.Fori(0, n) as b:
                pool.wait_ge(dn_ev, b + 1)
                for h in range(2):
                    pool.dma_start(yv[bass.ds(b, 1), h].rearrange("b s q n -> (b s) q n"), ysb[C * h:C * h + C]
                                   ).then_inc(y_st, 16)
            pool.wait_ge(y_st, n * 32)

    with ExitStack() as es:
        yg = sb("yg", [P, 2, 3, D], scope=es)
        gtm = sb("gtm", [P, 2, D], scope=es)
        gtr = sb("gtr", [P, D], scope=es)
        fg = sb("fg", [P, D], scope=es)
        hot = sb("hot", [P, 2, P], scope=es)
        s_own, v_own, q_own, sb2 = (sem("z_" + n, es) for n in "s_own v_own q_own sb2".split())
        block = es.enter_context(nc.Block())

        @block.gpsimd
        def _(pool):
            for k in range(2):
                for i, (t0, n) in enumerate(TILES):
                    pool.indirect_dma_start(yg[0:n, k, i, :], None, ybuf[:, :],
                                            bass.IndirectOffsetOnAxis(ap=d01i[0:n, 3 * k + i:3 * k + i + 1], axis=0)
                                            ).then_inc(y_in, 16)
            n_ = [0]

            def own(ins):
                n_[0] += 1
                ins.then_inc(q_own, 1)
                pool.wait_ge(q_own, n_[0])

            own(nc.gpsimd.memset(gtr[:, :], 0.0))
            own(nc.gpsimd.memset(hot[:, :, :], 0.0))
            own(nc.gpsimd.memset(hot[0:1, 0, :], 1.0))
            own(nc.gpsimd.affine_select(out=hot[:, 1, 0:C], in_=ones[:, 0:C], compare_op=ALU.is_ge, fill=0.0, base=8,
                                        pattern=[[1, C]], channel_multiplier=-8))
            own(nc.gpsimd.affine_select(out=hot[:, 1, 0:C], in_=hot[:, 1, 0:C], compare_op=ALU.is_ge, fill=0.0, base=-1,
                                        pattern=[[-1, C]], channel_multiplier=8))
            pool.sem_inc(s_own, 1)

        @block.sync
        def _(sp):
            sp.dma_start(fg[:, :], A["final_g"].partition_broadcast(P)).then_inc(s_fg, 16)
            for i, (t0, n) in enumerate(TILES):
                dst = O["y_prompt"][0, t0:t0 + n] if i < 2 else O["y_sample"].rearrange("b l d -> (b l) d")
                sp.wait_ge(s_fin, i + 1)
                sp.dma_start(dst, x2[0:n, i, :]).then_inc(y_out, 16)
            sp.wait_ge(y_out, 48)

        @block.tensor
        def _(pe):
            for k in range(KT):
                m = nc.tensor.transpose(PS[0:NC9, k // 4, (k % 4) * P:(k % 4 + 1) * P], adaT[:, GT_M + k, :], ident[:, :])
            m.then_inc(t_gt, 1)
            pe.wait_ge(gt_ev, 1)
            pe.wait_ge(s_own, 1)
            for v in range(2):
                for c in range(4):
                    m = nc.tensor.matmul(PS[:, 4 * v + c, :], hot[:, v, :], gtr[:, 512 * c:512 * c + 512], start=True,
                                         stop=True)
                m.then_inc(t_gm, 1)

        @block.scalar
        def _(act):
            act.wait_ge(t_gt, 1)
            act.wait_ge(s_own, 1)
            nc.scalar.copy(gtr[0:NC9, :], PS[0:NC9, 0:4, :].rearrange("p c n -> p (c n)")).then_inc(gt_ev, 1)
            for v in range(2):
                act.wait_ge(t_gm, v + 1)
                nc.scalar.copy(gtm[:, v, :], PS[:, 4 * v:4 * v + 4, :].rearrange("p c n -> p (c n)")).then_inc(gm_ev, 1)
            for i, (t0, n) in enumerate(TILES):
                act.wait_ge(v_own, 3 * i + 3)
                nc.scalar.activation(yg[0:n, 0, i, :], x2[0:n, i, :], ACT.Square, accum_out=ssq[0:n, i:i + 1]
                                     ).then_inc(a_own, 1)
                act.wait_ge(a_own, 2 * i + 1)
                nc.scalar.activation(ssq[0:n, 4 + i:5 + i], ssq[0:n, i:i + 1], ACT.Sqrt, bias=eps[0:n, 0:1],
                                     scale=1.0 / D).then_inc(a_own, 1)

        @block.vector
        def _(ve):
            ve.wait_ge(gm_ev, 2)
            o = Order(ve, v_own)
            ve.wait_ge(y_in, 96)
            for i, (t0, n) in enumerate(TILES):
                y0, y1, xx = yg[0:n, 0, i, :], yg[0:n, 1, i, :], x2[0:n, i, :]
                o.did(nc.vector.tensor_scalar(y0, y0, w01[0:n, 0, i:i + 1], None, ALU.mult))
                o.settle()
                o.did(nc.vector.scalar_tensor_tensor(out=y0, in0=y1, scalar=w01[0:n, 1, i:i + 1], in1=y0,
                                                     op0=ALU.mult, op1=ALU.add))
                o.settle()
                nc.vector.tensor_tensor(y0, y0, gtm[0:n, i // 2, :], ALU.mult).then_inc(sb2, 1)
                ve.wait_ge(sb2, i + 1)
                o.did(nc.vector.tensor_tensor(xx, xx, y0, ALU.add))
            ve.wait_ge(s_fg, 16)
            for i, (t0, n) in enumerate(TILES):
                xx = x2[0:n, i, :]
                ve.wait_ge(a_own, 2 * i + 2)
                o.did(nc.vector.reciprocal(ssq[0:n, 4 + i:5 + i], ssq[0:n, 4 + i:5 + i]))
                o.settle()
                nc.vector.scalar_tensor_tensor(out=xx, in0=xx, scalar=ssq[0:n, 4 + i:5 + i], in1=fg[0:n, :],
                                               op0=ALU.mult, op1=ALU.mult).then_inc(s_fin, 1)


INPUTS = ["x_prompt", "x_sample", "state_wkv", "state_pool", "state_shift", "c_prompt", "c_sample", "w_ada", "b_ada",
          "norm1_g", "norm2_g", "w_in", "w_pool", "pool_scale", "mu_shift", "w0", "w2", "a0", "a2", "g2", "k_k", "k_a",
          "r_k", "lnx_w", "lnx_b", "w_out", "w_router", "b_router", "w_gate", "w_up", "w_down", "final_g"]
OUTPUTS = [("y_prompt", (1, NP_TOK, D)), ("y_sample", (NB, NL, D)), ("wkv_p", (1, 1, RW // HD, HD, HD)),
           ("pool_p", (1, 1, BUF, PW)), ("shift_p", (1, 1, SH)), ("wkv_s", (1, NB, RW // HD, HD, HD)),
           ("pool_s", (1, NB, BUF, PW)), ("shift_s", (1, NB, SH))]


def kernel(**inputs):
    import numpy as np
    import concourse.bacc as bacc
    from concourse.bass_utils import run_bass_kernel_spmd

    nc = bacc.Bacc("TRN2", target_bir_lowering=False, num_devices=1)
    arrays = {f"in_{n}": np.ascontiguousarray(inputs[n]) for n in INPUTS}
    A = {n: nc.dram_tensor(f"in_{n}", arrays[f"in_{n}"].shape, F32, kind="ExternalInput").ap() for n in INPUTS}
    O = {n: nc.dram_tensor(f"out_{n}", shape, F32, kind="ExternalOutput").ap() for n, shape in OUTPUTS}
    build(nc, A, O)
    r = run_bass_kernel_spmd(nc, [arrays], core_ids=[0])
    return tuple(r.results[0][f"out_{n}"] for n, _ in OUTPUTS)
```

```python
from contextlib import ExitStack

import concourse.bass as bass
from concourse import mybir
from concourse.alu_op_type import AluOpType as ALU

ACT = mybir.ActivationFunctionType
AX = mybir.AxisListType
F32 = mybir.dt.float32
I32 = mybir.dt.int32
U32 = mybir.dt.uint32

P = 128
D = 2048
KT = D // P
NP_TOK, NB, NL = 256, 8, 8
T = NP_TOK + NB * NL
TILES = [(0, 128), (128, 128), (256, 64)]
NC9 = 1 + NB
WIN = (2, 4, 8, 16)
BUF = 15
PW = 1024
RW = 1024
HD = 64
PAIRS = RW // P
SH = 3 * RW + 64 + 64 + 160
PROJ = PW + SH
C = 64
NCH = T // C
EXT = BUF + NP_TOK
EXTS = BUF + NL
ZS = 1 + NL
ZW = 1 + NP_TOK + NB * ZS
NE, NG, EPG = 16, 4, 4
FE = 1024
FT = FE // P
UNIT = 4096
SLOT = 64
MAXB = NE + (2 * T - 1) // SLOT
RMS_EPS, LNX_EPS = 1e-6, 64e-5
DECAY = 0.6065306597126334
K_MU, K_W0, K_A0, K_KK, K_KA, K_RK, K_LW, K_LB = 0, 3, 4, 5, 6, 7, 8, 9
R_PS, R_G1, R_G2, R_MUT = 80, 88, 104, 120
NROW = 123
NADA = 6 * KT
SH_A, SC_A, GT_A, SH_M, SC_M, GT_M = (k * KT for k in range(6))


def at(first, n=1):
    return slice(first, first + n) if isinstance(first, int) else bass.ds(first, n)


def earlier(eng, sem, turns, each=1):
    if not isinstance(turns, int) or turns > 0:
        eng.wait_ge(sem, turns * each)


class Order:

    def __init__(self, eng, sem, base=0):
        self.eng, self.sem, self.base, self.n = eng, sem, base, 0

    def did(self, ins):
        self.n += 1
        ins.then_inc(self.sem, 1)
        return ins

    def settle(self):
        self.eng.wait_ge(self.sem, self.base + self.n)


def clear(nc, sems):
    nums = sorted(s.num for s in sems)
    runs = []
    for n in nums:
        if runs and n == runs[-1][1]:
            runs[-1][1] = n + 1
        else:
            runs.append([n, n + 1])
    with nc.Block() as block:
        @block.gpsimd
        def _(pool):
            for lo, hi in runs:
                pool.sem_clear(range(lo, hi))


def build(nc, A, O):
    ctx = ExitStack()
    with ctx:
        def sb(name, shape, dt=F32, scope=None):
            return (scope or ctx).enter_context(nc.sbuf_tensor(name, shape, dt))

        own = {}

        def sem(name, scope=None):
            handle = (scope or ctx).enter_context(nc.semaphore(name))
            own.setdefault(id(scope), []).append(handle)
            return handle

        PS = ctx.enter_context(nc.psum_tensor("PS", [P, 8, 512], F32))
        ident = sb("ident", [P, P])
        eps = sb("eps", [P, 2])
        PT = sb("PT", [P, P])
        bT = sb("bT", [P, NADA])
        adaT = sb("adaT", [P, NADA, NC9])
        silT = sb("silT", [P, KT, 32])
        catT = sb("catT", [P, KT, T])

        ring = sb("ring", [P, 6 * UNIT])
        cut, taken = {}, 0
        for name, shape in (("hT", (KT, T)), ("abuf", (2, KT // 2, 512)), ("sprevT", (27, NB)), ("spT", (8, NB * BUF)),
                            ("asum", (512,)), ("onesb", (P,)), ("onesd", (P,)), ("gs", (KT, NC9)),
                            ("zs", (2, NCH, C)), ("gs_", (P,)), ("sgy", (2, C)), ("a4", (4, NC9))):
            size = 1
            for n in shape:
                size *= n
            v, taken = ring[:, taken:taken + size], taken + size
            cut[name] = (v if len(shape) == 1 else v.rearrange("p (a b) -> p a b", a=shape[0]) if len(shape) == 2 else
                         v.rearrange("p (a b c) -> p a b c", a=shape[0], b=shape[1]))
        hT, abuf, sprevT, spT, asum, onesb, onesd, gs, zs, gs_, sgy, a4 = cut.values()
        assert taken <= 4 * UNIT
        wo = ring[:, 4 * UNIT:6 * UNIT].rearrange("p (j k n) -> p j k n", j=4, k=KT)
        wbuf = wo[:, 0:3]
        prep = ExitStack()
        w_in = A["w_in"][0].rearrange("(k p) n -> p k n", p=P)
        w_ada = A["w_ada"][0].rearrange("(u k p) n -> u p k n", p=P, u=2)
        ld_w = [sem(f"ld_w{j}") for j in range(3)]
        s_wo = [sem(f"s_wo{j}") for j in range(4)]
        w_out = A["w_out"][0].rearrange("(k p) n -> p k n", p=P)
        shift_out = sem("shift_out")
        past_pe, past_ve, past_pool = (sem(n) for n in "past_pe past_ve past_pool".split())

        phase_a(nc, A, O, sb, sem, prep, locals())
        clear(nc, own[id(prep)])
        prep.close()
        heads = ExitStack()
        phase_b(nc, A, O, sb, sem, heads, locals())
        clear(nc, own[id(heads)])
        heads.close()
        phase_mix(nc, A, O, sb, sem, locals())


def phase_a(nc, A, O, sb, sem, sc, G):
    PS, ident, eps, PT, bT, adaT, silT = (G[k] for k in "PS ident eps PT bT adaT silT".split())
    hT, wbuf, abuf, sprevT, spT, onesb, onesd, asum = (G[k] for k in "hT wbuf abuf sprevT spT onesb onesd asum".split())
    w_in, w_ada, ld_w = G["w_in"], G["w_ada"], G["ld_w"]
    with ExitStack() as es:
        x = sb("x_a", [P, 3, D], scope=sc)
        junk = sb("junk", [P, D], scope=sc)
        crow = sb("crow", [NC9, D], scope=sc)
        srow = sb("srow", [NB, SH], scope=sc)
        prow = sb("prow", [P, P], scope=sc)
        brow = sb("brow", [NADA, P], scope=sc)
        poolrow = sb("poolrow", [NB * BUF, PW], scope=sc)
        ss = sb("ss", [P, 4], scope=sc)
        ss2 = sb("ss2", [P, 4], scope=sc)
        gs = G["gs"]
        asum4 = sb("asum4", [P, 4, NC9], scope=sc)
        ld_x = [sem(f"ld_x{i}", sc) for i in range(3)]
        ld_c, ld_s, ld_p, ld_b, ld_pool = (sem(n, sc) for n in "ld_c ld_s ld_p ld_b ld_pool".split())
        ld_a = [sem(f"ld_a{j}", sc) for j in range(2)]
        id_ready, prow_zero, cs_ready = (sem(n, sc) for n in "id_ready prow_zero cs_ready".split())
        t_par, t_c, t_s, t_pool, t_x, x_evac, ada_mm, ada_used, ada_psum_free = (
            sem(n, sc) for n in "t_par t_c t_s t_pool t_x x_evac ada_mm ada_used ada_psum_free".split())
        ada_copied, ada_red, par_ev, c_ev, sq_done, sqrt_done, xs_done, gp_seq, ve_seq, sil_a, x_evac2 = (
            sem(n, sc) for n in "ada_copied ada_red par_ev c_ev sq_done sqrt_done xs_done gp_seq ve_seq sil_a x_evac2".split())
        block = es.enter_context(nc.Block())

        @block.sync
        def _(sp):
            sp.dma_start(crow[0:1, :], A["c_prompt"]).then_inc(ld_c, 16)
            sp.dma_start(crow[1:NC9, :], A["c_sample"]).then_inc(ld_c, 16)
            for u in range(2):
                sp.dma_start(abuf[:, u], w_ada[u, :, :, 0:512]).then_inc(ld_a[u], 16)
            sp.wait_ge(prow_zero, 1)
            rows = [("mu_shift", 0, 0, 24)] + [(n, 24 + 8 * k, 0, 8) for k, n in enumerate(
                ["w0", "a0", "k_k", "k_a", "r_k", "lnx_w", "lnx_b", "pool_scale"])]
            rows += [("norm1_g", R_G1, 0, 16), ("norm2_g", R_G2, 0, 16), ("mu_shift", R_MUT, 24, 2)]
            for name, at, r0, n in rows:
                sp.dma_start(prow[at:at + n, :], A[name][0, r0 * P:(r0 + n) * P].rearrange("(r c) -> r c", c=P)
                             ).then_inc(ld_p, 16)
            sp.dma_start(prow[R_MUT + 2:R_MUT + 3, 0:32], A["mu_shift"][0:1, 26 * P:SH]).then_inc(ld_p, 16)
            with sp.Fori(1, 8) as i:
                for u in range(2):
                    sp.wait_ge(ada_used, i * 2 - 1 + u)
                    sp.dma_start(abuf[:, u], w_ada[u, :, :, bass.ds(i * 512, 512)]).then_inc(ld_a[u], 16)
            for j in range(3):
                sp.dma_start(wbuf[:, j], w_in[:, :, j * P:(j + 1) * P]).then_inc(ld_w[j], 16)

        @block.scalar
        def _(act):
            for i, (t0, n) in enumerate(TILES):
                src = A["x_prompt"][0, t0:t0 + n] if i < 2 else A["x_sample"].rearrange("b l d -> (b l) d")
                act.dma_start(x[0:n, i, :], src).then_inc(ld_x[i], 16)
            act.dma_start(brow[:, :], A["b_ada"][0].rearrange("(r c) -> r c", c=P)).then_inc(ld_b, 16)
            act.dma_start(srow[:, :], A["state_shift"][0]).then_inc(ld_s, 16)
            act.dma_start(poolrow[:, :], A["state_pool"][0].rearrange("b l d -> (b l) d")).then_inc(ld_pool, 16)
            act.wait_ge(ld_c, 32)
            nc.scalar.activation(junk[0:NC9, :], crow[:, :], ACT.Sigmoid).then_inc(sil_a, 1)
            act.wait_ge(cs_ready, 1)
            for i, (t0, n) in enumerate(TILES):
                act.wait_ge(ld_x[i], 16)
                nc.scalar.activation(junk[0:n, :], x[0:n, i, :], ACT.Square,
                                     accum_out=ss[0:n, i:i + 1]).then_inc(sq_done, 1)
                act.wait_ge(sq_done, i + 1)
            act.wait_ge(gp_seq, 1)
            for i, (t0, n) in enumerate(TILES):
                nc.scalar.activation(ss2[0:n, i:i + 1], ss[0:n, i:i + 1], ACT.Sqrt, bias=eps[0:n, 0:1],
                                     scale=1.0 / D).then_inc(sqrt_done, 1)
            for k in range(0, KT, 2):
                act.wait_ge(t_x, k + 1)
                nc.scalar.copy(hT[:, k, :], PS[:, 4 + k % 4, 0:T]).then_inc(x_evac, 1)

        @block.gpsimd
        def _(pool):
            nc.gpsimd.memset(eps[:, 0:1], RMS_EPS)
            nc.gpsimd.memset(eps[:, 1:2], LNX_EPS).then_inc(gp_seq, 1)
            nc.gpsimd.memset(ident[:, :], 0.0).then_inc(gp_seq, 1)
            pool.wait_ge(gp_seq, 2)
            nc.gpsimd.affine_select(out=ident[:, :], in_=ident[:, :], compare_op=ALU.not_equal, fill=1.0, base=0,
                                    pattern=[[-1, P]], channel_multiplier=1).then_inc(id_ready, 1)
            for t, v in ((onesb, 1.0), (onesd, 1.0 / HD)):
                nc.gpsimd.memset(t[:, :], 0.0).then_inc(gp_seq, 1)
            pool.wait_ge(gp_seq, 4)
            for t, v in ((onesb, 1.0), (onesd, 1.0 / HD)):
                nc.gpsimd.memset(t[0:64, 0:64], v)
                nc.gpsimd.memset(t[64:P, 64:P], v)

        @block.tensor
        def _(pe):
            pe.wait_ge(id_ready, 1)
            pe.wait_ge(cs_ready, 1)
            for k in range(KT):
                m = nc.tensor.transpose(PS[:, 0, k * NC9:(k + 1) * NC9], crow[:, k * P:(k + 1) * P],
                                        ident[0:NC9, 0:NC9])
            m.then_inc(t_c, 1)

            def halves(i):
                for u in range(2):
                    pe.wait_ge(ld_a[u], 16 * i + 16)
                    if u == 0:
                        pe.wait_ge(ada_psum_free, i + 1)
                    ada_half(nc, PS[:, 0, :], silT, abuf, u).then_inc(ada_used, 1)

            def turn(i):
                pe.wait_ge(ada_copied, i + 1)
                ada_turn(nc, PS[:, 3, :], asum, ident).then_inc(ada_mm, 1)

            pe.wait_ge(c_ev, 1)
            halves(0)
            pe.wait_ge(ld_p, 16 * 13)
            nc.tensor.transpose(PS[:, 1, 0:NROW], prow[0:NROW, :], ident[0:NROW, 0:NROW])
            pe.wait_ge(ld_b, 16)
            nc.tensor.transpose(PS[:, 1, P:P + NADA], brow[:, :], ident[0:NADA, 0:NADA]).then_inc(t_par, 1)
            pe.wait_ge(ld_s, 16)
            for j in range(27):
                n = min(P, SH - j * P)
                m = nc.tensor.transpose(PS[0:n, 2, j * NB:(j + 1) * NB], srow[:, j * P:j * P + n],
                                        ident[0:NB, 0:NB])
            m.then_inc(t_s, 1)
            pe.wait_ge(ld_pool, 16)
            for j in range(8):
                m = nc.tensor.transpose(PS[:, 4 + j // 4, (j % 4) * 120:(j % 4) * 120 + 120],
                                        poolrow[:, j * P:(j + 1) * P], ident[0:120, 0:120])
            m.then_inc(t_pool, 1)
            turn(0)
            halves(1)
            pe.wait_ge(par_ev, 1)
            pe.wait_ge(xs_done, 3)
            for k in range(KT):
                if k >= 4:
                    pe.wait_ge((x_evac, x_evac2)[k % 2], k // 2 - 1)
                for i, (t0, n) in enumerate(TILES):
                    m = nc.tensor.transpose(PS[:, 4 + k % 4, t0:t0 + n], x[0:n, i, k * P:(k + 1) * P],
                                            ident[0:n, 0:n])
                m.then_inc(t_x, 1)
            turn(1)
            with pe.Fori(2, 8) as i:
                halves(i)
                turn(i)

        @block.vector
        def _(ve):
            o = Order(ve, ve_seq)
            nc.vector.memset(prow[:, :], 0.0).then_inc(prow_zero, 1)
            ve.wait_ge(sil_a, 1)
            nc.vector.tensor_tensor(crow[:, :], crow[:, :], junk[0:NC9, :], ALU.mult).then_inc(cs_ready, 1)
            ve.wait_ge(t_c, 1)
            o.did(nc.vector.memset(silT[:, :, :], 0.0))
            o.settle()
            nc.vector.tensor_copy(silT[:, :, 0:NC9], PS[:, 0, 0:KT * NC9].rearrange("p (k c) -> p k c", c=NC9)
                                  ).then_inc(c_ev, 1)
            ve.sem_inc(ada_psum_free, 1)

            def ada_copy(i):
                ve.wait_ge(ada_used, 2 * i + 2)
                nc.vector.tensor_copy(asum[:, :], PS[:, 0, :]).then_inc(ada_copied, 1)

            def ada_store(i):
                ve.wait_ge(ada_mm, i + 1)
                nc.vector.tensor_reduce(asum4[:, :, :], ada_parts(PS[:, 3, :]), AX.X, ALU.add).then_inc(ada_red, 1)
                ve.wait_ge(ada_red, i + 1)
                nc.vector.tensor_tensor(adaT[:, at(i * 4, 4), :], asum4[:, :, :],
                                        bT[:, at(i * 4, 4)].unsqueeze(2).broadcast_to([P, 4, NC9]),
                                        ALU.add).then_inc(ada_psum_free, 1)

            ada_copy(0)
            ve.wait_ge(t_par, 1)
            o.did(nc.vector.tensor_copy(PT[:, 0:NROW], PS[:, 1, 0:NROW]))
            o.did(nc.vector.tensor_copy(bT[:, :], PS[:, 1, P:P + NADA]))
            ve.wait_ge(t_s, 1)
            o.did(nc.vector.tensor_copy(sprevT[:, 0:26, :], PS[:, 2, 0:26 * NB].rearrange("p (j b) -> p j b", b=NB)))
            o.did(nc.vector.tensor_copy(sprevT[0:32, 26, :], PS[0:32, 2, 26 * NB:27 * NB]))
            ve.wait_ge(t_pool, 1)
            for h in range(2):
                m = o.did(nc.vector.tensor_copy(spT[:, 4 * h:4 * h + 4, :],
                                                PS[:, 4 + h, 0:480].rearrange("p (j b) -> p j b", b=120)))
            o.settle()
            o.did(nc.vector.memset(ss2[:, 3:4], 0.0))
            nc.vector.memset(ss[:, 3:4], 0.0).then_inc(par_ev, 1)
            ada_store(0)
            for i, (t0, n) in enumerate(TILES):
                ve.wait_ge(sqrt_done, i + 1)
                o.did(nc.vector.reciprocal(ss2[0:n, i:i + 1], ss2[0:n, i:i + 1]))
            o.settle()
            for i, (t0, n) in enumerate(TILES):
                nc.vector.tensor_scalar(x[0:n, i, :], x[0:n, i, :], ss2[0:n, i:i + 1], None, ALU.mult
                                        ).then_inc(xs_done, 1)
            ada_copy(1)
            for k in range(1, KT, 2):
                ve.wait_ge(t_x, k + 1)
                nc.vector.tensor_copy(hT[:, k, :], PS[:, 4 + k % 4, 0:T]).then_inc(x_evac2, 1)
            ada_store(1)
            with ve.Fori(2, 8) as i:
                ada_copy(i)
                ada_store(i)
            ve.wait_ge(ada_psum_free, 9)
            o.did(nc.vector.tensor_scalar(gs[:, :, :], adaT[:, SC_A:SC_A + KT, :], 1.0, None, ALU.add))
            o.settle()
            o.did(nc.vector.tensor_tensor(gs[:, :, :], gs[:, :, :],
                                          PT[:, R_G1:R_G1 + KT].unsqueeze(2).broadcast_to([P, KT, NC9]), ALU.mult))
            o.settle()
            ve.wait_ge(x_evac, KT // 2)


def ada_half(nc, psum, silT, abuf, u):
    for k in range(KT // 2):
        kt, g = u * (KT // 2) + k, k % 4
        m = nc.tensor.matmul(psum[32 * g:32 * g + 32, :], silT[:, kt, :], abuf[:, u, k, :],
                             start=(kt < 4), stop=(kt >= KT - 4))
    return m


def ada_turn(nc, psum, asum, ident):
    for m_ in range(4):
        m = nc.tensor.transpose(psum[:, m_ * P:(m_ + 1) * P], asum[:, m_ * P:(m_ + 1) * P], ident[:, :])
    return m


def ada_parts(psum):
    return psum.rearrange("p (m g c) -> p m c g", m=4, g=4)[:, :, 0:NC9, :]


def modulate(nc, ve, o, hT, gs, sh, here=None, done=None):
    for k0 in range(0, KT, 4):
        if here is not None:
            ve.wait_ge(here, k0 + 4)
        for k in range(k0, k0 + 4) if here is None else ():
            o.did(nc.vector.tensor_scalar(hT[:, k, 0:NP_TOK], hT[:, k, 0:NP_TOK], gs[:, k, 0:1], sh[:, k, 0:1],
                                          ALU.mult, ALU.add))
        s = hT[:, k0:k0 + 4, NP_TOK:T].rearrange("p k (b l) -> p k b l", l=NL)
        for op, v in ((ALU.mult, gs), (ALU.add, sh)):
            o.did(nc.vector.tensor_tensor(s, s, v[:, k0:k0 + 4, 1:NC9].unsqueeze(3).broadcast_to([P, 4, NB, NL]), op))
            o.settle()
        if done is not None:
            ve.sem_inc(done, 1)


def ext_prompt(e, k0=0, n=NP_TOK):
    return e[:, BUF + k0:BUF + k0 + n]


def ext_sample(e, k0=BUF, n=NL):
    return e[:, EXT:EXT + NB * EXTS].rearrange("p (b l) -> p b l", l=EXTS)[:, :, k0:k0 + n]


FILL = (11, 3, 4, 0, 1, 0, 2, 1, 1, 1, 4, 2, 1)
N_DVE, N_POOL = 55, 6
NPRE = 11
LEVELS = (2, 4, 8, 16)


def phase_b(nc, A, O, sb, sem, sc, G):
    PS, ident, eps, PT, bT, adaT, silT, catT = (G[k] for k in "PS ident eps PT bT adaT silT catT".split())
    hT, wbuf, abuf, sprevT, spT, onesb, onesd, asum = (
        G[k] for k in "hT wbuf abuf sprevT spT onesb onesd asum".split())
    w_in, w_ada, ld_w = G["w_in"], G["w_ada"], G["ld_w"]
    past_pe, past_ve, past_pool = G["past_pe"], G["past_ve"], G["past_pool"]
    shift_out = G["shift_out"]
    W = [PS[:, 4 + b, :] for b in range(4)]
    with ExitStack() as es:
        t = lambda name, shape, dt=F32: sb(name, shape, dt, scope=sc)
        s = lambda names: [sem(n, None if n in ("ld_lora", "ld_sraw", "out_w", "out_p") else sc)
                           for n in names.split()]
        EW = EXT + NB * EXTS
        sraw, s0t, sfin, sout = (t(n, [P, NB, C]) for n in "sraw s0t sfin sout".split())
        ext, sa, sb_ = (x_[:, :, :].rearrange("p b i -> p (b i)")[:, 0:EW] for x_ in (sout, s0t, sfin))
        uvx = t("uvx", [P, 2, NB, C])
        rc = uvx[:, :, :, :].rearrange("p h b i -> p (h b i)").rearrange("p (g n) -> p g n", g=4)
        zd = t("zd", [P, 3, T])
        pooled = zd[:, 0:2, :]
        late = t("late", [P, 2048])
        wp = late[:, :].rearrange("p (g k n) -> p g k n", g=4, k=2)
        kk, rn, ka, k2, rk, bv, tb, yw = (t(n, [P, T]) for n in "kk rn ka k2 rk bv tb yw".split())
        plast = t("plast", [P, P])
        mrow, mcol = t("mrow", [P, P], I32), t("mcol", [P, P], I32)
        mx, mf, mg = t("mx", [P, P], I32), kk[:, 0:P], rn[:, 0:P]
        mask_p, mask_s = t("mask_p", [P, P]), t("mask_s", [P, P])
        lvl_t, lvl_n = t("lvl_t", [C, 6, C], I32), t("lvl_n", [C, 6, C], I32)
        bmask, bmask_i = t("bmask", [P, NB]), t("bmask_i", [P, NB], I32)
        rmask = t("rmask", [P, T])
        lwa, lg1, lg2 = t("lwa", [P, T]), t("lg1", [P, T]), t("lg2", [P, T])
        lz, lzd = t("lz", [P, ZW]), bv
        w2a2, g2a, g2b = t("w2a2", [P, 2, P]), t("g2a", [P, P]), t("g2b", [P, P])
        pc, pomk = t("pc", [P, 10]), t("pomk", [P, 1])
        z3 = t("z3", [P, 3, ZW])
        zr, zk, vp = t("zr", [P, T]), t("zk", [P, T]), t("vp", [P, C + T])
        sg, aa, gg, cs, cse = (t(n, [P, T]) for n in "sg aa gg cs cse".split())
        lam, ilam, lame = (t(n, [P, T]) for n in "lam ilam lame".split())
        ra = t("ra", [P, NCH, 2, 2, C])
        bk = t("bk", [P, NCH, 2, C])
        ptok = bk[:, :, :, :].rearrange("p c x t -> p (c x t)")[:, 0:512]
        bkt = late[:, 1280:1920].rearrange("p (c j) -> p c j", c=NCH)
        uv = t("uv", [P, NCH, P])
        mm = late[:, 0:1280].rearrange("p (c h x t) -> p c h x t", c=NCH, h=2, x=2)
        inv, invt = (t(n, [P, 2, NCH, C]) for n in "inv invt".split())
        zs, gs_, sgy, a4 = (G[n] for n in "zs gs_ sgy a4".split())
        st, stl, pout = late[:, 1920:1984], late[:, 1984:2048], t("pout", [C, P])
        ys = t("ys", [C, NCH, P])
        zlast = t("zlast", [P, 27, NC9])
        (k_iota, k_masks, k_zero, pre_mm, pre_ev, w_used, pool_in, pooled_ok, t_pool, t_pt, ptok_ok, ld_wp,
         ld_lora, ld_sraw, ld_a2) = s(
            "k_iota k_masks k_zero pre_mm pre_ev w_used pool_in pooled_ok t_pool2 t_pt ptok_ok ld_wp "
            "ld_lora ld_sraw ld_a2")
        ld_a2 = [ld_a2, sem("ld_a3", sc)]
        wu, h_ok, n_own, ln_ev, ssm_ok = s("wu0 wu1 wu2"), *s("h_ok n_own ln_ev ssm_ok")
        (t_s0, s0_ev, l_q, l_a, l_g, lev, z_ev, z_done, pc_ok, t_ss, sq_ok, ss_ev, t_bs, rk_ok, bs_ev, bk_ok, ra_ok,
         v_ok, t_tok, tok_ev, t_mm, mm_ev, rst, t_z, z_cp, t_e, inv_ok, a_half, a_cp, a_turn, a_red, t_sg, sg_ev,
         t_g, g_ev, t_u, u_ev, t_st, st_ok, t_y, y_ev, uvx_ok, t_sf, sf_ok, t_so, so_ev, t_yt, yt_ev, t_mn, yc_ok,
         t_vr, vr_ev, fin, cs_ok, cse_ok, e_ok, k2_ok, t_proj, out_w, a_own, v_own, p_own, t_sh, sh_ev, out_p, mix_ev, ptok_ev, ext_ok, ext_used, lzs_ok, lora_ok, k_masks2) = s(
            "t_s0 s0_ev l_q l_a l_g lev z_ev z_done pc_ok t_ss sq_ok ss_ev t_bs rk_ok bs_ev bk_ok ra_ok "
            "v_ok t_tok tok_ev t_mm mm_ev rst t_z z_cp t_e inv_ok a_half a_cp a_turn a_red t_sg sg_ev "
            "t_g g_ev t_u u_ev t_st st_ok t_y y_ev uvx_ok t_sf sf_ok t_so so_ev t_yt yt_ev t_mn yc_ok "
            "t_vr vr_ev fin cs_ok cse_ok e_ok k2_ok t_proj out_w a_own v_own p_own t_sh sh_ev out_p mix_ev ptok_ev ext_ok ext_used lzs_ok lora_ok k_masks2")
        shrow = abuf[0:NC9].rearrange("p u k n -> p (u k n)")
        state_in = A["state_wkv"][0].rearrange("b h i j -> (h i) b j")
        state_out = O["wkv_s"][0].rearrange("(q b) h i j -> b i q h j", b=2)
        prompt_out = O["wkv_p"][0, 0].rearrange("h i j -> i h j")
        RKV = [PW + j * RW for j in range(3)]
        LORA = PW + 3 * RW
        pre_cols = [(k * P, P) for k in range(8)] + [(LORA, P), (LORA + P, P), (LORA + 2 * P, 32)]
        WBASE = [16 * len(range(j, NPRE, 3)) for j in range(3)]
        UBASE = [len(range(j, NPRE, 3)) for j in range(3)]
        lvl_bank = [(0, 3, 1, 2, 0, 3), (1, 2, 0, 3, 1, 2)]
        def mix_out(act, g):
            act.wait_ge(t_pool, g + 1)
            for m_ in range(2):
                m = nc.scalar.activation(catT[:, 2 * g + m_, :], W[m_][:, 0:T], ACT.Copy,
                                         scale=PT[:, R_PS + 2 * g + m_:R_PS + 2 * g + m_ + 1])
            m.then_inc(mix_ev, 1)

        def masks(ve, o):
            ve.wait_ge(k_iota, 6)
            tt, ts = nc.vector.tensor_tensor, nc.vector.tensor_scalar
            o.did(tt(mx[:, :], mrow[:, :], mcol[:, :], ALU.bitwise_xor))
            o.did(tt(mask_p[:, 0:C], mcol[:, 0:C], mrow[:, 0:C], ALU.is_ge))
            o.did(tt(mask_p[:, C:P], mcol[:, C:P], mrow[:, C:P], ALU.is_gt))
            o.settle()
            o.did(ts(mf[:, :], mx[:, :], float(NL), None, ALU.is_lt))
            o.settle()
            o.did(tt(mask_s[:, :], mask_p[:, :], mf[:, :], ALU.mult))
            for n in range(6):
                o.settle()
                o.did(ts(mf[0:C, 0:C], mx[0:C, 0:C], float(2 ** n), None, ALU.is_ge))
                o.did(ts(mg[0:C, 0:C], mx[0:C, 0:C], float(2 ** (n + 1)), None, ALU.is_lt))
                o.settle()
                o.did(tt(mf[0:C, 0:C], mf[0:C, 0:C], mg[0:C, 0:C], ALU.mult))
                o.settle()
                o.did(tt(lvl_t[:, n, :], mf[0:C, 0:C], mask_p[0:C, C:P], ALU.mult))
                o.settle()
                o.did(ts(mg[0:C, 0:C], mask_p[0:C, 0:C], -1.0, 1.0, ALU.mult, ALU.add))
                o.settle()
                o.did(tt(lvl_n[:, n, :], mf[0:C, 0:C], mg[0:C, 0:C], ALU.mult))
                o.settle()
            o.did(ts(bmask[:, :], bmask_i[:, :], 0.0, None, ALU.is_ge))
            o.did(ts(mg[:, 0:NB], bmask_i[:, :], float(NL), None, ALU.is_lt))
            o.settle()
            o.did(tt(bmask[:, :], bmask[:, :], mg[:, 0:NB], ALU.mult))
            o.settle()

        block = es.enter_context(nc.Block())

        @block.sync
        def _(sp):
            sp.dma_start(wp[:, :, :, :], A["w_pool"][0].rearrange("g (k p) n -> p g k n", p=P)).then_inc(ld_wp, 16)
            for u in range(2):
                sp.dma_start(abuf[:, u], w_ada[u, :, :, 8 * 512:9 * 512]).then_inc(ld_a2[u], 16)
            for q in range(3, NPRE):
                c0, n = pre_cols[q]
                sp.wait_ge(wu[q % 3], q // 3)
                sp.dma_start(wbuf[:, q % 3, :, 0:n], w_in[:, :, c0:c0 + n]).then_inc(ld_w[q % 3], 16)
            for j in range(3):
                sp.wait_ge(wu[j], UBASE[j])
                sp.dma_start(wbuf[:, j], w_in[:, :, RKV[j]:RKV[j] + P]).then_inc(ld_w[j], 16)

            with sp.Fori(0, PAIRS - 1) as i:
                for j in range(3):
                    sp.wait_ge(wu[j], UBASE[j] + 1 + i)
                    sp.dma_start(wbuf[:, j], w_in[:, :, bass.ds(RKV[j] + (i + 1) * P, P)]).then_inc(ld_w[j], 16)
                for ch in range(2):
                    for u in range(2):
                        sp.wait_ge(a_half, 4 * i + 2 * ch + u + 1)
                        sp.dma_start(abuf[:, u], w_ada[u, :, :, bass.ds((2 * i + ch + 9) * 512, 512)]
                                     ).then_inc(ld_a2[u], 16)
            for u in range(2):
                sp.wait_ge(a_half, 4 * (PAIRS - 1) + u + 1)
                sp.dma_start(abuf[:, u], w_ada[u, :, :, 23 * 512:24 * 512]).then_inc(ld_a2[u], 16)
            for j in range(4):
                if j < 3:
                    sp.wait_ge(wu[j], UBASE[j] + PAIRS)
                sp.dma_start(G["wo"][:, j], G["w_out"][:, :, j * P:(j + 1) * P]).then_inc(G["s_wo"][j], 16)
            sp.wait_ge(sh_ev, 1)
            for dst, r0, nr in (("shift_p", 0, 1), ("shift_s", 1, NB)):
                sp.dma_start(O[dst][0], shrow[r0:r0 + nr, 0:SH]).then_inc(shift_out, 16)

        @block.gpsimd
        def _(pool):
            for t_, n in ((mrow, 0), (mcol, 1)):
                for h in range(2):
                    nc.gpsimd.iota(t_[64 * h:64 * h + 64, :], pattern=[[0, 2], [n, C]], base=0,
                                   channel_multiplier=1 - n).then_inc(k_iota, 1)
            for h in range(2):
                nc.gpsimd.iota(bmask_i[64 * h:64 * h + 64, :], pattern=[[-8, NB]], base=0,
                               channel_multiplier=1).then_inc(k_iota, 1)
            pool.wait_ge(k_iota, 6)
            for x_ in (ext, rmask, ra, inv, invt, zs, gs_, uv, vp, z3, lz, g2b, lg2, w2a2, zlast):
                nc.gpsimd.memset(x_ if x_ in (ext, zs, gs_) else x_[:], 1.0 if x_ is rmask else 0.0).then_inc(p_own, 1)
            pool.wait_ge(p_own, 15)
            nc.gpsimd.memset(rmask[:, 0:NP_TOK:C], 0.0)
            nc.gpsimd.memset(rmask[:, NP_TOK:T:NL], 0.0)
            for g, w in enumerate(WIN):
                nc.gpsimd.memset(rc[:, g, w - 1:], 1.0 / w)
                for n in range(w - 1):
                    nc.gpsimd.memset(rc[:, g, n:n + 1], 1.0 / (n + 1))
            nc.gpsimd.memset(plast[:, :], 0.0).then_inc(k_zero, 1)
            pool.wait_ge(k_zero, 1)
            pool.dma_start(O["pool_s"][0, :, 0:BUF - NL, :], A["state_pool"][0, :, NL:BUF, :]).then_inc(out_p, 16)
            nc.gpsimd.dma_start(g2b[0:32, :], A["g2"][0, P:160, 0:P]).then_inc(ld_lora, 16)
            nc.gpsimd.dma_start(g2a[:, :], A["g2"][0, 0:P, 0:P]).then_inc(ld_lora, 16)
            nc.gpsimd.dma_start(w2a2[0:64, 0, :], A["w2"][0, :, 0:P]).then_inc(ld_lora, 16)
            nc.gpsimd.dma_start(w2a2[64:P, 1, :], A["a2"][0, :, 0:P]).then_inc(ld_lora, 16)
            nc.gpsimd.dma_start(sraw[:, :, :], state_in[0:P]).then_inc(ld_sraw, 16)
            for hf in range(2):
                pool.wait_ge(ptok_ev, hf + 1)
                pool.dma_start(O["pool_p"][0, 0, :, 512 * hf:512 * hf + 512], ptok[C - BUF:C, :]).then_inc(out_p, 16)
                pool.dma_start(O["pool_s"][0, :, BUF - NL:BUF, 512 * hf:512 * hf + 512], ptok[C:P, :]).then_inc(out_p, 16)
                pool.wait_ge(out_p, 16 * (3 + 2 * hf))
                pool.sem_inc(ptok_ok, 1)

            def pair(i, last):
                o = Order(pool, p_own, 15 + i * N_POOL)
                earlier(pool, t_y, i, NCH)
                pool.sem_inc(past_pool, 1)
                irep = ident[0:C, 0:C].unsqueeze(1).broadcast_to([C, 2 * NCH, C])
                for x_ in (inv, invt):
                    o.did(nc.gpsimd.tensor_copy(x_[0:C].rearrange("p h c t -> p (h c) t"), irep))
                o.did(nc.gpsimd.memset(uv[0:C, :, :], 0.0))
                o.settle()
                pool.sem_inc(rst, 1)
                pool.wait_ge(cs_ok, i + 1)
                earlier(pool, fin, i)
                nc.gpsimd.tensor_tensor(cse[:, :], cs[:, :], sg[:, :], ALU.subtract).then_inc(cse_ok, 1)
                pool.wait_ge(lev, 3 * i + 2)
                pool.sem_inc(past_pool, 1)
                o.did(nc.gpsimd.tensor_scalar(ka[:, :], aa[:, :], pc[:, K_KA:K_KA + 1], pomk[:, 0:1], ALU.mult, ALU.add))
                o.settle()
                pool.wait_ge(z_done, i + 1)
                nc.gpsimd.tensor_tensor(k2[:, :], zk[:, :], ka[:, :], ALU.mult).then_inc(k2_ok, 1)
                if not last:
                    n = i + 1
                    pool.wait_ge(l_g, i + 1)
                    nc.gpsimd.dma_start(g2b[0:32, :], A["g2"][0, P:160, at(n * P, P)]).then_inc(ld_lora, 16)
                    nc.gpsimd.dma_start(g2a[:, :], A["g2"][0, 0:P, at(n * P, P)]).then_inc(ld_lora, 16)
                    nc.gpsimd.dma_start(w2a2[0:64, 0, :], A["w2"][0, :, at(n * P, P)]).then_inc(ld_lora, 16)
                    nc.gpsimd.dma_start(w2a2[64:P, 1, :], A["a2"][0, :, at(n * P, P)]).then_inc(ld_lora, 16)
                    pool.wait_ge(t_s0, i + 1)
                    nc.gpsimd.dma_start(sraw[:, :, :], state_in[at(n * P, P)]).then_inc(ld_sraw, 16)
                pool.wait_ge(u_ev, NCH * i + NCH)
                for h in range(2):
                    o.did(nc.gpsimd.tensor_tensor(
                        uvx[:, h], uv[:, 4, C * h:C * h + C].unsqueeze(1).broadcast_to([P, NB, C]),
                        bmask[:, :].unsqueeze(2).broadcast_to([P, NB, C]), ALU.mult))
                o.settle()
                pool.sem_inc(uvx_ok, 1)
                pool.wait_ge(so_ev, 2 * i + 2)
                so = sout[:, :, :].rearrange("p (q h) j -> p q h j", h=2)
                for b in range(2):
                    for h in range(2):
                        pool.dma_start(state_out[b, :, :, at(2 * i + h), :], so[C * b:C * b + C, :, h:h + 1, :]
                                       ).then_inc(out_w, 16)
                pool.dma_start(prompt_out[:, at(2 * i, 2), :],
                               pout[:, :].rearrange("p (h j) -> p h j", h=2)).then_inc(out_w, 16)
                assert o.n == N_POOL, o.n

            pair(0, False)
            with pool.Fori(1, PAIRS - 1) as i:
                pair(i, False)
            pair(PAIRS - 1, True)
            pool.wait_ge(out_w, 16 * 5 * PAIRS)
            pool.wait_ge(out_p, 16 * 5)

        @block.tensor
        def _(pe):
            def project(j, k, i):
                if k == 0:
                    pe.wait_ge(ld_w[j], WBASE[j] + 16 * (i + 2))
                    pe.wait_ge(z_done, i + 1)
                m = nc.tensor.matmul(PS[:, j, 0:T], wbuf[:, j, k, :], hT[:, k, :], start=(k == 0), stop=(k == KT - 1))
                if k == KT - 1:
                    m.then_inc(wu[j], 1)

            def pool_mix(g):
                pe.wait_ge(pooled_ok, g + 1)
                pe.wait_ge(ld_wp, 16)
                for m_ in range(2):
                    for k in range(2):
                        m = nc.tensor.matmul(W[m_][:, 0:T], wp[:, g, k, m_ * P:(m_ + 1) * P], pooled[:, k, :],
                                             start=(k == 0), stop=(k == 1))
                m.then_inc(t_pool, 1)

            for q in range(NPRE):
                c0, n = pre_cols[q]
                pe.wait_ge(ld_w[q % 3], 16 * (q // 3 + 1))
                if q >= 4:
                    pe.wait_ge(pre_ev, q - 3)
                for k in range(KT):
                    if q == 0 and k % 4 == 0:
                        pe.wait_ge(h_ok, k // 4 + 1)
                    m = nc.tensor.matmul(PS[0:n, q % 4, 0:T], wbuf[:, q % 3, k, 0:n], hT[:, k, :],
                                         start=(k == 0), stop=(k == KT - 1))
                m.then_inc(wu[q % 3], 1)
                if 1 <= q <= 8:
                    pe.wait_ge(pool_in, q)
                    if q == 5:
                        pe.wait_ge(ptok_ok, 1)
                    nc.tensor.transpose(W[2][:, ((q - 1) % 4) * P:((q - 1) % 4 + 1) * P], plast[:, :], ident[:, :]
                                        ).then_inc(t_pt, 1)
                if q in (2, 4, 6, 8):
                    if q > 2:
                        pe.wait_ge(mix_ev, q // 2 - 1)
                    pool_mix(q // 2 - 1)
            pe.wait_ge(ptok_ok, 2)
            pe.wait_ge(mix_ev, 4)
            pe.wait_ge(lora_ok, 1)
            for j in range(3):
                pe.wait_ge(ld_w[j], WBASE[j] + 16)
                pe.wait_ge(pre_ev, NPRE)
                for k in range(KT):
                    m = nc.tensor.matmul(PS[:, j, 0:T], wbuf[:, j, k, :], hT[:, k, :], start=(k == 0), stop=(k == KT - 1))
                m.then_inc(wu[j], 1)

            def ada(i, ch, u):
                pe.wait_ge(ld_a2[u], 16 * (2 * i + ch + 1))
                if u == 0:
                    earlier(pe, a_red, 2 * i + ch)
                ada_half(nc, PS[:, 3, :], silT, abuf, u).then_inc(a_half, 1)

            def turn(i, ch):
                pe.wait_ge(a_cp, 2 * i + ch + 1)
                ada_turn(nc, PS[:, 3, :], asum, ident).then_inc(a_turn, 1)

            def pair(i, last):
                units = iter([] if last else [(j, k) for j in (1, 0, 2) for k in range(KT)])

                def fill(n):
                    for _, (j, k) in zip(range(n), units):
                        project(j, k, i)

                earlier(pe, yc_ok, i)
                earlier(pe, so_ev, i, 2)
                pe.wait_ge(ld_sraw, 16 * i + 16)
                for q in range(4):
                    m = nc.tensor.transpose(W[0][:, q * P:(q + 1) * P], sraw[:, 2 * q:2 * q + 2, :], ident[:, :])
                m.then_inc(t_s0, 1)
                pe.wait_ge(ld_lora, 64 * i + 64)
                nc.tensor.matmul(W[1][:, 0:T], w2a2[:, 0, :], lwa[:, :], start=True, stop=True).then_inc(l_q, 1)
                nc.tensor.matmul(W[2][:, 0:T], w2a2[:, 1, :], lwa[:, :], start=True, stop=True).then_inc(l_a, 1)
                earlier(pe, ln_ev, i, 2)
                nc.tensor.matmul(W[3][:, 0:T], g2a[:, :], lg1[:, :], start=True, stop=False)
                nc.tensor.matmul(W[3][:, 0:T], g2b[:, :], lg2[:, :], start=False, stop=True).then_inc(l_g, 1)
                ada(i, 0, 0)
                pe.wait_ge(sq_ok, i + 1)
                pe.wait_ge(s0_ev, i + 1)
                nc.tensor.matmul(W[0][:, 0:T], onesb[:, :], tb[:, :], start=True, stop=True).then_inc(t_ss, 1)
                ada(i, 0, 1)
                fill(FILL[0])
                pe.wait_ge(rk_ok, i + 1)
                pe.wait_ge(lev, 3 * i + 1)
                nc.tensor.matmul(W[1][:, 0:T], onesb[:, :], rk[:, :], start=True, stop=True).then_inc(t_bs, 1)
                pe.wait_ge(bk_ok, i + 1)
                pe.wait_ge(ssm_ok, i + 1)
                pe.wait_ge(lev, 3 * i + 3)
                for c in range(NCH):
                    dst = W[2][:, c * P:(c + 1) * P] if c < 4 else W[3][:, 0:P]
                    nc.tensor.transpose(dst, bk[:, c].rearrange("p x t -> p (x t)"), ident[:, :])
                for c in range(NCH):
                    dst = W[0][:, c * P:(c + 1) * P] if c < 4 else W[3][:, P:2 * P]
                    m = nc.tensor.transpose(dst, vp[:, c * C:c * C + P], ident[:, :])
                m.then_inc(t_tok, 1)
                fill(FILL[1])
                pe.wait_ge(tok_ev, i + 1)
                pe.wait_ge(ra_ok, i + 1)
                pe.wait_ge(bs_ev, i + 1)
                for c in range(NCH):
                    m = nc.tensor.matmul(W[c // 2][:, (c % 2) * 256:(c % 2) * 256 + 256],
                                         bk[:, c].rearrange("p x t -> p (x t)"),
                                         ra[:, c].rearrange("p h x t -> p (h x t)"), start=True, stop=True)
                m.then_inc(t_mm, 1)
                fill(FILL[2])
                pe.wait_ge(mm_ev, i + 1)
                pe.wait_ge(rst, i + 1)
                for h in range(2):
                    for c in range(NCH):
                        m = nc.tensor.matmul(W[3 * h][0:C, c * C:(c + 1) * C], mm[:, c, h, 1, :], inv[:, h, c, :],
                                             start=(c == 0), stop=(c == NCH - 1), skip_group_check=True)
                    m.then_inc(t_z, 1)
                nlev = 1
                for n, size in enumerate(LEVELS):
                    zb = lvl_bank[(n + 1) % 2]
                    for h in range(2):
                        fill(FILL[3 + h])
                        pe.wait_ge(inv_ok, 12 * i + 2 * n + h + 1)
                        for c in range(NCH):
                            m = nc.tensor.matmul(W[zb[h]][0:C, c * C:(c + 1) * C], mm[:, c, h, 1, :], inv[:, h, c, :],
                                                 start=(c == 0), stop=(c == NCH - 1), skip_group_check=True)
                        m.then_inc(t_z, 1)
                    if n == 0:
                        fill(FILL[12])
                    elif n == 1:
                        turn(i, 0)
                        fill(FILL[5])
                    else:
                        ada(i, 1, n - 2)
                    for h in range(2):
                        pe.wait_ge(z_cp, 10 * i + 2 * n + h + 1)
                        if h == 0 and n == 0:
                            pe.wait_ge(inv_ok, 12 * i + 2)
                        for a_, b_, bank in ((invt, zs, zb[2 + 2 * h]), (zs, invt, zb[3 + 2 * h])):
                            for c in range(NCH):
                                m = nc.tensor.matmul(W[bank][0:C, c * C:(c + 1) * C], a_[:, h, c, :], b_[:, h, c, :],
                                                     start=(c == 0), stop=(c == NCH - 1), skip_group_check=True)
                        m.then_inc(t_e, 1)
                zb = lvl_bank[1]
                for h in range(2):
                    fill(FILL[3 + h])
                    pe.wait_ge(inv_ok, 12 * i + 8 + h + 1)
                    for c in range(NCH):
                        m = nc.tensor.matmul(W[zb[h]][0:C, c * C:(c + 1) * C], mm[:, c, h, 1, :], inv[:, h, c, :],
                                             start=(c == 0), stop=(c == NCH - 1), skip_group_check=True)
                    m.then_inc(t_z, 1)
                turn(i, 1)
                for h in range(2):
                    pe.wait_ge(z_cp, 10 * i + 8 + h + 1)
                    for c in range(NCH):
                        m = nc.tensor.matmul(W[zb[2 + h]][0:C, c * C:(c + 1) * C], zs[:, h, c, :], invt[:, h, c, :],
                                             start=(c == 0), stop=(c == NCH - 1), skip_group_check=True)
                    m.then_inc(t_e, 1)
                fill(FILL[6])
                pe.wait_ge(inv_ok, 12 * i + 12)
                for b in range(NB):
                    for h in range(2):
                        m = nc.tensor.matmul(
                            W[0][C * h:C * h + C, 0:P].rearrange("p (x t) -> p x t", x=2)[:, :, 8 * b:8 * b + 8],
                            s0t[:, b, :], ra[:, 4, h, :, 8 * b:8 * b + 8],
                            start=(b == 0), stop=(b == NB - 1), skip_group_check=True)
                m.then_inc(t_sg, 1)
                for c in range(NCH):
                    fill(FILL[7])
                    if c >= 1:
                        pe.wait_ge(g_ev, NCH * i + c)
                    if 1 <= c <= 3:
                        pe.wait_ge(st_ok, 4 * i + c)
                    if c == 0:
                        pe.wait_ge(sg_ev, i + 1)
                    if c >= 1:
                        pe.wait_ge(y_ev, NCH * i + c)

                    def state_part(x_, bank, stop):
                        if c == 4:
                            nc.tensor.matmul(W[bank][0:C, 0:P], sgy[:, x_, :], ident[:, :], start=True, stop=False,
                                             skip_group_check=True)
                        elif c >= 1:
                            for h in range(2):
                                nc.tensor.matmul(W[bank][0:C, C * h:C * h + C], ra[:, c, h, x_, :], st[:, :],
                                                 start=(h == 0), stop=False, skip_group_check=True)

                    state_part(1, 0, False)
                    for h in range(2):
                        m = nc.tensor.matmul(W[0][0:C, C * h:C * h + C], mm[:, c, h, 1, :], uv[:, c, C * h:C * h + C],
                                             start=(c == 0 and h == 0), stop=(h == 1), skip_group_check=True)
                    m.then_inc(t_g, 1)
                    state_part(0, 3, False)
                    fill(FILL[8])
                    pe.wait_ge(g_ev, NCH * i + c + 1)
                    if c >= 1:
                        pe.wait_ge(u_ev, NCH * i + c)
                    for h in range(2):
                        m = nc.tensor.matmul(W[1][0:C, C * h:C * h + C], invt[:, h, c, :], gs_[:, C * h:C * h + C],
                                             start=(h == 0), stop=(h == 1), skip_group_check=True)
                    m.then_inc(t_u, 1)
                    fill(FILL[9])
                    pe.wait_ge(u_ev, NCH * i + c + 1)
                    if c < 4:
                        for h in range(2):
                            m = nc.tensor.matmul(W[2][C * h:C * h + C, 0:C], bkt[:, c, C * h:C * h + C],
                                                 uv[:, c, C * h:C * h + C], start=True, stop=True,
                                                 skip_group_check=True)
                        m.then_inc(t_st, 1)
                    for h in range(2):
                        m = nc.tensor.matmul(W[3][0:C, C * h:C * h + C], mm[:, c, h, 0, :], uv[:, c, C * h:C * h + C],
                                             start=(c == 0 and h == 0), stop=(h == 1), skip_group_check=True)
                    m.then_inc(t_y, 1)
                fill(FILL[10])
                pe.wait_ge(uvx_ok, i + 1)
                for h in range(2):
                    m = nc.tensor.matmul(W[0][C * h:C * h + C, :], bkt[:, 4, C * h:C * h + C],
                                         uvx[:, h].rearrange("p b i -> p (b i)"), start=True, stop=True,
                                         skip_group_check=True)
                m.then_inc(t_sf, 1)
                pe.wait_ge(y_ev, NCH * i + NCH)
                pe.sem_inc(past_pe, 1)
                for c in range(NCH):
                    m = nc.tensor.transpose(W[3][:, c * C:(c + 1) * C], ys[:, c, :], ident[0:C, 0:C])
                m.then_inc(t_yt, 1)
                fill(FILL[11])
                pe.wait_ge(st_ok, 4 * i + 4)
                pe.wait_ge(sf_ok, i + 1)
                pe.sem_inc(past_pe, 1)
                nc.tensor.transpose(W[2][0:C, 0:P], st[:, :], ident[:, :])
                for q in range(4):
                    m = nc.tensor.transpose(W[1][:, q * P:(q + 1) * P], sfin[:, 2 * q:2 * q + 2, :], ident[:, :])
                m.then_inc(t_so, 1)
                pe.wait_ge(yt_ev, i + 1)
                nc.tensor.matmul(W[0][:, 0:T], onesd[:, :], yw[:, :], start=True, stop=True).then_inc(t_mn, 1)
                fill(KT * 3)
                pe.wait_ge(yc_ok, i + 1)
                nc.tensor.matmul(W[3][:, 0:T], onesd[:, :], tb[:, :], start=True, stop=True).then_inc(t_vr, 1)

            pair(0, False)
            with pe.Fori(1, PAIRS - 1) as i:
                pair(i, False)
            pair(PAIRS - 1, True)
            pe.wait_ge(yc_ok, PAIRS)
            pe.wait_ge(so_ev, 2 * PAIRS)
            pe.wait_ge(a_red, 2 * PAIRS)
            pe.wait_ge(z_done, PAIRS)
            for j in range(27):
                n = min(P, SH - j * P)
                m = nc.tensor.transpose(PS[0:NC9, j // 4, (j % 4) * P:(j % 4) * P + n], zlast[0:n, j, :],
                                        ident[0:n, 0:n])
            m.then_inc(t_sh, 1)

        @block.scalar
        def _(act):
            act.wait_ge(k_zero, 1)
            for q in range(8):
                act.wait_ge(wu[q % 3], q // 3 + 1)
                act.wait_ge(ext_used, q)
                nc.scalar.copy(ext_prompt(ext), PS[:, q % 4, 0:NP_TOK])
                nc.scalar.copy(ext_sample(ext, 0, BUF), spT[:, q, :].rearrange("p (b l) -> p b l", l=BUF))
                nc.scalar.copy(ext_sample(ext), PS[:, q % 4, NP_TOK:T].rearrange("p (b l) -> p b l", l=NL)
                               ).then_inc(ext_ok, 1)
                act.wait_ge(t_pt, q)
                nc.scalar.copy(plast[:, :], PS[:, q % 4, T - P:T]).then_inc(pool_in, 1)
                act.wait_ge(pool_in, q + 1)
                act.sem_inc(pre_ev, 1)
                if q == 4:
                    nc.scalar.copy(ptok[:, :], W[2]).then_inc(ptok_ev, 1)
                if q in (3, 5, 7):
                    mix_out(act, q // 2 - 1)
            act.wait_ge(t_pt, 8)
            act.wait_ge(ptok_ok, 1)
            nc.scalar.copy(ptok[:, :], W[2]).then_inc(ptok_ev, 1)
            mix_out(act, 3)
            act.wait_ge(lzs_ok, 1)
            nc.scalar.activation(lwa[0:64, :], lwa[0:64, :], ACT.Tanh)
            act.wait_ge(lzs_ok, 3)
            nc.scalar.activation(lg1[:, :], lg1[:, :], ACT.Sigmoid)
            nc.scalar.activation(lg2[0:32, :], lg2[0:32, :], ACT.Sigmoid).then_inc(lora_ok, 1)

            def pair(i, last):
                for j in (1, 0, 2):
                    act.wait_ge(wu[j], UBASE[j] + 1 + i)
                    nc.scalar.copy(z3[:, j, 1:1 + NP_TOK], PS[:, j, 0:NP_TOK])
                    nc.scalar.copy(z3[:, j, 1 + NP_TOK:ZW].rearrange("p (b l) -> p b l", l=ZS)[:, :, 1:ZS],
                                   PS[:, j, NP_TOK:T].rearrange("p (b l) -> p b l", l=NL)).then_inc(z_ev, 1)
                act.wait_ge(t_s0, i + 1)
                w0 = W[0].rearrange("p (q h i) -> p q h i", q=4, h=2)
                s0 = s0t[:, :, :].rearrange("p (q b) i -> p q b i", b=2)
                for b in range(2):
                    for h in range(2):
                        m = nc.scalar.copy(s0[C * h:C * h + C, :, b, :], w0[C * b:C * b + C, :, h, :])
                m.then_inc(s0_ev, 1)
                act.wait_ge(pc_ok, i + 1)
                act.wait_ge(l_q, i + 1)
                nc.scalar.activation(sg[:, :], W[1][:, 0:T], ACT.Sigmoid, bias=pc[:, K_W0:K_W0 + 1]).then_inc(lev, 1)
                act.wait_ge(l_a, i + 1)
                nc.scalar.activation(aa[:, :], W[2][:, 0:T], ACT.Sigmoid, bias=pc[:, K_A0:K_A0 + 1]).then_inc(lev, 1)
                act.wait_ge(ssm_ok, i + 1)
                nc.scalar.activation(rn[:, :], rn[:, :], ACT.Ln).then_inc(ln_ev, 1)
                act.wait_ge(ln_ev, 2 * i + 1)
                nc.scalar.activation(rn[:, :], rn[:, :], ACT.Exp, scale=-0.5).then_inc(ss_ev, 1)
                act.wait_ge(cs_ok, i + 1)
                nc.scalar.activation(ilam[:, :], cs[:, :], ACT.Exp, scale=DECAY).then_inc(e_ok, 1)
                nc.scalar.activation(lam[:, :], cs[:, :], ACT.Exp, scale=-DECAY).then_inc(e_ok, 1)
                act.wait_ge(l_g, i + 1)
                earlier(act, fin, i)
                nc.scalar.copy(gg[:, :], W[3][:, 0:T]).then_inc(lev, 1)
                act.wait_ge(cse_ok, i + 1)
                nc.scalar.activation(lame[:, :], cse[:, :], ACT.Exp, scale=-DECAY).then_inc(e_ok, 1)
                act.wait_ge(t_tok, i + 1)
                nc.scalar.copy(bkt[:, 0:4, :].rearrange("p c j -> p (c j)"), W[2])
                nc.scalar.copy(bkt[:, 4, :], W[3][:, 0:P])
                nc.scalar.copy(uv[C:P, 0:4, :].rearrange("p c j -> p (c j)"), W[0][C:P, :])
                nc.scalar.copy(uv[C:P, 4, :], W[3][C:P, P:2 * P]).then_inc(tok_ev, 1)

                def z_copy(n, h, bank):
                    act.wait_ge(t_z, 12 * i + 2 + 2 * n + h + 1)
                    nc.scalar.copy(zs[0:C, h].rearrange("p c t -> p (c t)"), W[bank][0:C, 0:T]).then_inc(z_cp, 1)

                def a_copy(ch):
                    act.wait_ge(a_half, 4 * i + 2 * ch + 2)
                    if ch == 0:
                        earlier(act, a_turn, i, 2)
                    else:
                        act.wait_ge(a_turn, 2 * i + 1)
                    nc.scalar.copy(asum[:, :], PS[:, 3, :]).then_inc(a_cp, 1)

                for n in range(5):
                    if n >= 1:
                        act.wait_ge(t_e, 10 * i + 2 * n)
                    for h in range(2):
                        z_copy(n, h, lvl_bank[(n + 1) % 2][h])
                    if n in (0, 3):
                        a_copy(n // 3)
                act.wait_ge(t_sg, i + 1)
                nc.scalar.copy(sgy[:, :, :].rearrange("p x t -> p (x t)"), W[0][:, 0:P]).then_inc(sg_ev, 1)
                for c in range(NCH):
                    act.wait_ge(t_g, NCH * i + c + 1)
                    nc.scalar.copy(gs_[0:C, :], W[0][0:C, 0:P]).then_inc(g_ev, 1)
                    act.wait_ge(t_y, NCH * i + c + 1)
                    if c == 0:
                        earlier(act, t_yt, i)
                    nc.scalar.copy(ys[:, c, :], W[3][0:C, 0:P]).then_inc(y_ev, 1)
                act.wait_ge(t_yt, i + 1)
                nc.scalar.copy(yw[:, :], W[3][:, 0:T]).then_inc(yt_ev, 1)
                act.wait_ge(t_so, i + 1)
                earlier(act, out_w, i, 80)
                nc.scalar.copy(pout[:, :], W[2][0:C, 0:P]).then_inc(so_ev, 1)
                nc.scalar.copy(sout[:, :, :].rearrange("p b j -> p (b j)"), W[1]).then_inc(so_ev, 1)
                act.wait_ge(t_vr, i + 1)
                nc.scalar.activation(cse[:, :], W[3][:, 0:T], ACT.Ln, bias=eps[:, 1:2]).then_inc(ln_ev, 1)
                act.wait_ge(ln_ev, 2 * i + 2)
                nc.scalar.activation(cse[:, :], cse[:, :], ACT.Exp, scale=-0.5).then_inc(vr_ev, 1)

            pair(0, False)
            with act.Fori(1, PAIRS - 1) as i:
                pair(i, False)
            pair(PAIRS - 1, True)
            act.wait_ge(t_sh, 1)
            nc.scalar.copy(shrow[:, 0:27 * P], PS[0:NC9, 0:7, :].rearrange("p b n -> p (b n)")[:, 0:27 * P]
                           ).then_inc(sh_ev, 1)

        @block.vector
        def _(ve):
            o = Order(ve, v_own)
            modulate(nc, ve, o, hT, G["gs"], adaT[:, SH_A:SH_A + KT, :], done=h_ok)
            masks(ve, o)
            ve.wait_ge(k_zero, 1)
            for q in range(8):
                g, w = q // 2, WIN[q // 2]
                ve.wait_ge(ext_ok, q + 1)
                src = ext
                for n in range(g + 1):
                    dst, lo, d = (sa, sb_)[n % 2], 2 ** (n + 1) - 1, 2 ** n
                    o.did(nc.vector.tensor_tensor(dst[:, lo:EW], src[:, lo:EW], src[:, lo - d:EW - d], ALU.add))
                    o.settle()
                    src = dst
                if g >= 1:
                    ve.wait_ge(t_pool, g)
                o.did(nc.vector.tensor_tensor(pooled[:, q % 2, 0:NP_TOK], ext_prompt(src), rc[:, g, :], ALU.mult))
                o.settle()
                o.did(nc.vector.tensor_tensor(pooled[:, q % 2, 0:NP_TOK], pooled[:, q % 2, 0:NP_TOK], ext_prompt(ext),
                                              ALU.subtract))
                o.did(nc.vector.scalar_tensor_tensor(
                    out=pooled[:, q % 2, NP_TOK:T].rearrange("p (b l) -> p b l", l=NL), in0=ext_sample(src),
                    scalar=1.0 / w, in1=ext_sample(ext), op0=ALU.mult, op1=ALU.subtract))
                o.settle()
                ve.sem_inc(ext_used, 1)
                if q % 2:
                    ve.sem_inc(pooled_ok, 1)
            for r, (q, n, dst) in enumerate(((8, P, lwa), (9, P, lg1), (10, 32, lg2))):
                ve.wait_ge(wu[q % 3], q // 3 + 1)
                bank = PS[0:n, q % 4, :]
                cur = lz[0:n, 1 + NP_TOK:ZW].rearrange("p (b l) -> p b l", l=ZS)
                o.did(nc.vector.tensor_copy(lz[0:n, 1:1 + NP_TOK], bank[:, 0:NP_TOK]))
                o.did(nc.vector.tensor_copy(cur[:, :, 1:ZS], bank[:, NP_TOK:T].rearrange("p (b l) -> p b l", l=NL)))
                o.did(nc.vector.tensor_copy(cur[:, :, 0], sprevT[0:n, 24 + r, :]))
                o.did(nc.vector.tensor_copy(zlast[0:n, 24 + r, :], bank[:, NP_TOK - 1:T:NL]))
                o.settle()
                o.did(nc.vector.tensor_tensor(lzd[0:n, 0:NP_TOK], lz[0:n, 0:NP_TOK], lz[0:n, 1:1 + NP_TOK], ALU.subtract))
                o.did(nc.vector.tensor_tensor(lzd[0:n, NP_TOK:T].rearrange("p (b l) -> p b l", l=NL),
                                              cur[:, :, 0:NL], cur[:, :, 1:ZS], ALU.subtract))
                o.settle()
                o.did(nc.vector.scalar_tensor_tensor(out=dst[0:n, :], in0=lzd[0:n, :],
                                                     scalar=PT[0:n, R_MUT + r:R_MUT + r + 1], in1=bank[:, 0:T],
                                                     op0=ALU.mult, op1=ALU.add))
                o.settle()
                ve.sem_inc(pre_ev, 1)
                ve.sem_inc(lzs_ok, 1)
            base = o.n

            def pair(i, last):
                o = Order(ve, v_own, base + i * N_DVE)
                o.did(nc.vector.tensor_copy(pc[:, :].unsqueeze(2), PT[:, 0:80].rearrange("p (k q) -> p k q", q=8)[:, :, at(i)]))

                def first(j):
                    ve.wait_ge(wu[j], UBASE[j] + 1 + i)
                    zc = z3[:, j, 1 + NP_TOK:ZW].rearrange("p (b l) -> p b l", l=ZS)
                    o.did(nc.vector.tensor_copy(zc[:, :, 0].unsqueeze(1), sprevT[:, at(i + 8 * j), :]))

                def differ(js):
                    o.did(nc.vector.tensor_tensor(zd[:, js, 0:NP_TOK], z3[:, js, 0:NP_TOK], z3[:, js, 1:1 + NP_TOK],
                                                  ALU.subtract))
                    zc = z3[:, js, 1 + NP_TOK:ZW].rearrange("p j (b l) -> p j b l", l=ZS)
                    o.did(nc.vector.tensor_tensor(zd[:, js, NP_TOK:T].rearrange("p j (b l) -> p j b l", l=NL),
                                                  zc[:, :, :, 0:NL], zc[:, :, :, 1:ZS], ALU.subtract))
                    o.settle()

                def shifted(j, dst):
                    o.did(nc.vector.scalar_tensor_tensor(out=dst, in0=zd[:, j, :], scalar=pc[:, K_MU + j:K_MU + j + 1],
                                                         in1=PS[:, j, 0:T], op0=ALU.mult, op1=ALU.add))

                first(1)
                o.settle()
                nc.vector.tensor_scalar(pomk[:, :], pc[:, K_KA:K_KA + 1], -1.0, 1.0, ALU.mult, ALU.add).then_inc(pc_ok, 1)
                ve.wait_ge(z_ev, 3 * i + 1)
                differ(slice(1, 2))
                shifted(1, zk[:, :])
                o.settle()
                o.did(nc.vector.tensor_scalar(kk[:, :], zk[:, :], pc[:, K_KK:K_KK + 1], None, ALU.mult))
                o.settle()
                nc.vector.tensor_tensor(tb[:, :], kk[:, :], kk[:, :], ALU.mult).then_inc(sq_ok, 1)
                first(0)
                first(2)
                ve.wait_ge(z_ev, 3 * i + 3)
                o.settle()
                differ(slice(0, 3, 2))
                shifted(0, zr[:, :])
                shifted(2, vp[:, C:C + T])
                for j in range(3):
                    o.did(nc.vector.tensor_copy(zlast[:, at(i + 8 * j), :], z3[:, j, NP_TOK:ZW:ZS].unsqueeze(1)))
                o.settle()
                ve.sem_inc(z_done, 1)
                ve.wait_ge(lev, 3 * i + 1)
                nc.vector.tensor_tensor_scan(cs[:, :], rmask[:, :], sg[:, :], 0.0, ALU.mult, ALU.add).then_inc(cs_ok, 1)
                ve.wait_ge(t_ss, i + 1)
                nc.vector.tensor_scalar(rn[:, :], W[0][:, 0:T], 1e-24, None, ALU.max).then_inc(ssm_ok, 1)
                if not isinstance(i, int) or i:
                    norm(i - 1)
                ve.wait_ge(k2_ok, i + 1)
                nc.vector.scalar_tensor_tensor(out=rk[:, :], in0=zr[:, :], scalar=pc[:, K_RK:K_RK + 1], in1=k2[:, :],
                                               op0=ALU.mult, op1=ALU.mult).then_inc(rk_ok, 1)
                ve.wait_ge(ss_ev, i + 1)
                o.did(nc.vector.tensor_tensor(kk[:, :], kk[:, :], rn[:, :], ALU.mult))
                o.settle()
                o.did(nc.vector.tensor_tensor(tb[:, :], kk[:, :], aa[:, :], ALU.mult))
                o.settle()
                ve.wait_ge(e_ok, 3 * i + 3)
                cut = lambda x_: x_.rearrange("p (c t) -> p c t", t=C)
                o.did(nc.vector.tensor_tensor(bk[:, :, 0, :], cut(tb[:, :]), cut(ilam[:, :]), ALU.mult))
                nc.vector.tensor_tensor(bk[:, :, 1, :], cut(k2[:, :]), cut(ilam[:, :]), ALU.mult).then_inc(bk_ok, 1)
                for h in range(2):
                    r_ = slice(C * h, C * h + C)
                    o.did(nc.vector.tensor_tensor(ra[r_, :, h, 0, :], cut(zr[r_, :]), cut(lam[r_, :]), ALU.mult))
                    m = nc.vector.scalar_tensor_tensor(out=ra[r_, :, h, 1, :], in0=cut(kk[r_, :]), scalar=-1.0,
                                                       in1=cut(lame[r_, :]), op0=ALU.mult, op1=ALU.mult)
                    if h == 0:
                        o.did(m)
                m.then_inc(ra_ok, 1)
                ve.wait_ge(t_bs, i + 1)
                nc.vector.tensor_tensor(bv[:, :], W[1][:, 0:T], vp[:, C:C + T], ALU.mult).then_inc(bs_ev, 1)
                ve.wait_ge(t_mm, i + 1)
                for b, mask, n in ((0, mask_p, 2), (1, mask_p, 2), (2, mask_s, 1)):
                    o.did(nc.vector.tensor_tensor(
                        mm[:, 2 * b:2 * b + n].rearrange("p c h x t -> p (c h) (x t)"),
                        W[b][:, 0:256 * n].rearrange("p (g n) -> p g n", n=P),
                        mask[:, :].unsqueeze(1).broadcast_to([P, 2 * n, P]), ALU.mult))
                o.settle()
                ve.sem_inc(mm_ev, 1)
                ve.wait_ge(rst, i + 1)

                def put(dst, mask, src):
                    nc_ = mask.unsqueeze(1).broadcast_to([C, NCH, C])
                    return o.did(nc.vector.copy_predicated(dst, nc_, src))

                for h in range(2):
                    ve.wait_ge(t_z, 12 * i + h + 1)
                    ve.sem_inc(past_ve, 1)
                    put(inv[0:C, h], lvl_n[:, 0, :], cut(W[3 * h][0:C, 0:T]))
                    put(invt[0:C, h], lvl_t[:, 0, :], mm[0:C, :, h, 1, :])
                    o.settle()
                    ve.sem_inc(inv_ok, 1)
                for n in range(4):
                    zb = lvl_bank[(n + 1) % 2]
                    for h in range(2):
                        ve.wait_ge(t_e, 10 * i + 2 * n + h + 1)
                        ve.sem_inc(past_ve, 1)
                        put(inv[0:C, h], lvl_n[:, n + 1, :], cut(W[zb[2 + 2 * h]][0:C, 0:T]))
                        put(invt[0:C, h], lvl_t[:, n + 1, :], cut(W[zb[3 + 2 * h]][0:C, 0:T]))
                        o.settle()
                        ve.sem_inc(inv_ok, 1)
                    if n == 1:
                        ada_store(i, 0, o, last)
                for h in range(2):
                    ve.wait_ge(t_e, 10 * i + 8 + h + 1)
                    ve.sem_inc(past_ve, 1)
                    put(invt[0:C, h], lvl_t[:, 5, :], cut(W[lvl_bank[1][2 + h]][0:C, 0:T]))
                    o.settle()
                    ve.sem_inc(inv_ok, 1)
                ada_store(i, 1, o, last)
                for c in range(NCH):
                    ve.wait_ge(t_u, NCH * i + c + 1)
                    nc.vector.tensor_copy(uv[0:C, c, :], W[1][0:C, 0:P]).then_inc(u_ev, 1)
                    if c < 4:
                        ve.wait_ge(t_st, 4 * i + c + 1)
                        end = lam[:, C * c + C - 1:C * c + C]
                        if c == 0:
                            nc.vector.tensor_scalar(st[:, :], W[2][:, 0:C], end, None, ALU.mult).then_inc(st_ok, 1)
                        else:
                            nc.vector.scalar_tensor_tensor(out=st[:, :], in0=W[2][:, 0:C], scalar=end, in1=stl[:, :],
                                                           op0=ALU.mult, op1=ALU.add).then_inc(st_ok, 1)
                        if c < 3:
                            ve.wait_ge(st_ok, 4 * i + c + 1)
                            o.did(nc.vector.tensor_scalar(stl[:, :], st[:, :], lam[:, C * c + 2 * C - 1:C * c + 2 * C],
                                                          None, ALU.mult))
                            o.settle()
                ve.wait_ge(t_sf, i + 1)
                earlier(ve, so_ev, i, 2)
                o.did(nc.vector.tensor_tensor(sfin[:, :, :], W[0].rearrange("p (b j) -> p b j", j=C), s0t[:, :, :], ALU.add))
                o.settle()
                nc.vector.tensor_tensor(sfin[:, :, :], sfin[:, :, :],
                                        lam[:, NP_TOK + NL - 1:T:NL].unsqueeze(2).broadcast_to([P, NB, C]), ALU.mult
                                        ).then_inc(sf_ok, 1)
                ve.wait_ge(t_mn, i + 1)
                o.did(nc.vector.tensor_tensor(yw[:, :], yw[:, :], W[0][:, 0:T], ALU.subtract))
                o.settle()
                nc.vector.tensor_tensor(tb[:, :], yw[:, :], yw[:, :], ALU.mult).then_inc(yc_ok, 1)
                assert o.n == N_DVE, o.n

            def norm(i):
                o = Order(ve, n_own, 3 * i)
                ve.wait_ge(vr_ev, i + 1)
                o.did(nc.vector.tensor_tensor(yw[:, :], yw[:, :], cse[:, :], ALU.mult))
                o.settle()
                o.did(nc.vector.tensor_scalar(yw[:, :], yw[:, :], PT[:, at(8 * K_LW + i)], PT[:, at(8 * K_LB + i)],
                                              ALU.mult, ALU.add))
                o.settle()
                o.did(nc.vector.tensor_tensor(yw[:, :], yw[:, :], bv[:, :], ALU.add))
                o.settle()
                nc.vector.tensor_tensor(catT[:, at(i + 8), :], yw[:, :].unsqueeze(1), gg[:, :].unsqueeze(1), ALU.mult
                                        ).then_inc(fin, 1)

            def ada_store(i, ch, o, last):
                ve.wait_ge(a_turn, 2 * i + ch + 1)
                o.did(nc.vector.tensor_reduce(a4[:, :, :], ada_parts(PS[:, 3, :]), AX.X, ALU.add))
                o.settle()
                ve.sem_inc(a_red, 1)
                rows = at(32 + 4 * (2 * i + ch), 4)
                o.did(nc.vector.tensor_tensor(adaT[:, rows, :], a4[:, :, :],
                                              bT[:, rows].unsqueeze(2).broadcast_to([P, 4, NC9]), ALU.add))

            pair(0, False)
            with ve.Fori(1, PAIRS - 1) as i:
                pair(i, False)
            pair(PAIRS - 1, True)
            norm(PAIRS - 1)



def phase_mix(nc, A, O, sb, sem, G):
    PS, ident, eps, PT, adaT, catT, ring, wo, w_out, s_wo, past_pe, past_pool, ld_w = (
        G[k] for k in "PS ident eps PT adaT catT ring wo w_out s_wo past_pe past_pool ld_w".split())
    x2 = sb("x2", [P, 3, D])
    h2 = sb("h2", [P, 3, D])
    chosen, scores, sel, wts, dest = (sb(n, [P, 3, NE]) for n in "chosen scores sel wts dest".split())
    d01 = sb("d01", [P, 2, 3])
    w01 = sb("w01", [P, 2, 3])
    bei = sb("bei", [1, 64], I32)
    slotf, slotw = sb("slotf", [P, SLOT]), sb("slotw", [P, SLOT])
    pick = sb("pick", [P, 3, SLOT])
    pick2 = sb("pick2", [P, 3, SLOT])
    ss4 = sb("ss4", [P, 3, 4])
    ssq = sb("ssq", [P, 8])
    cat = catT[:, :, :].rearrange("p k t -> p (k t)")
    gtm = cat[:, 0:2 * D].rearrange("p (v n) -> p v n", v=2)
    ysb = cat[:, 2 * D:2 * D + 1024].rearrange("p (q n) -> p q n", q=2)
    (s_x, s_br, s_rt, o_own, p_own, t_mix, u_wo, gated, t_back, x2_ok, ss_ok, sd_ok, xn_ok, t_h, h_ev, hm_ok, t_rt,
     rt_ev, t_lg, lg_ok, sc_ok, t_hb, hb_ev, ch_ok, t_pos, be_ok, k_own, a_own, s_fg, s_fin, y_out, t_gt, gt_ev,
     t_gm, gm_ev, gm_ev2, rz, gs_ok) = (
        sem("m_" + n) for n in ("s_x s_br s_rt o_own p_own t_mix u_wo gated t_back x2_ok ss_ok sd_ok xn_ok t_h h_ev "
                                "hm_ok t_rt rt_ev t_lg lg_ok sc_ok t_hb hb_ev ch_ok t_pos be_ok k_own a_own s_fg "
                                "s_fin y_out t_gt gt_ev t_gm gm_ev gm_ev2 rz gs_ok").split())
    (pick_ok, t_pk, xs_ev, t_xt, xt_ev, act_ev, up_ev, gu_ok, t_at, at_ev, dn_ev, pw_ok, t_pw, pw_ev, t_sc, sc_ev,
     x_ok, p2, pz, w_own, sq_ok, f_own, fin_own) = (
        sem("e_" + n) for n in ("pick_ok t_pk xs_ev t_xt xt_ev act_ev up_ev gu_ok t_at at_ev dn_ev pw_ok t_pw pw_ev "
                                "t_sc sc_ev x_ok p2 pz w_own sq_ok f_own fin_own").split())
    ld_e = [sem(f"ld_e{j}") for j in range(6)]
    used = [sem(f"used{j}") for j in range(6)]
    w_gate = A["w_gate"][0].rearrange("e (q k p) n -> e q p k n", q=4, p=P)
    w_up = A["w_up"][0].rearrange("e (q k p) n -> e q p k n", q=4, p=P)
    w_down = A["w_down"][0].rearrange("e (q k p) n -> e q p k n", q=4, p=P)

    def load_unit(eng, e, u):
        src = (w_gate, w_up)[u % 2][at(e), u // 2] if u < 8 else w_down[at(e), u - 8]
        src = src.rearrange("e p k n -> p (e k) n")
        eng.dma_start(unit(u, src.shape[2]), src).then_inc(ld_e[u % 6], 16)

    def unit(u, n):
        return ring[:, (u % 6) * UNIT:(u % 6 + 1) * UNIT].rearrange("p (k n) -> p k n", n=n)

    mixing = ExitStack()
    G["ctx"].enter_context(mixing)
    mt = lambda name, shape, dt=F32: sb(name, shape, dt, scope=mixing)
    mg = mt("mg", [P, KT, T])
    gated_tile = mt("gated_tile", [P, 4, T])
    rlg = gated_tile[:, 0, :]
    gtr = mg[:, :, :].rearrange("p k t -> p (k t)")[:, 0:D]
    hot = mt("hot", [P, 2, P])
    gs2 = mt("gs2", [P, KT, NC9])
    wrt = mt("wrt", [P, KT, 32])
    r4 = mt("r4", [P, 8, 12])
    rank = mt("rank", [P, 12, EPG])
    cmp_ = mt("cmp", [P, 12, EPG])
    small = mt("small", [P, 16, 3])
    nb = mt("nb", [P, 4, NE])
    browt = mt("browt", [P, NE])
    be = mt("be", [1, 32, NE])
    bef = mt("bef", [1, 32])
    bnum = mt("bnum", [1, 32])
    bnum_i = mt("bnum_i", [1, 32], I32)
    slot_i = mt("slot_i", [P, SLOT], I32)
    tri = mt("tri", [P, P])
    ones = mt("ones", [P, P])
    logit = mt("logit", [P, 3, NE])
    GB = (7, 0, 1, 2, 3)
    with nc.Block() as block:

        @block.sync
        def _(sp):
            for i, (t0, n) in enumerate(TILES):
                src = A["x_prompt"][0, t0:t0 + n] if i < 2 else A["x_sample"].rearrange("b l d -> (b l) d")
                sp.dma_start(x2[0:n, i, :], src).then_inc(s_x, 16)
            sp.dma_start(browt[:, :], A["b_router"].partition_broadcast(P)).then_inc(s_br, 16)
            sp.wait_ge(rz, 1)
            sp.dma_start(wrt[:, :, 0:NE], A["w_router"].rearrange("(k p) e -> p k e", p=P)).then_inc(s_rt, 16)
            sp.wait_ge(G["shift_out"], 32)
            load_unit(sp, 0, 0)
            for g in range(1, 4):
                for j in range(4):
                    sp.wait_ge(u_wo, 4 * g - 3 + j)
                    sp.dma_start(wo[:, j], w_out[:, :, g * 512 + j * P:g * 512 + (j + 1) * P]).then_inc(s_wo[j], 16)
                load_unit(sp, 0, g)
            for u in (4, 5):
                sp.wait_ge(u_wo, 2 * u + 6)
                load_unit(sp, 0, u)

        @block.gpsimd
        def _(pool):
            n_ = [0]

            def own(ins):
                n_[0] += 1
                ins.then_inc(k_own, 1)
                pool.wait_ge(k_own, n_[0])

            own(nc.gpsimd.memset(wrt[:, :, :], 0.0))
            pool.sem_inc(rz, 1)
            own(nc.gpsimd.memset(gtr[:, :], 0.0))
            own(nc.gpsimd.memset(ones[:, :], 1.0))
            own(nc.gpsimd.memset(ss4[:, :, :], 0.0))
            own(nc.gpsimd.memset(scores[:, :, :], 0.0))
            own(nc.gpsimd.memset(h2[C:P, 2, :], 0.0))
            pool.sem_inc(p_own, 1)
            own(nc.gpsimd.affine_select(out=tri[:, :], in_=ones[:, :], compare_op=ALU.is_gt, fill=0.0, base=0,
                                        pattern=[[1, P]], channel_multiplier=-1))
            own(nc.gpsimd.iota(slot_i[:, :], pattern=[[1, SLOT]], base=0, channel_multiplier=0))
            own(nc.gpsimd.iota(bnum_i[:, :], pattern=[[1, 32]], base=0, channel_multiplier=0))
            own(nc.gpsimd.tensor_copy(slotf[:, :], slot_i[:, :]))
            own(nc.gpsimd.tensor_copy(slotw[:, :], slot_i[:, :]))
            own(nc.gpsimd.tensor_copy(bnum[:, :], bnum_i[:, :]))
            own(nc.gpsimd.memset(hot[:, :, :], 0.0))
            own(nc.gpsimd.memset(hot[0:1, 0, :], 1.0))
            own(nc.gpsimd.affine_select(out=hot[:, 1, 0:C], in_=ones[:, 0:C], compare_op=ALU.is_ge, fill=0.0, base=8,
                                        pattern=[[1, C]], channel_multiplier=-8))
            own(nc.gpsimd.affine_select(out=hot[:, 1, 0:C], in_=hot[:, 1, 0:C], compare_op=ALU.is_ge, fill=0.0, base=-1,
                                        pattern=[[-1, C]], channel_multiplier=8))
            pool.sem_inc(p_own, 1)

        @block.tensor
        def _(pe):
            def product(g, j):
                pe.wait_ge(s_wo[j], 16 * g + 16)
                if not isinstance(g, int):
                    pe.wait_ge(gated, 4 * g - 3 + j)
                for k in range(KT):
                    m = nc.tensor.matmul(PS[:, j, 0:T], wo[:, j, k, :], catT[:, k, :], start=(k == 0),
                                         stop=(k == KT - 1))
                m.then_inc(u_wo, 1)

            def back(g):
                pe.wait_ge(gated, 4 * g + 4)
                pe.wait_ge(x2_ok, g + 1)
                for j in range(4):
                    for i, (t0, n) in enumerate(TILES):
                        m = nc.tensor.transpose(PS[0:n, 4 + i, j * P:(j + 1) * P], gated_tile[:, j, t0:t0 + n],
                                                ident[:, :])
                m.then_inc(t_back, 1)

            for k in range(KT):
                m = nc.tensor.transpose(PS[0:NC9, 4 + k // 4, (k % 4) * P:(k % 4 + 1) * P], adaT[:, GT_M + k, :],
                                        ident[:, :])
            m.then_inc(t_gt, 1)
            for j in range(4):
                product(0, j)
            pe.wait_ge(gt_ev, 1)
            with pe.Fori(1, 4) as g:
                product(g, 0)
                back(g - 1)
                for j in range(1, 4):
                    product(g, j)
            back(3)
            pe.wait_ge(p_own, 2)
            for q in range(8):
                if q >= 5:
                    pe.wait_ge((gm_ev, gm_ev2)[(q - 5) % 2], (q - 5) // 2 + 1)
                nc.tensor.matmul(PS[:, GB[q % 5], :], hot[:, q // 4, :], gtr[:, 512 * (q % 4):512 * (q % 4) + 512],
                                 start=True, stop=True).then_inc(t_gm, 1)
            pe.wait_ge(xn_ok, 3)
            for k in range(KT):
                if k < 4:
                    pe.wait_ge((gm_ev, gm_ev2, gm_ev2, gm_ev)[k], 4)
                if k >= 8:
                    pe.wait_ge(h_ev, k - 7)
                for i, (t0, n) in enumerate(TILES):
                    m = nc.tensor.transpose(PS[:, k % 8, t0:t0 + n], h2[0:n, i, k * P:(k + 1) * P], ident[0:n, 0:n])
                m.then_inc(t_h, 1)
            pe.wait_ge(s_rt, 16)
            pe.wait_ge(h_ev, 9)
            for k in range(KT):
                if k % 4 == 0:
                    pe.wait_ge(hm_ok, k // 4 + 1)
                g = k % 4
                m = nc.tensor.matmul(PS[32 * g:32 * g + 32, 0, 0:T], wrt[:, k, :], mg[:, k, :], start=(k < 4),
                                     stop=(k >= KT - 4), skip_group_check=True)
            m.then_inc(t_rt, 1)
            pe.wait_ge(rt_ev, 1)
            for i, (t0, n) in enumerate(TILES):
                m = nc.tensor.transpose(PS[0:n, 7, i * P:(i + 1) * P], rlg[:, t0:t0 + n], ident[:, :])
            m.then_inc(t_lg, 1)
            for q in range(12):
                i, (t0, n), c = q % 3, TILES[q % 3], q // 3
                if q >= 6:
                    pe.wait_ge(hb_ev, q - 5)
                for j in range(4):
                    m = nc.tensor.transpose(PS[0:n, 1 + q % 6, j * P:(j + 1) * P], mg[:, 4 * c + j, t0:t0 + n],
                                            ident[:, :])
                m.then_inc(t_hb, 1)
            pe.wait_ge(p_own, 2)
            pe.wait_ge(ch_ok, 1)
            for i in range(3):
                for i2 in range(i + 1):
                    nc.tensor.matmul(PS[:, 7, i * NE:(i + 1) * NE], tri[:, :] if i2 == i else ones[:, :],
                                     chosen[:, i2, :], start=(i2 == 0), stop=(i2 == i))
            for i in range(3):
                m = nc.tensor.matmul(PS[:, 7, 48:64], ones[:, :], chosen[:, i, :], start=(i == 0), stop=(i == 2))
            m.then_inc(t_pos, 1)
        @block.scalar
        def _(act):
            act.wait_ge(t_gt, 1)
            act.wait_ge(p_own, 1)
            nc.scalar.copy(gtr[0:NC9, :], PS[0:NC9, 4:8, :].rearrange("p c n -> p (c n)")).then_inc(gt_ev, 1)
            for g in range(4):
                act.wait_ge(x2_ok, g + 2)
                for i, (t0, n) in enumerate(TILES):
                    m = nc.scalar.activation(h2[0:n, i, 512 * g:512 * g + 512], x2[0:n, i, 512 * g:512 * g + 512],
                                             ACT.Square, accum_out=ss4[0:n, i, g:g + 1])
                m.then_inc(ss_ok, 1)

            def gates(q):
                act.wait_ge(t_gm, q + 1)
                nc.scalar.copy(gtm[:, q // 4, 512 * (q % 4):512 * (q % 4) + 512], PS[:, GB[q % 5], :]).then_inc(gm_ev, 1)

            for q in (0, 2, 4):
                gates(q)
            act.wait_ge(sd_ok, 1)
            nc.scalar.activation(ssq[:, 4:7], ssq[:, 0:3], ACT.Sqrt, bias=eps[:, 0:1], scale=1.0 / D).then_inc(ss_ok, 1)
            gates(6)
            act.wait_ge(sd_ok, 2)
            nc.scalar.activation(h2[:, 1, :], x2[:, 1, :], ACT.Copy, scale=ssq[:, 5:6]).then_inc(xn_ok, 1)
            act.wait_ge(gs_ok, 1)
            for k in range(KT):
                act.wait_ge(t_h, k + 1)
                nc.scalar.activation(mg[:, k, 0:NP_TOK], PS[:, k % 8, 0:NP_TOK], ACT.Identity, scale=gs2[:, k, 0:1],
                                     bias=adaT[:, SH_M + k, 0:1])
                nc.scalar.copy(mg[:, k, NP_TOK:T], PS[:, k % 8, NP_TOK:T]).then_inc(h_ev, 1)
            act.wait_ge(t_rt, 1)
            nc.scalar.copy(rlg, PS[:, 0, 0:T]).then_inc(rt_ev, 1)
            act.wait_ge(lg_ok, 1)
            for i, (t0, n) in enumerate(TILES):
                m = nc.scalar.activation(scores[0:n, i, :], logit[0:n, i, :], ACT.Sigmoid)
            m.then_inc(sc_ok, 1)
            for q in range(12):
                i, (t0, n), c = q % 3, TILES[q % 3], q // 3
                act.wait_ge(t_hb, q + 1)
                nc.scalar.copy(h2[0:n, i, 512 * c:512 * c + 512], PS[0:n, 1 + q % 6, :]).then_inc(hb_ev, 1)

        @block.vector
        def _(ve):
            o = Order(ve, o_own)
            tt, ts = nc.vector.tensor_tensor, nc.vector.tensor_scalar

            def step(ins):
                o.did(ins)
                o.settle()

            def gate(g):
                for j in range(4):
                    ve.wait_ge(u_wo, 4 * g + j + 1)
                    nc.vector.tensor_scalar(gated_tile[:, j, 0:NP_TOK], PS[:, j, 0:NP_TOK],
                                            adaT[:, at(GT_A + 4 * g + j), 0:1].rearrange("p a b -> p (a b)"),
                                            None, ALU.mult)
                    nc.vector.tensor_tensor(
                        gated_tile[:, j, NP_TOK:T].rearrange("p (b l) -> p b l", l=NL),
                        PS[:, j, NP_TOK:T].rearrange("p (b l) -> p b l", l=NL),
                        adaT[:, at(GT_A + 4 * g + j), 1:NC9].rearrange("p a b -> p (a b)").unsqueeze(2)
                        .broadcast_to([P, NB, NL]), ALU.mult).then_inc(gated, 1)

            def add(g):
                ve.wait_ge(t_back, g + 1)
                for i, (t0, n) in enumerate(TILES):
                    xs = x2[0:n, i, at(g * 512, 512)]
                    m = nc.vector.tensor_tensor(xs, xs, PS[0:n, 4 + i, :], ALU.add)
                m.then_inc(x2_ok, 1)

            ve.wait_ge(s_x, 48)
            ve.sem_inc(x2_ok, 1)
            gate(0)
            with ve.Fori(1, 4) as g:
                add(g - 1)
                gate(g)
            add(3)
            step(ts(gs2[:, :, :], adaT[:, SC_M:SC_M + KT, :], 1.0, None, ALU.add))
            step(tt(gs2[:, :, :], gs2[:, :, :], PT[:, R_G2:R_G2 + KT].unsqueeze(2).broadcast_to([P, KT, NC9]), ALU.mult))
            ve.sem_inc(gs_ok, 1)
            for q in range(1, 8, 2):
                ve.wait_ge(t_gm, q + 1)
                nc.vector.tensor_copy(gtm[:, q // 4, 512 * (q % 4):512 * (q % 4) + 512], PS[:, GB[q % 5], :]
                                      ).then_inc(gm_ev2, 1)
            ve.wait_ge(p_own, 1)
            ve.wait_ge(ss_ok, 4)
            nc.vector.tensor_reduce(ssq[:, 0:3], ss4[:, :, :], AX.X, ALU.add).then_inc(sd_ok, 1)
            ve.wait_ge(ss_ok, 5)
            nc.vector.reciprocal(ssq[:, 4:7], ssq[:, 4:7]).then_inc(sd_ok, 1)
            ve.wait_ge(sd_ok, 2)
            for i in (0, 2):
                n = TILES[i][1]
                ts(h2[0:n, i, :], x2[0:n, i, :], ssq[0:n, 4 + i:5 + i], None, ALU.mult).then_inc(xn_ok, 1)
            modulate(nc, ve, o, mg, gs2, adaT[:, SH_M:SH_M + KT, :], h_ev, hm_ok)
            ve.wait_ge(t_lg, 1)
            for i0, i1, n in ((0, 2, P), (2, 3, C)):
                m = nc.vector.tensor_reduce(
                    logit[0:n, i0:i1, :], PS[0:n, 7, i0 * P:i1 * P].rearrange("p (i g e) -> p i e g", g=4, e=32)
                    [:, :, 0:NE, :], AX.X, ALU.add)
            m.then_inc(lg_ok, 1)
            ve.wait_ge(sc_ok, 1)
            ve.wait_ge(s_br, 16)
            step(tt(sel[:, :, :], scores[:, :, :], browt[:, :].unsqueeze(1).broadcast_to([P, 3, NE]), ALU.add))
            s4 = sel[:, :, :].rearrange("p i (g e) -> p (i g) e", e=EPG)
            for n, (a, b, op) in enumerate(((0, 1, ALU.max), (0, 1, ALU.min), (2, 3, ALU.max), (2, 3, ALU.min))):
                o.did(tt(r4[:, n, :], s4[:, :, a], s4[:, :, b], op))
            o.did(nc.vector.memset(rank[:, :, :], 0.0))
            o.did(nc.vector.memset(small[:, 1, :], 1.0))
            o.settle()
            o.did(tt(r4[:, 4, :], r4[:, 0, :], r4[:, 2, :], ALU.max))
            o.did(tt(r4[:, 5, :], r4[:, 0, :], r4[:, 2, :], ALU.min))
            o.did(tt(r4[:, 6, :], r4[:, 1, :], r4[:, 3, :], ALU.max))
            o.settle()
            step(tt(r4[:, 5, :], r4[:, 5, :], r4[:, 6, :], ALU.max))
            step(tt(r4[:, 4, :], r4[:, 4, :], r4[:, 5, :], ALU.add))
            gsc = r4[:, 4, :].rearrange("p (i g) -> p i g", g=NG)
            step(nc.vector.tensor_reduce(small[:, 0, :], gsc, AX.X, ALU.max))
            eq = r4[:, 5, :].rearrange("p (i g) -> p i g", g=NG)
            step(tt(eq, gsc, small[:, 0, :].unsqueeze(2).broadcast_to([P, 3, NG]), ALU.is_equal))
            for g in range(NG):
                step(tt(eq[:, :, g], eq[:, :, g], small[:, 1, :], ALU.mult))
                step(tt(small[:, 1, :], small[:, 1, :], eq[:, :, g], ALU.subtract))
            for j in range(EPG):
                for lo, hi, op in ((0, j, ALU.is_gt), (j + 1, EPG, ALU.is_ge)):
                    if lo < hi:
                        o.did(tt(cmp_[:, :, lo:hi], s4[:, :, j:j + 1].broadcast_to([P, 12, hi - lo]), s4[:, :, lo:hi], op))
                o.settle()
                for lo, hi in ((0, j), (j + 1, EPG)):
                    if lo < hi:
                        o.did(tt(rank[:, :, lo:hi], rank[:, :, lo:hi], cmp_[:, :, lo:hi], ALU.add))
                o.settle()
            step(ts(rank[:, :, :], rank[:, :, :], 2.0, None, ALU.is_lt))
            c4 = chosen[:, :, :].rearrange("p i (g e) -> p (i g) e", e=EPG)
            step(tt(c4, rank[:, :, :], r4[:, 5, :].unsqueeze(2).broadcast_to([P, 12, EPG]), ALU.mult))
            step(nc.vector.memset(chosen[C:P, 2, :], 0.0))
            ve.sem_inc(ch_ok, 1)
            o.did(tt(wts[:, :, :], scores[:, :, :], chosen[:, :, :], ALU.mult))
            o.did(nc.vector.memset(nb[:, 0, :], 0.0))
            o.did(nc.vector.memset(nb[:, 3, :], 1.0))
            o.settle()
            step(nc.vector.tensor_reduce(small[:, 2, :], wts[:, :, :], AX.X, ALU.add))
            step(ts(small[:, 2, :], small[:, 2, :], 1e-37, None, ALU.max))
            step(nc.vector.reciprocal(small[:, 2, :], small[:, 2, :]))
            step(tt(wts[:, :, :], wts[:, :, :], small[:, 2, :].unsqueeze(2).broadcast_to([P, 3, NE]), ALU.mult))
            ve.wait_ge(t_pos, 1)
            ve.wait_ge(p_own, 2)
            for k in range(T // SLOT):
                step(nc.vector.scalar_tensor_tensor(out=nb[:, 0, :], in0=PS[:, 7, 48:64], scalar=float(k * SLOT),
                                                    in1=nb[:, 0, :], op0=ALU.is_gt, op1=ALU.add))
            step(ts(nb[:, 0, :], nb[:, 0, :], 1.0, None, ALU.max))
            step(nc.vector.tensor_tensor_scan(nb[:, 1, :], nb[:, 3, :], nb[:, 0, :], 0.0, ALU.mult, ALU.add))
            o.did(tt(nb[:, 2, :], nb[:, 1, :], nb[:, 0, :], ALU.subtract))
            o.did(tt(be[:, :, :], nb[0:1, 1, :].unsqueeze(1).broadcast_to([1, 32, NE]),
                     bnum[:, :].unsqueeze(2).broadcast_to([1, 32, NE]), ALU.is_le))
            o.settle()
            o.did(ts(nb[:, 2, :], nb[:, 2, :], float(SLOT), None, ALU.mult))
            o.did(nc.vector.tensor_reduce(bef[:, :], be[:, :, :], AX.X, ALU.add))
            o.settle()
            o.did(ts(bef[:, :], bef[:, :], float(NE - 1), None, ALU.min))
            o.did(tt(dest[:, :, :], PS[:, 7, 0:48].rearrange("p (i e) -> p i e", e=NE),
                     nb[:, 2, :].unsqueeze(1).broadcast_to([P, 3, NE]), ALU.add))
            o.settle()
            o.did(nc.vector.tensor_copy(bei[:, 0:32], bef[:, :]))
            o.did(nc.vector.tensor_copy(bei[:, 32:33], nb[0:1, 1, NE - 1:NE]))
            big = 8192.0
            step(ts(sel[:, :, :], dest[:, :, :], -1.0, big, ALU.mult, ALU.add))
            step(tt(sel[:, :, :], sel[:, :, :], chosen[:, :, :], ALU.mult))
            step(nc.vector.tensor_reduce(d01[:, 0, :], sel[:, :, :], AX.X, ALU.max))
            o.did(ts(d01[:, 0, :], d01[:, 0, :], -1.0, big, ALU.mult, ALU.add))
            step(ts(sel[:, :, :], dest[:, :, :], 1.0, None, ALU.add))
            step(tt(sel[:, :, :], sel[:, :, :], chosen[:, :, :], ALU.mult))
            step(nc.vector.tensor_reduce(d01[:, 1, :], sel[:, :, :], AX.X, ALU.max))
            step(ts(d01[:, 1, :], d01[:, 1, :], -1.0, None, ALU.add))
            for k in range(2):
                step(tt(sel[:, :, :], dest[:, :, :], d01[:, k, :].unsqueeze(2).broadcast_to([P, 3, NE]), ALU.is_equal))
                step(tt(sel[:, :, :], sel[:, :, :], wts[:, :, :], ALU.mult))
                step(nc.vector.tensor_reduce(w01[:, k, :], sel[:, :, :], AX.X, ALU.add))
    mixing.close()

    with ExitStack() as es:
        t = lambda name, shape: sb(name, shape, scope=es)
        xs = t("xs", [P, 2, 512])
        xt = t("xt", [P, KT, SLOT])
        sgt = t("sgt", [SLOT, FE])
        ups = t("ups", [SLOT, FE])
        att = t("att", [P, FT, SLOT])
        pw = t("pw", [P, 2, 3, SLOT])
        pwt = t("pwt", [P, 2, T])
        tmp = t("tmp", [P, 2, 512])
        fg = h2[:, 0, :]
        block = es.enter_context(nc.Block())
        blocks = lambda eng: eng.value_load(bei[0:1, 32:33], min_val=NE, max_val=MAXB)
        back = [(i, t0, n, c) for i, (t0, n) in enumerate(TILES) for c in range(4)]
        NBK = len(back)

        @block.sync
        def _(sp):
            n = blocks(sp)
            for u in range(6, 12):
                sp.wait_ge(used[u % 6], 1)
                load_unit(sp, 0, u)
            with sp.Fori(1, n) as b:
                e = sp.value_load(bei[0:1, bass.ds(b, 1)], min_val=0, max_val=NE - 1)
                for u in range(12):
                    sp.wait_ge(used[u % 6], 2 * b + u // 6)
                    load_unit(sp, e, u)
            sp.wait_ge(t_pk, n + 1)
            sp.dma_start(fg, A["final_g"].partition_broadcast(P)).then_inc(s_fg, 16)
            for i, (t0, n) in enumerate(TILES):
                dst = O["y_prompt"][0, t0:t0 + n] if i < 2 else O["y_sample"].rearrange("b l d -> (b l) d")
                sp.wait_ge(s_fin, i + 1)
                sp.dma_start(dst, x2[0:n, i, :]).then_inc(y_out, 16)
            sp.wait_ge(y_out, 48)

        @block.tensor
        def _(pe):
            n = blocks(pe)

            def gather(b):
                pe.wait_ge(pick_ok, b + 1)
                for c in range(4):
                    for i in range(3):
                        m = nc.tensor.matmul(PS[C * (c % 2):C * (c % 2) + C, 4 + c // 2, :], pick[:, i, :],
                                             h2[:, i, 512 * c:512 * c + 512], start=(i == 0), stop=(i == 2),
                                             skip_group_check=True)
                m.then_inc(t_pk, 1)

            def gather_turn(b):
                pe.wait_ge(xs_ev, b + 1)
                for q in range(2):
                    for m_ in range(4):
                        m = nc.tensor.transpose(PS[:, 6 + q, m_ * P:(m_ + 1) * P], xs[:, q, m_ * P:(m_ + 1) * P],
                                                ident[:, :])
                m.then_inc(t_xt, 1)

            def send_back(b, r):
                i, t0, n_, c = back[r]
                if r == 0:
                    pe.wait_ge(dn_ev, b)
                    pe.wait_ge(pw_ev, b)
                pe.wait_ge(sc_ev, NBK * b + r + 1)
                nc.tensor.matmul(PS[0:n_, 2 + r % 2, :], pwt[:, c % 2, t0:t0 + n_], ysb[:, c // 2, :], start=True,
                                 stop=True).then_inc(t_sc, 1)

            def experts(b):
                pe.wait_ge(xt_ev, b + 1)
                earlier(pe, gu_ok, b)
                for q in range(4):
                    for u in (2 * q, 2 * q + 1):
                        pe.wait_ge(ld_e[u % 6], 32 * b + 16 * (u // 6) + 16)
                    for k in range(4):
                        for c in range(2):
                            for g in range(2):
                                m = nc.tensor.matmul(PS[C * g:C * g + C, c, :], xt[:, 4 * q + k, :],
                                                     unit(2 * q + g, FE)[:, k, 512 * c:512 * c + 512],
                                                     start=(q == 0 and k == 0), stop=(q == 3 and k == 3),
                                                     skip_group_check=True)
                                if k == 3 and c == 1:
                                    m.then_inc(used[(2 * q + g) % 6], 1)
                        if 1 <= 4 * q + k <= NBK and not isinstance(b, int):
                            send_back(b, 4 * q + k - 1)
                gather(b + 1)
                pe.wait_ge(act_ev, 2 * b + 2)
                pe.sem_inc(past_pe, 1)
                for f in range(FT):
                    m = nc.tensor.transpose(PS[:, 3, f * SLOT:(f + 1) * SLOT], sgt[:, f * P:(f + 1) * P],
                                            ident[0:SLOT, 0:SLOT])
                m.then_inc(t_at, 1)
                gather_turn(b + 1)
                pe.wait_ge(pw_ok, b + 1)
                pe.wait_ge(sc_ev, NBK * b + NBK + 2)
                pe.sem_inc(past_pe, 1)
                for h in range(2):
                    for i in range(3):
                        m = nc.tensor.matmul(PS[C * h:C * h + C, 2, i * P:(i + 1) * P], pw[:, 0, i, :], ident[:, :],
                                             start=(i == 0), stop=(i == 2), skip_group_check=True)
                m.then_inc(t_pw, 1)
                pe.wait_ge(at_ev, b + 1)
                pe.wait_ge(xs_ev, b + 2)
                for q in range(4):
                    u = 8 + q
                    pe.wait_ge(ld_e[u % 6], 32 * b + 32)
                    for k in range(2):
                        for c in range(4):
                            m = nc.tensor.matmul(PS[C * (c % 2):C * (c % 2) + C, 4 + c // 2, :], att[:, 2 * q + k, :],
                                                 unit(u, D)[:, k, 512 * c:512 * c + 512],
                                                 start=(q == 0 and k == 0), stop=(q == 3 and k == 1),
                                                 skip_group_check=True)
                    m.then_inc(used[u % 6], 1)

            pe.sem_inc(t_sc, NBK)
            gather(0)
            gather_turn(0)
            experts(0)
            with pe.Fori(1, n) as b:
                experts(b)
            for r in range(NBK):
                send_back(n, r)

        @block.scalar
        def _(act):
            n = blocks(act)

            def gather_out(b):
                act.wait_ge(t_pk, b + 1)
                nc.scalar.copy(xs[:, 0, :], PS[:, 4, :])
                nc.scalar.copy(xs[:, 1, :], PS[:, 5, :]).then_inc(xs_ev, 1)

            def experts(b):
                act.wait_ge(used[7 % 6], 2 * b + 2)
                earlier(act, t_at, b)
                nc.scalar.activation(sgt[:, :], PS[0:C, 0:2, :].rearrange("p c n -> p (c n)"), ACT.Sigmoid
                                     ).then_inc(up_ev, 1)
                nc.scalar.copy(ups[:, :], PS[C:P, 0:2, :].rearrange("p c n -> p (c n)")).then_inc(up_ev, 1)
                gather_out(b + 1)
                act.wait_ge(t_at, b + 1)
                nc.scalar.copy(att[:, :, :].rearrange("p f s -> p (f s)"), PS[:, 3, :]).then_inc(at_ev, 1)
                act.wait_ge(t_pw, b + 1)
                act.wait_ge(t_sc, NBK * b + NBK)
                for h in range(2):
                    m = nc.scalar.copy(pwt[C * h:C * h + C, h, :], PS[C * h:C * h + C, 2, 0:T])
                m.then_inc(pw_ev, 1)
                act.wait_ge(used[11 % 6], 2 * b + 2)
                for c in range(2):
                    m = nc.scalar.copy(ysb[:, c, :], PS[:, 4 + c, :])
                m.then_inc(dn_ev, 1)

            gather_out(0)
            act.wait_ge(pz, 1)
            experts(0)
            with act.Fori(1, n) as b:
                experts(b)
            for r, (i, t0, n_, c) in enumerate(back):
                act.wait_ge(x_ok, n * NBK + r + 3)
                nc.scalar.activation(h2[0:n_, 1, 512 * c:512 * c + 512], x2[0:n_, i, 512 * c:512 * c + 512], ACT.Square,
                                     accum_out=ss4[0:n_, i, c:c + 1]).then_inc(sq_ok, 1)
                if c == 3:
                    act.wait_ge(f_own, i + 1)
                    nc.scalar.activation(ssq[0:n_, 4 + i:5 + i], ssq[0:n_, i:i + 1], ACT.Sqrt, bias=eps[0:n_, 0:1],
                                         scale=1.0 / D).then_inc(a_own, 1)

        @block.vector
        def _(ve):
            n = blocks(ve)

            def picks(b):
                earlier(ve, t_pk, b)
                for i in range(3):
                    ts_ = nc.vector.tensor_scalar(pick2[:, i, :], slotf[:, :], d01[:, 0, i:i + 1], None, ALU.is_equal)
                ts_.then_inc(p2, 1)
                ve.wait_ge(p2, 2 * b + 1)
                for i in range(3):
                    m = nc.vector.scalar_tensor_tensor(out=pick[:, i, :], in0=slotf[:, :], scalar=d01[:, 1, i:i + 1],
                                                       in1=pick2[:, i, :], op0=ALU.is_equal, op1=ALU.add)
                m.then_inc(pick_ok, 1)
                ve.wait_ge(pick_ok, b + 1)
                nc.vector.tensor_scalar(slotf[:, :], slotf[:, :], float(SLOT), None, ALU.add).then_inc(p2, 1)
                ve.wait_ge(p2, 2 * b + 2)

            def turned(b):
                ve.wait_ge(t_xt, b + 1)
                for q in range(2):
                    m = nc.vector.tensor_copy(xt[:, 8 * q:8 * q + 8, :].rearrange("p (h m) s -> p m h s", h=2),
                                              PS[:, 6 + q, :].rearrange("p (m h s) -> p m h s", m=4, h=2))
                m.then_inc(xt_ev, 1)

            def gated(b, r):
                i, t0, n_, c = back[r]
                ve.wait_ge(t_sc, NBK * b + r + 1)
                ve.wait_ge(x_ok, NBK * b + r + 1)
                nc.vector.tensor_tensor(tmp[0:n_, r % 2, :], PS[0:n_, 2 + r % 2, :],
                                        gtm[0:n_, i // 2, 512 * c:512 * c + 512], ALU.mult).then_inc(sc_ev, 1)

            def experts(b):
                picks(b + 1)
                if not isinstance(b, int):
                    for r in range(NBK):
                        gated(b, r)
                ve.wait_ge(up_ev, 2 * b + 1)
                nc.vector.tensor_tensor(sgt[:, :], sgt[:, :], PS[0:C, 0:2, :].rearrange("p c n -> p (c n)"), ALU.mult
                                        ).then_inc(act_ev, 1)
                ve.wait_ge(up_ev, 2 * b + 2)
                ve.wait_ge(act_ev, 2 * b + 1)
                ve.sem_inc(gu_ok, 1)
                nc.vector.tensor_tensor(sgt[:, :], sgt[:, :], ups[:, :], ALU.mult).then_inc(act_ev, 1)
                turned(b + 1)

            ve.sem_inc(sc_ev, 2 + NBK)
            picks(0)
            nc.vector.memset(pwt[:, :, :], 0.0).then_inc(pz, 1)
            turned(0)
            experts(0)
            with ve.Fori(1, n) as b:
                experts(b)
            o = Order(ve, f_own)

            def squares(i):
                n_ = TILES[i][1]
                ve.wait_ge(sq_ok, 4 * i + 4)
                o.did(nc.vector.tensor_reduce(ssq[0:n_, i:i + 1], ss4[0:n_, i, :], AX.X, ALU.add))

            def finish(i):
                n_ = TILES[i][1]
                ve.wait_ge(a_own, i + 1)
                nc.vector.reciprocal(ssq[0:n_, 4 + i:5 + i], ssq[0:n_, 4 + i:5 + i]).then_inc(fin_own, 1)
                ve.wait_ge(fin_own, 2 * i + 1)
                if i == 0:
                    ve.wait_ge(s_fg, 16)
                xx = x2[0:n_, i, :]
                nc.vector.scalar_tensor_tensor(out=xx, in0=xx, scalar=ssq[0:n_, 4 + i:5 + i], in1=fg[0:n_, :],
                                               op0=ALU.mult, op1=ALU.mult).then_inc(fin_own, 1)
                ve.wait_ge(fin_own, 2 * i + 2)
                ve.sem_inc(s_fin, 1)

            for r in range(NBK):
                gated(n, r)
                if r in (5, 9):
                    squares(r // 4 - 1)
                if r == 8:
                    finish(0)
            finish(1)
            squares(2)
            finish(2)

        @block.gpsimd
        def _(pool):
            n = blocks(pool)
            pool.sem_inc(x_ok, 2 + NBK)

            def weights(b):
                earlier(pool, t_pw, b)
                pool.sem_inc(past_pool, 1)
                for k in range(2):
                    for i in range(3):
                        m = nc.gpsimd.tensor_scalar(pw[:, k, i, :], slotw[:, :], d01[:, k, i:i + 1], w01[:, k, i:i + 1],
                                                    ALU.is_equal, ALU.mult)
                m.then_inc(w_own, 1)
                pool.wait_ge(w_own, 2 * b + 1)
                nc.gpsimd.tensor_tensor(pw[:, 0], pw[:, 0], pw[:, 1], ALU.add).then_inc(pw_ok, 1)
                pool.wait_ge(pw_ok, b + 1)
                pool.sem_inc(past_pool, 1)
                nc.gpsimd.tensor_scalar(slotw[:, :], slotw[:, :], float(SLOT), None, ALU.add).then_inc(w_own, 1)
                pool.wait_ge(w_own, 2 * b + 2)

            def add(b, r):
                i, t0, n_, c = back[r]
                pool.wait_ge(sc_ev, NBK * b + r + 3)
                xx = x2[0:n_, i, 512 * c:512 * c + 512]
                nc.gpsimd.tensor_tensor(xx, xx, tmp[0:n_, r % 2, :], ALU.add).then_inc(x_ok, 1)

            weights(0)
            with pool.Fori(1, n) as b:
                for r in range(NBK):
                    add(b, r)
                weights(b)
            for r in range(NBK):
                add(n, r)


INPUTS = ["x_prompt", "x_sample", "state_wkv", "state_pool", "state_shift", "c_prompt", "c_sample", "w_ada", "b_ada",
          "norm1_g", "norm2_g", "w_in", "w_pool", "pool_scale", "mu_shift", "w0", "w2", "a0", "a2", "g2", "k_k", "k_a",
          "r_k", "lnx_w", "lnx_b", "w_out", "w_router", "b_router", "w_gate", "w_up", "w_down", "final_g"]
OUTPUTS = [("y_prompt", (1, NP_TOK, D)), ("y_sample", (NB, NL, D)), ("wkv_p", (1, 1, RW // HD, HD, HD)),
           ("pool_p", (1, 1, BUF, PW)), ("shift_p", (1, 1, SH)), ("wkv_s", (1, NB, RW // HD, HD, HD)),
           ("pool_s", (1, NB, BUF, PW)), ("shift_s", (1, NB, SH))]


def kernel(**inputs):
    import numpy as np
    import concourse.bacc as bacc
    from concourse.bass_utils import run_bass_kernel_spmd

    nc = bacc.Bacc("TRN2", target_bir_lowering=False, num_devices=1)
    arrays = {f"in_{n}": np.ascontiguousarray(inputs[n]) for n in INPUTS}
    A = {n: nc.dram_tensor(f"in_{n}", arrays[f"in_{n}"].shape, F32, kind="ExternalInput").ap() for n in INPUTS}
    O = {n: nc.dram_tensor(f"out_{n}", shape, F32, kind="ExternalOutput").ap() for n, shape in OUTPUTS}
    build(nc, A, O)
    r = run_bass_kernel_spmd(nc, [arrays], core_ids=[0])
    return tuple(r.results[0][f"out_{n}"] for n, _ in OUTPUTS)
```
